# Optimizing a Trainium2 kernel written in Bass

```python
import jax, jax.numpy as jnp
from jax import lax
import numpy as np

D_MODEL = 1024
BATCH = 1
SEQ = 512
DEPTH = 2

GRID_W = 64
CTX_LEN = 256
N_MIXERS = 3
RW_HEAD = 64
RW_HEADS = D_MODEL // RW_HEAD
RW_DECAY_LORA = 64
RW_AAA_LORA = 64
RW_GATE_LORA = 128
AT_HEAD = 128
AT_Q_HEADS = D_MODEL // AT_HEAD
AT_KV_HEADS = 2
Q_BLOCK = 128
ROPE_BASE = 10000.0
NA_HEAD = 64
NA_HEADS = D_MODEL // NA_HEAD
WIN_H = 8
WIN_W = 16
D_FF = -(-8 * D_MODEL // (3 * 256)) * 256
N_RWKV = len(range(0, DEPTH, N_MIXERS))
N_GQA = len(range(1, DEPTH, N_MIXERS))
N_NA = len(range(2, DEPTH, N_MIXERS))
RMS_EPS = 1e-6
LNX_EPS = 64e-5
NORM_EPS = 1e-12

kernel_name = "hybrid_rwkv7_gqa_natten_prefix_dit"

def rms_norm(x, g):
    xf = x.astype(jnp.float32)
    y = xf * lax.rsqrt(jnp.mean(xf * xf, axis=-1, keepdims=True) + RMS_EPS)
    return (y * g).astype(x.dtype)

def swiglu(h, w1, w3, w2):
    return (jax.nn.silu(h @ w1) * (h @ w3)) @ w2

def softmax_attend(q, k, v):
    s = jnp.einsum('bkgqd,bksd->bkgqs', q, k).astype(jnp.float32) * (q.shape[-1] ** -0.5)
    p = jax.nn.softmax(s, axis=-1).astype(v.dtype)
    return jnp.einsum('bkgqs,bksd->bkgqd', p, v)

def axial_rope(n_tok, head_dim):
    t = jnp.arange(n_tok)
    rows = (t // GRID_W).astype(jnp.float32)
    cols = (t % GRID_W).astype(jnp.float32)
    d_axis = head_dim // 2
    inv = jnp.float32(ROPE_BASE) ** (-jnp.arange(0, d_axis, 2, dtype=jnp.float32) / d_axis)
    ang = jnp.concatenate([rows[:, None] * inv, cols[:, None] * inv], axis=-1)
    return jnp.cos(ang), jnp.sin(ang)

def apply_rope(x, cos, sin):
    xp = x.reshape(x.shape[:-1] + (-1, 2))
    x1, x2 = xp[..., 0], xp[..., 1]
    c, s = cos[None, :, None, :], sin[None, :, None, :]
    out = jnp.stack([x1 * c - x2 * s, x1 * s + x2 * c], axis=-1)
    return out.reshape(x.shape).astype(x.dtype)

def centred_shift(h):
    prev = jnp.pad(h[:, :-1], ((0, 0), (1, 0), (0, 0)))
    nxt = jnp.pad(h[:, 1:], ((0, 0), (0, 1), (0, 0)))
    return 0.5 * (prev + nxt) - h

def _heads(t):
    return t.reshape(t.shape[:-1] + (RW_HEADS, RW_HEAD))

def rwkv7_features(h, mu, wr, wk, wv, w0, w1, w2, a0, a1, a2, k_k, k_a):
    f32 = jnp.float32
    xx = centred_shift(h)
    xr, xw, xk, xv, xa = (h + xx * mu[i] for i in range(5))
    r = _heads(xr @ wr)
    k = _heads(xk @ wk)
    v = _heads(xv @ wv)
    kk = (k * _heads(k_k)).astype(f32)
    kk = kk / jnp.maximum(jnp.linalg.norm(kk, axis=-1, keepdims=True), NORM_EPS)
    lora_w = jnp.einsum('ebtr,erd->ebtd', jnp.tanh(jnp.einsum('btd,edr->ebtr', xw, w1)), w2)
    w_log = -jax.nn.softplus(-(w0[:, None, None, :] + lora_w).astype(f32)) - 0.5
    decay = _heads(jnp.exp(-jnp.exp(w_log)))
    lora_a = jnp.einsum('ebtr,erd->ebtd', jnp.einsum('btd,edr->ebtr', xa, a1), a2)
    a = _heads(jax.nn.sigmoid((a0[:, None, None, :] + lora_a).astype(f32)))
    k_dir = k[None] * (1.0 + (a - 1.0) * _heads(k_a))
    return xx, r, v, kk, decay, a, k_dir

def rwkv7_scan(S0, r, decay, k, v, kk, a, reverse):
    def step(S, inp):
        r_t, w_t, k_t, v_t, kk_t, a_t = inp
        sa = jnp.einsum('bhvk,bhk->bhv', S, -kk_t)
        S = (S * w_t[:, :, None, :] + sa[..., None] * (kk_t * a_t)[:, :, None, :]
             + v_t[..., None] * k_t[:, :, None, :])
        return S, jnp.einsum('bhvk,bhk->bhv', S, r_t)
    xs = tuple(jnp.moveaxis(t.astype(jnp.float32), 1, 0) for t in (r, decay, k, v, kk, a))
    S, ys = lax.scan(step, S0, xs, reverse=reverse)
    return S, jnp.moveaxis(ys, 0, 1)

def rwkv7_mixer(h_lat, h_ctx, mu, wr, wk, wv, wo, w0, w1, w2, a0, a1, a2, g1, g2,
                k_k, k_a, r_k, lnx_g, lnx_b, need_ctx):
    feat_l = rwkv7_features(h_lat, mu, wr, wk, wv, w0, w1, w2, a0, a1, a2, k_k, k_a)
    feat_c = rwkv7_features(h_ctx, mu, wr, wk, wv, w0, w1, w2, a0, a1, a2, k_k, k_a)
    xx_l, r_l, v_l, kk_l, d_l, a_l, k_l = feat_l
    xx_c, r_c, v_c, kk_c, d_c, a_c, k_c = feat_c
    S0 = jnp.zeros((h_lat.shape[0], RW_HEADS, RW_HEAD, RW_HEAD), jnp.float32)
    ys_l, ys_c = [], []
    for d, rev in enumerate((False, True)):
        S_c, yc_d = rwkv7_scan(S0, r_c, d_c[d], k_c[d], v_c, kk_c, a_c[d], rev)
        _, yl_d = rwkv7_scan(S_c, r_l, d_l[d], k_l[d], v_l, kk_l, a_l[d], rev)
        ys_l.append(yl_d)
        ys_c.append(yc_d)

    def readout(h, xx, y, r, k_dir, v):
        B, T, D = h.shape
        mean = jnp.mean(y, axis=-1, keepdims=True)
        var = jnp.mean(jnp.square(y - mean), axis=-1, keepdims=True)
        yn = ((y - mean) * lax.rsqrt(var + LNX_EPS)).reshape(B, T, D) * lnx_g + lnx_b
        bonus = jnp.sum(jnp.sum(r[None] * k_dir * r_k, axis=-1, keepdims=True) * v[None], axis=0)
        g = jax.nn.sigmoid((h + xx * mu[5]) @ g1) @ g2
        return ((yn + bonus.reshape(B, T, D)) * g).astype(h.dtype) @ wo

    o_lat = readout(h_lat, xx_l, ys_l[0] + ys_l[1], r_l, k_l, v_l)
    o_ctx = readout(h_ctx, xx_c, ys_c[0] + ys_c[1], r_c, k_c, v_c) if need_ctx else None
    return o_lat, o_ctx

def gqa_mixer(h_lat, h_ctx, wq, wk, wv, wo, gq, gk, need_ctx):
    B, T, _ = h_lat.shape
    G = AT_Q_HEADS // AT_KV_HEADS

    def proj(h):
        n = h.shape[1]
        q = rms_norm((h @ wq).reshape(B, n, AT_Q_HEADS, AT_HEAD), gq)
        k = rms_norm((h @ wk).reshape(B, n, AT_KV_HEADS, AT_HEAD), gk)
        v = (h @ wv).reshape(B, n, AT_KV_HEADS, AT_HEAD)
        return q, k, v

    def to_groups(q):
        return q.reshape(B, q.shape[1], AT_KV_HEADS, G, AT_HEAD).transpose(0, 2, 3, 1, 4)

    def from_groups(o):
        return o.transpose(0, 3, 1, 2, 4).reshape(B, o.shape[3], AT_Q_HEADS * AT_HEAD)

    q_l, k_l, v_l = proj(h_lat)
    q_c, k_c, v_c = proj(h_ctx)
    cos, sin = axial_rope(T, AT_HEAD)
    q_l = apply_rope(q_l, cos, sin)
    k_l = apply_rope(k_l, cos, sin)
    k_all = jnp.concatenate([k_l, k_c], axis=1).transpose(0, 2, 1, 3)
    v_all = jnp.concatenate([v_l, v_c], axis=1).transpose(0, 2, 1, 3)
    nb = T // Q_BLOCK
    qb = to_groups(q_l).reshape(B, AT_KV_HEADS, G, nb, Q_BLOCK, AT_HEAD).transpose(3, 0, 1, 2, 4, 5)
    ob = lax.map(lambda q: softmax_attend(q, k_all, v_all), qb)
    o_l = ob.transpose(1, 2, 3, 0, 4, 5).reshape(B, AT_KV_HEADS, G, T, AT_HEAD)
    o_lat = from_groups(o_l) @ wo
    o_ctx = None
    if need_ctx:
        o_c = softmax_attend(to_groups(q_c), k_c.transpose(0, 2, 1, 3), v_c.transpose(0, 2, 1, 3))
        o_ctx = from_groups(o_c) @ wo
    return o_lat, o_ctx

def na_mixer(h_lat, h_ctx, wqkv, wo, gq, gk, rpb, need_ctx):
    B, T, _ = h_lat.shape
    rows = T // GRID_W
    kh, kw = min(WIN_H, rows), WIN_W
    n_win = kh * kw

    def proj(h):
        qkv = (h @ wqkv).reshape(B, h.shape[1], 3, NA_HEADS, NA_HEAD)
        q = rms_norm(qkv[:, :, 0], gq).transpose(0, 2, 1, 3)
        k = rms_norm(qkv[:, :, 1], gk).transpose(0, 2, 1, 3)
        v = qkv[:, :, 2].transpose(0, 2, 1, 3)
        return q, k, v

    q_l, k_l, v_l = proj(h_lat)
    q_c, k_c, v_c = proj(h_ctx)
    r_idx = np.arange(rows)
    c_idx = np.arange(GRID_W)
    key_rows = np.clip(r_idx - kh // 2, 0, rows - kh)[:, None] + np.arange(kh)
    key_cols = np.clip(c_idx - kw // 2, 0, GRID_W - kw)[:, None] + np.arange(kw)
    idx = (key_rows[:, None, :, None] * GRID_W + key_cols[None, :, None, :]).reshape(rows, GRID_W, n_win)
    off_r = jnp.asarray(key_rows - r_idx[:, None] + (WIN_H - 1), jnp.int32)
    off_c = jnp.asarray(key_cols - c_idx[:, None] + (WIN_W - 1), jnp.int32)
    idx = jnp.asarray(idx, jnp.int32)
    scale = NA_HEAD ** -0.5
    q_rows = q_l.reshape(B, NA_HEADS, rows, GRID_W, NA_HEAD).transpose(2, 0, 1, 3, 4)

    def row_block(args):
        q_row, idx_row, offr_row = args
        k_win = k_l[:, :, idx_row]
        v_win = v_l[:, :, idx_row]
        bias = rpb[:, offr_row[None, :, None], off_c[:, None, :]].reshape(NA_HEADS, GRID_W, n_win)
        s_win = jnp.einsum('bhqd,bhqkd->bhqk', q_row, k_win).astype(jnp.float32) * scale + bias
        s_ctx = jnp.einsum('bhqd,bhcd->bhqc', q_row, k_c).astype(jnp.float32) * scale
        p = jax.nn.softmax(jnp.concatenate([s_win, s_ctx], axis=-1), axis=-1).astype(v_l.dtype)
        return (jnp.einsum('bhqk,bhqkd->bhqd', p[..., :n_win], v_win)
                + jnp.einsum('bhqc,bhcd->bhqd', p[..., n_win:], v_c))

    o = lax.map(row_block, (q_rows, idx, off_r))
    o_lat = o.transpose(1, 0, 3, 2, 4).reshape(B, T, NA_HEADS * NA_HEAD) @ wo
    o_ctx = None
    if need_ctx:
        o_c = softmax_attend(q_c[:, :, None], k_c, v_c)[:, :, 0]
        o_ctx = o_c.transpose(0, 2, 1, 3).reshape(B, h_ctx.shape[1], NA_HEADS * NA_HEAD) @ wo
    return o_lat, o_ctx

def setup_inputs(seed: int = 0) -> dict:
    key = jax.random.key(seed)
    keys = iter(jax.random.split(key, 64))
    f32 = jnp.float32
    D = D_MODEL
    nA, nB, nC = N_RWKV, N_GQA, N_NA
    A_DIM = AT_Q_HEADS * AT_HEAD
    KV_DIM = AT_KV_HEADS * AT_HEAD
    N_DIM = NA_HEADS * NA_HEAD

    def nrm(shape, std):
        return jax.random.normal(next(keys), shape, f32) * std

    def unif(shape, lo, hi):
        return jax.random.uniform(next(keys), shape, f32, lo, hi)

    return {
        "x": nrm((BATCH, SEQ, D), 1.0),
        "c": nrm((BATCH, D), 1.0),
        "ctx": nrm((BATCH, CTX_LEN, D), 1.0),
        "c_ctx": nrm((D,), 1.0),
        "mod_w": nrm((DEPTH, D, 6 * D), 0.5 * D ** -0.5),
        "mod_b": nrm((DEPTH, 6 * D), 0.02),
        "norm_mix": 1.0 + nrm((DEPTH, D), 0.05),
        "norm_ffn": 1.0 + nrm((DEPTH, D), 0.05),
        "ff_w1": nrm((DEPTH, D, D_FF), D ** -0.5),
        "ff_w3": nrm((DEPTH, D, D_FF), D ** -0.5),
        "ff_w2": nrm((DEPTH, D_FF, D), D_FF ** -0.5),
        "rw_mu": unif((nA, 6, D), 0.0, 1.0),
        "rw_wr": nrm((nA, D, D), D ** -0.5),
        "rw_wk": nrm((nA, D, D), D ** -0.5),
        "rw_wv": nrm((nA, D, D), D ** -0.5),
        "rw_wo": nrm((nA, D, D), D ** -0.5),
        "rw_w0": unif((nA, 2, D), -5.0, 0.5),
        "rw_w1": nrm((nA, 2, D, RW_DECAY_LORA), D ** -0.5),
        "rw_w2": nrm((nA, 2, RW_DECAY_LORA, D), 0.5 * RW_DECAY_LORA ** -0.5),
        "rw_a0": nrm((nA, 2, D), 0.1),
        "rw_a1": nrm((nA, 2, D, RW_AAA_LORA), D ** -0.5),
        "rw_a2": nrm((nA, 2, RW_AAA_LORA, D), 0.5 * RW_AAA_LORA ** -0.5),
        "rw_g1": nrm((nA, D, RW_GATE_LORA), D ** -0.5),
        "rw_g2": nrm((nA, RW_GATE_LORA, D), RW_GATE_LORA ** -0.5),
        "rw_kk": 0.85 + nrm((nA, D), 0.05),
        "rw_ka": 1.0 + nrm((nA, D), 0.05),
        "rw_rk": nrm((nA, RW_HEADS, RW_HEAD), 0.1),
        "rw_lnx_g": 1.0 + nrm((nA, D), 0.05),
        "rw_lnx_b": nrm((nA, D), 0.02),
        "at_wq": nrm((nB, D, A_DIM), D ** -0.5),
        "at_wk": nrm((nB, D, KV_DIM), D ** -0.5),
        "at_wv": nrm((nB, D, KV_DIM), D ** -0.5),
        "at_wo": nrm((nB, A_DIM, D), A_DIM ** -0.5),
        "at_gq": 1.0 + nrm((nB, AT_HEAD), 0.05),
        "at_gk": 1.0 + nrm((nB, AT_HEAD), 0.05),
        "na_wqkv": nrm((nC, D, 3 * N_DIM), D ** -0.5),
        "na_wo": nrm((nC, N_DIM, D), N_DIM ** -0.5),
        "na_gq": 1.0 + nrm((nC, NA_HEAD), 0.05),
        "na_gk": 1.0 + nrm((nC, NA_HEAD), 0.05),
        "na_rpb": nrm((nC, NA_HEADS, 2 * WIN_H - 1, 2 * WIN_W - 1), 0.1),
    }

def reference(x, c, ctx, c_ctx, mod_w, mod_b, norm_mix, norm_ffn, ff_w1, ff_w3, ff_w2,
              rw_mu, rw_wr, rw_wk, rw_wv, rw_wo, rw_w0, rw_w1, rw_w2, rw_a0, rw_a1, rw_a2,
              rw_g1, rw_g2, rw_kk, rw_ka, rw_rk, rw_lnx_g, rw_lnx_b,
              at_wq, at_wk, at_wv, at_wo, at_gq, at_gk,
              na_wqkv, na_wo, na_gq, na_gk, na_rpb):
    mod_lat = jnp.einsum('bd,lde->lbe', jax.nn.silu(c), mod_w) + mod_b[:, None, :]
    mod_ctx = jnp.einsum('d,lde->le', jax.nn.silu(c_ctx), mod_w) + mod_b
    h_lat, h_ctx = x, ctx
    for i in range(DEPTH):
        need_ctx = i < DEPTH - 1
        kind, j = i % N_MIXERS, i // N_MIXERS
        sh_m, sc_m, gt_m, sh_f, sc_f, gt_f = jnp.split(mod_lat[i][:, None, :], 6, axis=-1)
        csh_m, csc_m, cgt_m, csh_f, csc_f, cgt_f = jnp.split(mod_ctx[i], 6, axis=-1)
        a_lat = rms_norm(h_lat, norm_mix[i]) * (1.0 + sc_m) + sh_m
        a_ctx = rms_norm(h_ctx, norm_mix[i]) * (1.0 + csc_m) + csh_m
        if kind == 0:
            o_lat, o_ctx = rwkv7_mixer(a_lat, a_ctx, rw_mu[j], rw_wr[j], rw_wk[j], rw_wv[j], rw_wo[j],
                                       rw_w0[j], rw_w1[j], rw_w2[j], rw_a0[j], rw_a1[j], rw_a2[j],
                                       rw_g1[j], rw_g2[j], rw_kk[j], rw_ka[j], rw_rk[j],
                                       rw_lnx_g[j], rw_lnx_b[j], need_ctx)
        elif kind == 1:
            o_lat, o_ctx = gqa_mixer(a_lat, a_ctx, at_wq[j], at_wk[j], at_wv[j], at_wo[j],
                                     at_gq[j], at_gk[j], need_ctx)
        else:
            o_lat, o_ctx = na_mixer(a_lat, a_ctx, na_wqkv[j], na_wo[j], na_gq[j], na_gk[j],
                                    na_rpb[j], need_ctx)
        h_lat = h_lat + gt_m * o_lat
        f_lat = rms_norm(h_lat, norm_ffn[i]) * (1.0 + sc_f) + sh_f
        h_lat = h_lat + gt_f * swiglu(f_lat, ff_w1[i], ff_w3[i], ff_w2[i])
        if need_ctx:
            h_ctx = h_ctx + cgt_m * o_ctx
            f_ctx = rms_norm(h_ctx, norm_ffn[i]) * (1.0 + csc_f) + csh_f
            h_ctx = h_ctx + cgt_f * swiglu(f_ctx, ff_w1[i], ff_w3[i], ff_w2[i])
    return h_lat


_drawn_inputs = setup_inputs


def setup_inputs(seed=0):
    import zlib

    import numpy as np

    out = dict(_drawn_inputs(seed))
    spreads = {}
    factors = {'norm_mix': 3.459,
     'rw_w1': 6.152,
     'rw_w2': 6.322,
     'rw_a0': 8.0,
     'rw_kk': 17.706,
     'rw_ka': 3.432,
     'rw_lnx_g': 7.075,
     'rw_lnx_b': 29.647,
     'at_wq': 3.08,
     'at_wk': 3.011,
     'at_gq': 8.0,
     'at_gk': 8.0,
     'norm_ffn': 6.304}
    for name, (base, spread) in spreads.items():
        noise = np.random.default_rng([zlib.crc32(name.encode()), seed]).standard_normal(out[name].shape)
        drawn = base * np.exp(spread * noise) if base else spread * noise
        out[name] = __import__('jax').numpy.asarray(drawn.astype(out[name].dtype))
    for name, factor in factors.items():
        out[name] = (out[name] * factor).astype(out[name].dtype)
    return out
```

```python
from contextlib import ExitStack

import numpy as np

import concourse.bass as bass
from concourse import mybir

F32 = mybir.dt.float32
ALU = mybir.AluOpType
ACT = mybir.ActivationFunctionType
AX = mybir.AxisListType.X

P = 128
D = 1024
CT = D // P
CTX, LAT = 256, 512
TOK = CTX + LAT
SEGS = ((0, CTX), (CTX, LAT))
FF = 2816
FT = FF // P
CH = 64
NCH = TOK // CH
NB = NCH // 2
LEVELS = 6
DECAY = float(np.exp(-0.5))
HEADS, KV_HEADS = 8, 2

PMODB, PC, PGQ, PGK = 0, 96, 112, 113
PMU = 114
PW0, PA0 = PMU + 48, PMU + 64
PKK, PKA, PRK, PLG, PLB = (PMU + 80 + 8 * n for n in range(5))
PLESS = PMU + 120
PNM = PLESS + CT
PNF = PNM + 16
NPAR = PNF + 16


class Order:

    def __init__(self, eng, sem):
        self.eng, self.sem, self.off, self.n, self.outer = eng, sem, 0, 0, []

    def __call__(self, ins):
        ins.then_inc(self.sem, 1)
        self.n += 1
        self.eng.wait_ge(self.sem, self.off + self.n)

    def enter(self, at, per):
        self.outer.append((self.off, self.n, per))
        self.off, self.n = self.off + self.n + at * per, 0

    def leave(self, trips):
        self.off, n, per = self.outer.pop()
        assert self.n == per, f"{self.n} steps, {per} expected"
        self.n = n + trips * per


def signal(eng, ins, sem, value):
    ins.then_inc(sem, 1)
    eng.wait_ge(sem, value)


class Core:

    def __init__(self, nc, ctx):
        self.nc, self.ctx, self.count = nc, ctx, 0

    def sb(self, name, shape):
        return self.ctx.enter_context(self.nc.sbuf_tensor(name, shape, F32))

    def sem(self, name):
        return self.ctx.enter_context(self.nc.semaphore(name))


def tokens(bank_ctx, bank_lat):
    return ((bank_ctx[:, 0:CTX], 0, CTX), (bank_lat[:, 0:LAT], CTX, LAT))


def setup(c, d):
    nc = c.nc
    with ExitStack() as ctx:
        rows = [ctx.enter_context(nc.sbuf_tensor(f"par_rows{n}", [P, P], F32)) for n in range(3)]
        loaded = ctx.enter_context(nc.semaphore("setup_loaded"))
        turned = ctx.enter_context(nc.semaphore("par_turned"))
        copied = ctx.enter_context(nc.semaphore("par_copied"))
        gated = ctx.enter_context(nc.semaphore("cond_silu"))
        row_of = lambda a: a.rearrange("(m p) -> m p", p=P)
        lists = [
            [d["mod_b"].rearrange("l (m p) -> (l m) p", p=P), d["c"].rearrange("b (m p) -> (b m) p", p=P),
             row_of(d["c_ctx"]), d["at_gq"], d["at_gk"]],
            [d["rw_mu"].rearrange("a n (m p) -> (a n m) p", p=P)]
            + [d[n].rearrange("a e (m p) -> (a e m) p", p=P) for n in ("rw_w0", "rw_a0")]
            + [d[n].rearrange("a (m p) -> (a m) p", p=P) for n in ("rw_kk", "rw_ka")]
            + [d["rw_rk"].rearrange("a (m h) k -> (a m) (h k)", h=2)]
            + [d[n].rearrange("a (m p) -> (a m) p", p=P) for n in ("rw_lnx_g", "rw_lnx_b")],
            [d[n].rearrange("a (m p) -> (a m) p", p=P) for n in ("norm_mix", "norm_ffn")],
        ]
        sizes = [114, 120, 32]
        n_loads = 5 + sum(len(x) for x in lists)
        with nc.Block() as block:
            @block.sync
            def _(sp):
                for t, s in ((c.ident, "k_ident"), (c.ones_head, "k_ones_head"), (c.level_mask, "k_level_mask"),
                             (c.score_mask, "k_score_mask"), (c.keep, "k_keep")):
                    sp.dma_start(t[:], d[s]).then_inc(loaded, 16)
                for tile, parts in zip(rows, lists):
                    at = 0
                    for part in parts:
                        n = part.shape[0]
                        sp.dma_start(tile[at:at + n, :], part).then_inc(loaded, 16)
                        at += n

            @block.tensor
            def _(pe):
                pe.wait_ge(loaded, 16 * n_loads)
                for n, m in enumerate(sizes):
                    pe.transpose(c.bank[n][:, 0:m], rows[n][0:m, :], c.ident[0:m, 0:m]).then_inc(turned, 1)

            @block.vector
            def _(dve):
                at = 0
                nc.vector.memset(c.ones[:], 1.0).then_inc(copied, 1)
                nc.vector.memset(c.eps[:, 0:1], 1e-6).then_inc(copied, 1)
                nc.vector.memset(c.eps[:, 1:2], 64e-5).then_inc(copied, 1)
                dve.wait_ge(turned, 3)
                for n, m in enumerate(sizes):
                    at += CT if n == 2 else 0
                    nc.vector.tensor_copy(c.par[:, at:at + m], c.bank[n][:, 0:m]).then_inc(copied, 1)
                    at += m
                dve.wait_ge(copied, 6)
                nc.vector.tensor_scalar(c.par[:, PLESS:PLESS + CT], c.par[:, PKA:PKA + CT], -1.0, 1.0, ALU.mult, ALU.add)\
                    .then_inc(copied, 1)

            @block.scalar
            def _(act):
                act.wait_ge(copied, 6)
                nc.scalar.activation(c.cond[:], c.par[:, PC:PC + 16], ACT.Silu).then_inc(gated, 1)


def modulation(c, d):
    nc = c.nc
    W = 512
    steps = 6 * D // W
    with ExitStack() as ctx:
        w = [ctx.enter_context(nc.sbuf_tensor(f"modw{s}", [P, CT, W], F32)) for s in range(2)]
        row = [ctx.enter_context(nc.sbuf_tensor(f"modrow{s}", [2, W], F32)) for s in range(2)]
        loaded = [ctx.enter_context(nc.semaphore(f"modw_loaded{s}")) for s in range(2)]
        product = ctx.enter_context(nc.semaphore("mod_product"))
        copied = ctx.enter_context(nc.semaphore("mod_row_copied"))
        turned = ctx.enter_context(nc.semaphore("mod_turned"))
        stored = ctx.enter_context(nc.semaphore("mod_stored"))
        gains = ctx.enter_context(nc.semaphore("norm_gains"))
        src = d["mod_w"].rearrange("l (k p) e -> l p k e", p=P)
        cond = c.cond[:].rearrange("p (r k) -> p r k", k=CT)
        with nc.Block() as block:
            @block.sync
            def _(sp):
                for s in range(2):
                    sp.dma_start(w[s][:], src[0][:, :, s * W:(s + 1) * W]).then_inc(loaded[s], 16)
                for l in range(2):
                    with sp.Fori(1 - l, steps // 2) as i:
                        for s in range(2):
                            sp.wait_ge(product, steps * l + 2 * i + s - 1)
                            sp.dma_start(w[s][:], src[l][:, :, bass.ds((2 * i + s) * W, W)]).then_inc(loaded[s], 16)

            @block.tensor
            def _(pe):
                for l in range(2):
                    with pe.Fori(0, steps // 2) as i:
                        for s in range(2):
                            n = steps * l + 2 * i + s
                            pe.wait_ge(loaded[s], (steps * l // 2 + i + 1) * 16)
                            pe.wait_ge(copied, n)
                            for k in range(CT):
                                mm = pe.matmul(c.bank[s][0:2, :], cond[:, :, k], w[s][:, k, :],
                                               start=(k == 0), stop=(k == CT - 1))
                            mm.then_inc(product, 1)
                            pe.wait_ge(copied, n + 1)
                            pe.wait_ge(stored, n)
                            for q in range(4):
                                mm = pe.matmul(c.bank[2][:, 2 * q:2 * q + 2], row[s][:, q * P:(q + 1) * P],
                                               c.ident[0:2, 0:2], start=True, stop=True)
                            mm.then_inc(turned, 1)

            @block.scalar
            def _(act):
                for l in range(2):
                    with act.Fori(0, steps // 2) as i:
                        for s in range(2):
                            n = steps * l + 2 * i + s
                            act.wait_ge(product, n + 1)
                            act.wait_ge(turned, n)
                            nc.scalar.copy(row[s][:], c.bank[s][0:2, :]).then_inc(copied, 1)
                            act.wait_ge(copied, n + 1)

            @block.vector
            def _(dve):
                for l in range(2):
                    with dve.Fori(0, steps // 2) as i:
                        for s in range(2):
                            n = steps * l + 2 * i + s
                            dve.wait_ge(turned, n + 1)
                            at = bass.ds((2 * i + s) * 4, 4)
                            signal(dve, nc.vector.tensor_tensor(
                                c.mod[:, l, at, :], c.bank[2][:, 0:8].rearrange("p (q r) -> p q r", r=2),
                                c.par[:, bass.ds(PMODB + 48 * l + (2 * i + s) * 4, 4)].unsqueeze(2).to_broadcast([P, 4, 2]),
                                ALU.add), stored, n + 1)
                n = 0
                for l in range(2):
                    for kind, base in ((0, PNM), (1, PNF)):
                        for r in range(2):
                            nc.vector.scalar_tensor_tensor(
                                c.gain[:, l, kind, r, :], c.mod[:, l, 24 * kind + 8:24 * kind + 16, r], 1.0,
                                c.par[:, base + 8 * l:base + 8 * l + 8], ALU.add, ALU.mult).then_inc(gains, 1)


def load_tokens(c, d, h, spilled):
    nc = c.nc
    T = TOK // P
    with ExitStack() as ctx:
        xt = ctx.enter_context(nc.sbuf_tensor("xt", [P, T, D], F32))
        loaded = ctx.enter_context(nc.semaphore("x_loaded"))
        turned = ctx.enter_context(nc.semaphore("x_turned"))
        lat_copied = ctx.enter_context(nc.semaphore("x_lat_copied"))
        ctx_copied = ctx.enter_context(nc.semaphore("x_ctx_copied"))
        spill_done = ctx.enter_context(nc.semaphore("x_spilled"))
        with nc.Block() as block:
            @block.sync
            def _(sp):
                sp.dma_start(xt[:, 0:2, :], d["ctx"][0].rearrange("(t p) e -> p t e", p=P)).then_inc(loaded, 16)
                sp.dma_start(xt[:, 2:T, :], d["x"][0].rearrange("(t p) e -> p t e", p=P)).then_inc(loaded, 16)
                sp.wait_ge(lat_copied, CT)
                sp.wait_ge(ctx_copied, CT)
                sp.dma_start(spilled, h[:]).then_inc(spill_done, 16)
                sp.wait_ge(spill_done, 16)

            @block.tensor
            def _(pe):
                pe.wait_ge(loaded, 32)
                for k in range(CT):
                    s = 2 * (k % 2)
                    if k >= 2:
                        pe.wait_ge(lat_copied, k - 1)
                        pe.wait_ge(ctx_copied, k - 1)
                    for t in range(T):
                        out = c.bank[s][:, t * P:(t + 1) * P] if t < 2 else c.bank[s + 1][:, (t - 2) * P:(t - 1) * P]
                        mm = pe.transpose(out, xt[:, t, k * P:(k + 1) * P], c.ident[:])
                    mm.then_inc(turned, 1)

            @block.vector
            def _(dve):
                for k in range(CT):
                    dve.wait_ge(turned, k + 1)
                    nc.vector.tensor_copy(h[:, k, CTX:TOK], c.bank[2 * (k % 2) + 1][:, 0:LAT]).then_inc(lat_copied, 1)

            @block.scalar
            def _(act):
                for k in range(CT):
                    act.wait_ge(turned, k + 1)
                    nc.scalar.copy(h[:, k, 0:CTX], c.bank[2 * (k % 2)][:, 0:CTX]).then_inc(ctx_copied, 1)


def norm(c, name, h, layer, kind, out, segs):
    nc = c.nc
    with ExitStack() as ctx:
        sb = lambda n, s: ctx.enter_context(nc.sbuf_tensor(f"{name}_{n}", s, F32))
        sem = lambda n: ctx.enter_context(nc.semaphore(f"{name}_{n}"))
        sq = sb("sq", [P, 2, TOK])
        std = sb("std", [P, TOK])
        scaled = sb("scaled", [P, 2, TOK])
        squared, summed, rooted, inverted, normed, written = (
            sem(n) for n in ("squared", "summed", "rooted", "inverted", "normed", "written"))
        lo = segs[0][0]
        banks = {CTX: c.bank[0], 0: c.bank[1]}
        with nc.Block() as block:
            @block.tensor
            def _(pe):
                for k in range(CT):
                    pe.wait_ge(squared, k + 1)
                    for at, n in segs:
                        mm = pe.matmul(banks[at][:, 0:n], c.ones[:], sq[:, k % 2, at:at + n],
                                       start=(k == 0), stop=(k == CT - 1))
                    mm.then_inc(summed, 1)

            @block.scalar
            def _(act):
                for k in range(CT):
                    if k >= 2:
                        act.wait_ge(summed, k - 1)
                    nc.scalar.activation(sq[:, k % 2, lo:], h[:, k, lo:], ACT.Square).then_inc(squared, 1)
                    act.wait_ge(squared, k + 1)
                act.wait_ge(summed, CT)
                for at, n in segs:
                    nc.scalar.activation(std[:, at:at + n], banks[at][:, 0:n], ACT.Sqrt, scale=1.0 / D,
                                         bias=c.eps[:, 0:1]).then_inc(rooted, 1)
                for k in range(CT):
                    act.wait_ge(normed, k + 1)
                    for s, (at, n) in enumerate(segs):
                        r = 1 if at == 0 else 0
                        nc.scalar.activation(out(k, at, n), scaled[:, k % 2, at:at + n], ACT.Identity,
                                             scale=c.gain[:, layer, kind, r, k:k + 1],
                                             bias=c.mod[:, layer, 24 * kind + k, r:r + 1]).then_inc(written, 1)

            @block.vector
            def _(dve):
                dve.wait_ge(rooted, len(segs))
                signal(dve, nc.vector.reciprocal(std[:, lo:], std[:, lo:]), inverted, 1)
                for k in range(CT):
                    if k >= 2:
                        dve.wait_ge(written, len(segs) * (k - 1))
                    signal(dve, nc.vector.tensor_tensor(scaled[:, k % 2, lo:], h[:, k, lo:], std[:, lo:], ALU.mult),
                           normed, k + 1)


WID = TOK + 1
GSEG = ((0, 0, CTX), (CTX + 1, CTX, LAT))


def rwkv_inputs(c, d, apad, rkv, hidden):
    nc = c.nc
    with ExitStack() as ctx:
        sb = lambda n, s: ctx.enter_context(nc.sbuf_tensor(n, s, F32))
        sem = lambda n: ctx.enter_context(nc.semaphore(n))
        xx = sb("xx", [P, CT, WID])
        mix = [sb(f"mix{s}", [P, CT, WID]) for s in range(2)]
        w = [sb(f"proj_w{s}", [P, CT, P]) for s in range(2)]
        shifted, mixed, used = sem("shifted"), sem("mixed"), sem("mix_used")
        loaded = [sem(f"proj_w_loaded{s}") for s in range(2)]
        product, evac_lat, evac_ctx = sem("proj_product"), sem("proj_lat_copied"), sem("proj_ctx_copied")
        order = sem("rwkv_in_order")
        small = (d["rw_w1"][0].rearrange("e (k p) r -> p k e r", p=P),
                 d["rw_a1"][0].rearrange("e (k p) r -> p k e r", p=P),
                 d["rw_g1"][0].rearrange("(k p) r -> p k r", p=P))
        large = [d[n][0].rearrange("(k p) e -> p k e", p=P) for n in ("rw_wr", "rw_wk", "rw_wv")]
        MIXES = (1, 4, 5, 0, 2, 3)
        with nc.Block() as block:
            @block.sync
            def _(sp):
                for n in range(3):
                    if n >= 2:
                        sp.wait_ge(product, n - 1)
                    if n < 2:
                        for e in range(2):
                            sp.dma_start(w[n % 2][:, :, 64 * e:64 * e + 64], small[n][:, :, e, :])\
                                .then_inc(loaded[n % 2], 16)
                    else:
                        sp.dma_start(w[0][:], small[2]).then_inc(loaded[0], 16)
                for m in range(3):
                    with sp.Fori(0, CT // 2) as i:
                        for s in range(2):
                            n = 3 + CT * m + 2 * i + s
                            sp.wait_ge(product, n - 1)
                            sp.dma_start(w[1 - s][:], large[m][:, :, bass.ds((2 * i + s) * P, P)])\
                                .then_inc(loaded[1 - s], 16)

            def evac_bank(n_mod):
                return c.bank[2 * n_mod], c.bank[2 * n_mod + 1]

            @block.tensor
            def _(pe):
                def tile(n, slot, x, loads):
                    pe.wait_ge(loaded[slot], 16 * loads)
                    bctx, blat = evac_bank(slot)
                    for k in range(CT):
                        for (g, at, width), bank in zip(GSEG, (bctx, blat)):
                            mm = pe.matmul(bank[:, 0:width], w[slot][:, k, :], x[:, k, g:g + width],
                                           start=(k == 0), stop=(k == CT - 1))
                    return mm

                for n in range(3):
                    if n == 2:
                        pe.wait_ge(evac_lat, 1)
                        pe.wait_ge(evac_ctx, 1)
                    pe.wait_ge(mixed, CT * (n + 1))
                    tile(n, n % 2, mix[n % 2], (2, 2, 3)[n]).then_inc(product, 1)
                for m in range(3):
                    pe.wait_ge(mixed, CT * (4 + m))
                    with pe.Fori(0, CT // 2) as i:
                        for s in range(2):
                            n = 3 + CT * m + 2 * i + s
                            pe.wait_ge(evac_lat, n - 1)
                            pe.wait_ge(evac_ctx, n - 1)
                            base = 2 if s == 0 else 3
                            tile(n, 1 - s, mix[(3 + m) % 2], CT // 2 * m + i + 1 + base).then_inc(product, 1)

            @block.vector
            def _(dve):
                step = Order(dve, order)
                with dve.Fori(0, CT) as k:
                    step.enter(k, 1)
                    step(nc.vector.tensor_tensor(xx[:, k, :], apad[:, k, 0:WID], apad[:, k, 2:WID + 2], ALU.add))
                    signal(dve, nc.vector.scalar_tensor_tensor(xx[:, k, :], xx[:, k, :], 0.5, apad[:, k, 1:WID + 1],
                                                               ALU.mult, ALU.subtract), shifted, k + 1)
                    step.leave(CT)

                def mixes(q):
                    if q >= 2:
                        dve.wait_ge(product, (1, 2, 3, 3 + CT)[q - 2])
                    with dve.Fori(0, CT) as k:
                        signal(dve, nc.vector.scalar_tensor_tensor(
                            mix[q % 2][:, k, :], xx[:, k, :], c.par[:, bass.ds(PMU + 8 * MIXES[q] + k, 1)],
                            apad[:, k, 1:WID + 1], ALU.mult, ALU.add), mixed, CT * q + k + 1)

                def copies(m):
                    with dve.Fori(0, CT // 2) as i:
                        for s in range(2):
                            n = 3 + CT * m + 2 * i + s
                            dve.wait_ge(product, n + 1)
                            signal(dve, nc.vector.tensor_copy(rkv[m][:, 2 * i + s, CTX:TOK],
                                                              evac_bank(1 - s)[1][:, 0:LAT]), evac_lat, n + 1)

                mixes(0), mixes(1), mixes(2), mixes(3), mixes(4)
                for m in range(3):
                    copies(m)
                    if m == 0:
                        mixes(5)

            @block.scalar
            def _(act):
                for n, f in enumerate((ACT.Tanh, ACT.Copy, ACT.Sigmoid)):
                    act.wait_ge(product, n + 1)
                    bctx, blat = evac_bank(n % 2)
                    nc.scalar.activation(hidden[:, n, CTX:TOK], blat[:, 0:LAT], f).then_inc(evac_lat, 1)
                    signal(act, nc.scalar.activation(hidden[:, n, 0:CTX], bctx[:, 0:CTX], f), evac_ctx, n + 1)
                for m in range(3):
                    with act.Fori(0, CT // 2) as i:
                        for s in range(2):
                            n = 3 + CT * m + 2 * i + s
                            act.wait_ge(product, n + 1)
                            signal(act, nc.scalar.copy(rkv[m][:, 2 * i + s, 0:CTX], evac_bank(1 - s)[0][:, 0:CTX]),
                                   evac_ctx, n + 1)


def half(h):
    return slice(CH * h, CH * h + CH)


def recurrence(c, d, rkv, hidden):
    nc = c.nc
    with ExitStack() as ctx:
        sb = lambda n, s: ctx.enter_context(nc.sbuf_tensor(n, s, F32))
        sem = lambda n: ctx.enter_context(nc.semaphore(n))
        cols = sb("pair_params", [P, 10])
        W0, A0, KK, KA, RK, LG, LB, LESS = 0, 2, 4, 5, 6, 7, 8, 9
        col = lambda n: cols[:, n:n + 1]
        lora_w = sb("lora_w", [P, 3, P])
        kk = sb("kk", [P, TOK])
        tmp = sb("tmp", [P, TOK])
        sig_w = [sb(f"sig_w{e}", [P, TOK]) for e in range(2)]
        cum = [sb(f"cum{e}", [P, TOK]) for e in range(2)]
        b_in = [sb(f"b_in{e}", [P, TOK]) for e in range(2)]
        k_in = [sb(f"k_in{e}", [P, TOK]) for e in range(2)]
        ep = [sb(f"ep{e}", [P, NCH, CH + 1]) for e in range(2)]
        ar = [sb(f"ar{e}", [P, NCH, 2, CH]) for e in range(2)]
        gate = sb("gate", [P, TOK])
        bk = sb("bk", [P, 2, 4, P])
        vbd = sb("vbd", [P, 4, P])
        arbd = [sb(f"arbd{p}", [P, 4, 2, P]) for p in range(2)]
        sc = [sb(f"sc{p}", [P, 4, 4, P]) for p in range(2)]
        tok = [sb(f"tok{p}", [P, 3, 4, P]) for p in range(2)]
        xt = [sb(f"xt{p}", [P, 4, P]) for p in range(2)]
        x = sb("x_inv", [P, 4, P])
        t_sb = sb("t_sb", [P, 4, P])
        lvl = [sb(f"lvl{n}", [P, 4, P]) for n in range(2)]
        rhs = sb("rhs_u", [P, 2, P])
        u_sb = sb("u_sb", [P, 2, P])
        state = [sb(f"state{q}", [P, 2, P]) for q in range(2)]
        decayed = sb("decayed", [P, 2, P])

        zeroed = sem("zeroed")
        lora_loaded = sem("lora_loaded")
        lora_used = sem("lora_used")
        maps, sigm, gated = sem("lora_maps"), sem("sigmoids"), sem("gate_copied")
        kk_raw, kk_sq, head_sum, sum_read, kk_root = (sem(n) for n in (
            "kk_raw", "kk_squared", "head_sums", "head_sums_read", "kk_root"))
        cumd, decays = sem("decay_sums"), sem("decays")
        bonus_in, features, pair_done = sem("bonus_in"), sem("features"), sem("pair_done")
        dve_order = sem("dve_order")
        bd_dve, bd_act = sem("bk_placed"), sem("ar_v_placed")
        scores, masked = sem("scores"), sem("scores_masked")
        turned, tok_copied = sem("bkv_turned"), sem("bkv_copied")
        lvl_ready, t_ready, t_copied, x_ready, x_added, xt_added = (sem(n) for n in (
            "level_masked", "t_product", "t_copied", "x_products", "x_added", "xt_added"))
        rhs_ready, rhs_copied, u_ready, u_copied = (sem(n) for n in ("rhs_ready", "rhs_copied", "u_ready", "u_copied"))
        s_decayed, s_ready, s_done = sem("state_decayed"), sem("state_products"), sem("state_done")
        y_ready, y_copied = sem("y_ready"), sem("y_copied")
        centred, y_sq, y_sum, y_mean, y_root = (sem(n) for n in (
            "y_centred", "y_squared", "y_summed", "y_in", "y_root"))
        bank = c.bank
        ones_head = c.ones_head
        ident4 = c.ident[:].unsqueeze(1).to_broadcast([P, 4, P])

        def blocks(j):
            return j, (NB + 1 - j) % NB

        def chunks(tile):
            return tile.rearrange("p (n t) -> p n t", t=CH)

        def units(q):
            return q, 2 + 1 - q

        def schedule(inv, inv_level, rhs_, u_, sy, y_out, ct):
            def together(i_g, i_j, i_p, c_g, c_j, c_p):
                if i_g is not None:
                    inv(i_g, i_j, i_p, 0)
                if c_g is not None:
                    rhs_(c_g, c_j, c_p, 0)
                if i_g is not None:
                    inv(i_g, i_j, i_p, 1)
                if c_g is not None:
                    u_(c_g, c_j, c_p, 0)
                if i_g is not None:
                    inv_level(i_g, i_p, 0)
                    inv_level(i_g, i_p, 1)
                if c_g is not None:
                    sy(c_g, c_j, c_p, 0)
                if i_g is not None:
                    inv_level(i_g, i_p, 2)
                if c_g is not None:
                    rhs_(c_g, c_j, c_p, 1)
                if i_g is not None:
                    inv_level(i_g, i_p, 3)
                if c_g is not None:
                    u_(c_g, c_j, c_p, 1)
                if i_g is not None:
                    inv_level(i_g, i_p, 4)
                if c_g is not None:
                    sy(c_g, c_j, c_p, 1)
                if i_g is not None:
                    inv_level(i_g, i_p, 5)
                if c_g is not None:
                    y_out(c_g, c_j, c_p)
            return together

        def batches(ct, together):
            g = ct * NB
            together(g, 0, 0, None, None, None)
            for j in range(1, NB):
                together(g + j, j, j % 2, g + j - 1, j - 1, (j - 1) % 2)
            together(None, None, None, g + NB - 1, NB - 1, (NB - 1) % 2)

        with nc.Block() as block:
            @block.sync
            def _(sp):
                with sp.Fori(0, CT) as ct:
                    sp.wait_ge(lora_used, ct)
                    cols = bass.ds(ct * P, P)
                    sp.dma_start(lora_w[:, 0, :], d["rw_w2"][0].rearrange("e r n -> (e r) n")[:, cols])\
                        .then_inc(lora_loaded, 16)
                    sp.dma_start(lora_w[:, 1, :], d["rw_a2"][0].rearrange("e r n -> (e r) n")[:, cols])\
                        .then_inc(lora_loaded, 16)
                    sp.dma_start(lora_w[:, 2, :], d["rw_g2"][0][:, cols]).then_inc(lora_loaded, 16)

            @block.tensor
            def _(pe):
                def head_sums(src, b, n):
                    for (out, at, width) in tokens(bank[b], bank[b + 1]):
                        mm = pe.matmul(out, ones_head[:], src[:, at:at + width], start=True, stop=True)
                    mm.then_inc(head_sum, 1)

                def inv(g, j, p, part):
                    if part == 0:
                        pe.wait_ge(bd_dve, g + 1)
                        pe.wait_ge(bd_act, g + 1)
                        for s in range(2):
                            pe.wait_ge(tok_copied, 3 * g)
                            pe.wait_ge(masked, 2 * g + s)
                            for e, b in enumerate(blocks(j)):
                                for n in range(2):
                                    mm = pe.matmul(bank[s][:, 256 * e + 128 * n:256 * e + 128 * n + 128],
                                                   bk[:, n, 2 * e + s, :],
                                                   ar[e][:].rearrange("p n k t -> p (n k t)")[:, (2 * b + s) * P:(2 * b + s + 1) * P],
                                                   start=True, stop=True)
                            mm.then_inc(scores, 1)
                    else:
                        for n, (b, src) in enumerate(((0, bk[:, 0]), (1, bk[:, 1]), (0, vbd))):
                            if n < 2:
                                pe.wait_ge(masked, 2 * g + n + 1)
                            else:
                                pe.wait_ge(tok_copied, 3 * g + 1)
                            for u in range(4):
                                mm = pe.transpose(bank[b][:, u * P:(u + 1) * P], src[:, u, :], c.ident[:])
                            mm.then_inc(turned, 1)

                def inv_level(g, p, n):
                    pe.wait_ge(lvl_ready, LEVELS * g + n + 1)
                    if n == 0:
                        pe.wait_ge(x_added, (LEVELS - 1) * g)
                        for u in range(4):
                            mm = pe.matmul(bank[3][:, u * P:(u + 1) * P], lvl[0][:, u, :], c.ident[:],
                                           start=True, stop=True)
                        mm.then_inc(x_ready, 1)
                        return
                    pe.wait_ge(x_added, (LEVELS - 1) * g + n)
                    pe.wait_ge(xt_added, LEVELS * g + n)
                    pe.wait_ge(t_copied, (LEVELS - 1) * g + n - 1)
                    for u in range(4):
                        mm = pe.matmul(bank[2][:, u * P:(u + 1) * P], lvl[n % 2][:, u, :], x[:, u, :],
                                       start=True, stop=True)
                    mm.then_inc(t_ready, 1)
                    pe.wait_ge(t_copied, (LEVELS - 1) * g + n)
                    for u in range(4):
                        mm = pe.matmul(bank[4][:, u * P:(u + 1) * P], t_sb[:, u, :], xt[p][:, u, :],
                                       start=True, stop=True)
                        if n < LEVELS - 1:
                            mm = pe.matmul(bank[3][:, u * P:(u + 1) * P], xt[p][:, u, :], t_sb[:, u, :],
                                           start=True, stop=True)
                    mm.then_inc(x_ready, 1)

                def rhs_(g, j, p, q):
                    pe.wait_ge(tok_copied, 3 * g + 3)
                    pe.wait_ge(s_done, (2 * g + q) * 2)
                    pe.wait_ge(u_copied, 2 * g + q)
                    for e, u in enumerate(units(q)):
                        out = bank[5][:, e * P:(e + 1) * P]
                        pe.matmul(out, sc[p][:, u, 2, :], tok[p][:, 2, u, :], start=True, stop=False)
                        mm = pe.matmul(out, arbd[p][:, u, 0, :], state[q][:, e, :], start=False, stop=True)
                    mm.then_inc(rhs_ready, 1)

                def u_(g, j, p, q):
                    pe.wait_ge(rhs_copied, 2 * g + q + 1)
                    pe.wait_ge(xt_added, LEVELS * (g + 1))
                    for e, u in enumerate(units(q)):
                        mm = pe.matmul(bank[5][:, 256 + e * P:256 + (e + 1) * P], xt[p][:, u, :], rhs[:, e, :],
                                       start=True, stop=True)
                    mm.then_inc(u_ready, 1)

                def sy(g, j, p, q):
                    pe.wait_ge(u_copied, 2 * g + q + 1)
                    for e, u in enumerate(units(q)):
                        out = bank[6][:, e * P:(e + 1) * P]
                        pe.matmul(out, tok[p][:, 1, u, :], tok[p][:, 2, u, :], start=True, stop=False)
                        mm = pe.matmul(out, tok[p][:, 0, u, :], u_sb[:, e, :], start=False, stop=True)
                    mm.then_inc(s_ready, 1)
                    if q == 0:
                        pe.wait_ge(y_copied, g)
                    for e, u in enumerate(units(q)):
                        out = bank[7][:, u * P:(u + 1) * P]
                        pe.matmul(out, state[q][:, e, :], arbd[p][:, u, 1, :], start=True, stop=False)
                        pe.matmul(out, tok[p][:, 2, u, :], sc[p][:, u, 3, :], start=False, stop=False)
                        mm = pe.matmul(out, u_sb[:, e, :], sc[p][:, u, 1, :], start=False, stop=True)
                    mm.then_inc(y_ready, 1)

                pe.wait_ge(zeroed, 1)
                together = schedule(inv, inv_level, rhs_, u_, sy, lambda g, j, p: None, None)
                with pe.Fori(0, CT) as ct:
                    pe.wait_ge(lora_loaded, 48 * (ct + 1))
                    pe.wait_ge(pair_done, ct)
                    for n in range(5):
                        if n == 4:
                            pe.wait_ge(sigm, 8 * ct + 2)
                        b = 2 * (n % 4)
                        rows = slice(64 * (n % 2), 64 * (n % 2) + 64) if n < 4 else slice(0, P)
                        for (out, at, width) in tokens(bank[b], bank[b + 1]):
                            mm = pe.matmul(out, lora_w[rows, n // 2, :], hidden[rows, n // 2, at:at + width],
                                           start=True, stop=True)
                        if n == 4:
                            mm.then_inc(lora_used, 1)
                        else:
                            mm.then_inc(maps, 1)
                    pe.wait_ge(kk_sq, ct + 1)
                    pe.wait_ge(sigm, 8 * ct + 4)
                    head_sums(tmp, 2, 0)
                    pe.wait_ge(bonus_in, ct + 1)
                    pe.wait_ge(sigm, 8 * ct + 6)
                    head_sums(tmp, 4, 1)
                    pe.wait_ge(features, ct + 1)
                    pe.wait_ge(gated, 2 * (ct + 1))
                    batches(ct, together)
                    pe.wait_ge(y_mean, ct + 1)
                    head_sums(cum[0], 0, 2)
                    pe.wait_ge(y_sq, ct + 1)
                    head_sums(tmp, 2, 3)

            @block.vector
            def _(dve):
                step = Order(dve, dve_order)
                v = nc.vector

                def inv(g, j, p, part):
                    if part == 0:
                        dve.wait_ge(turned, 3 * g)
                        if j:
                            dve.wait_ge(y_ready, 2 * g - 2)
                        for n, src in enumerate((b_in, k_in)):
                            for e, b in enumerate(blocks(j)):
                                for h in range(2):
                                    ins = v.tensor_copy(bk[half(h), n, 2 * e:2 * e + 2, half(h)],
                                                        chunks(src[e][half(h), 2 * b * CH:2 * (b + 1) * CH]))
                                    if (n, e, h) == (1, 1, 1):
                                        signal(dve, ins, bd_dve, g + 1)
                        for s in range(2):
                            dve.wait_ge(scores, 2 * g + s + 1)
                            for h in range(2):
                                psum = bank[s][half(h), :].rearrange("p (e k t) -> p e k t", e=2, t=CH)
                                ins = v.tensor_tensor(sc[p][half(h), s:s + 3:2, :, half(h)], psum,
                                                      c.score_mask[half(h), :, :, :], ALU.mult)
                                if h:
                                    signal(dve, ins, masked, 2 * g + s + 1)

                def inv_level(g, p, n):
                    if n == 0:
                        dve.wait_ge(lvl_ready, LEVELS * g + 1)
                        signal(dve, v.tensor_tensor(xt[p][:], lvl[0][:], ident4, ALU.add), xt_added, LEVELS * g + 1)
                        dve.wait_ge(x_ready, LEVELS * g + 1)
                        signal(dve, v.tensor_tensor(x[:], bank[3][:].rearrange("p (u t) -> p u t", t=P), ident4, ALU.add),
                               x_added, (LEVELS - 1) * g + 1)
                        return
                    dve.wait_ge(x_ready, LEVELS * g + n + 1)
                    signal(dve, v.tensor_tensor(xt[p][:], bank[4][:].rearrange("p (u t) -> p u t", t=P), xt[p][:],
                                                ALU.add), xt_added, LEVELS * g + n + 1)
                    if n < LEVELS - 1:
                        signal(dve, v.tensor_tensor(x[:], bank[3][:].rearrange("p (u t) -> p u t", t=P), x[:], ALU.add),
                               x_added, (LEVELS - 1) * g + n + 1)

                def sy(g, j, p, q):
                    dve.wait_ge(s_ready, 2 * g + q + 1)
                    dve.wait_ge(s_decayed, 2 * (2 * g + q + 1))
                    dve.wait_ge(y_ready, 2 * g + q)
                    for e, b in enumerate(blocks(j)):
                        n = 2 * b + (q if e == 0 else 1 - q)
                        signal(dve, v.scalar_tensor_tensor(
                            state[1 - q][:, e, :], bank[6][:, e * P:(e + 1) * P], chunk_end(e, n),
                            decayed[:, e, :], ALU.mult, ALU.add), s_done, 2 * (2 * g + q) + e + 1)

                def chunk_end(e, n):
                    at = n * (CH + 1) + (CH if e == 0 else 0)
                    return ep[e][:].rearrange("p n t -> p (n t)")[:, at:at + 1]

                nop = lambda *a: None
                for t in (bk, vbd, arbd[0], arbd[1], sc[0], sc[1]):
                    step(v.memset(t[:], 0.0))
                step(v.memset(ep[0][:, :, 0:1], 1.0))
                step(v.memset(ep[1][:, :, CH:CH + 1], 1.0))
                signal(dve, v.memset(kk[:], 0.0), zeroed, 1)
                together = schedule(inv, inv_level, nop, nop, sy, nop, None)
                with dve.Fori(0, CT) as ct:
                    step.enter(ct, DVE_STEPS)
                    if True:
                        step(v.tensor_copy(cols[:], c.par[:, PW0:PW0 + 10 * CT].rearrange("p (n k) -> p n k", k=CT)
                                           [:, :, bass.ds(ct, 1)].rearrange("p n k -> p (n k)")))
                        signal(dve, v.tensor_scalar(kk[:], rkv[1][:, ct, :], col(KK), None,
                                                    ALU.mult), kk_raw, ct + 1)
                        dve.wait_ge(sigm, 8 * ct + 2)
                        signal(dve, v.tensor_tensor_scan(cum[0][:], c.keep[:], sig_w[0][:], 0.0, ALU.mult, ALU.add),
                               cumd, 2 * ct + 1)
                        dve.wait_ge(sigm, 8 * ct + 4)
                        signal(dve, v.tensor_tensor_scan(cum[1][:, ::-1], c.keep[:], sig_w[1][:, ::-1], 0.0,
                                                         ALU.mult, ALU.add), cumd, 2 * ct + 2)
                        dve.wait_ge(head_sum, 4 * ct + 1)
                        for n, (src, at, width) in enumerate(tokens(bank[2], bank[3])):
                            signal(dve, v.tensor_scalar(tmp[:, at:at + width], src, 1e-24, None, ALU.max),
                                   sum_read, 2 * ct + n + 1)
                        dve.wait_ge(kk_root, ct + 1)
                        step(v.reciprocal(tmp[:], tmp[:]))
                        step(v.tensor_tensor(kk[:], kk[:], tmp[:], ALU.mult))
                        dve.wait_ge(sigm, 8 * ct + 8)
                        for e in range(2):
                            step(v.tensor_scalar(k_in[e][:], b_in[e][:], col(KA),
                                                 col(LESS), ALU.mult, ALU.add))
                            step(v.tensor_tensor(k_in[e][:], k_in[e][:], rkv[1][:, ct, :], ALU.mult))
                            step(v.tensor_tensor(b_in[e][:], b_in[e][:], kk[:], ALU.mult))
                        step(v.tensor_tensor(tmp[:], k_in[0][:], k_in[1][:], ALU.add))
                        signal(dve, v.scalar_tensor_tensor(tmp[:], tmp[:], col(RK),
                                                           rkv[0][:, ct, :], ALU.mult, ALU.mult), bonus_in, ct + 1)
                        dve.wait_ge(decays, 4 * (ct + 1))
                        for e in range(2):
                            before = ep[e][:, :, 0:CH] if e == 0 else ep[e][:, :, 1:CH + 1]
                            through = ep[e][:, :, 1:CH + 1] if e == 0 else ep[e][:, :, 0:CH]
                            step(v.scalar_tensor_tensor(ar[e][:, :, 0, :], chunks(kk[:]), -1.0, before, ALU.mult, ALU.mult))
                            step(v.tensor_tensor(ar[e][:, :, 1, :], chunks(rkv[0][:, ct, :]), through, ALU.mult))
                            step(v.tensor_tensor(b_in[e][:], b_in[e][:], sig_w[e][:], ALU.mult))
                            step(v.tensor_tensor(k_in[e][:], k_in[e][:], sig_w[e][:], ALU.mult))
                        dve.wait_ge(head_sum, 4 * ct + 2)
                        for src, at, width in tokens(bank[4], bank[5]):
                            step(v.tensor_tensor(sig_w[0][:, at:at + width], src, rkv[2][:, ct, at:at + width], ALU.mult))
                        dve.wait_ge(y_ready, 2 * NB * ct)
                        signal(dve, v.memset(state[0][:], 0.0), features, ct + 1)
                        batches(ct, together)
                        dve.wait_ge(y_copied, NB * (ct + 1))
                        signal(dve, v.tensor_tensor(cum[0][:], cum[0][:], cum[1][:], ALU.add), y_mean, ct + 1)
                        dve.wait_ge(head_sum, 4 * ct + 3)
                        for n, (src, at, width) in enumerate(tokens(bank[0], bank[1])):
                            signal(dve, v.scalar_tensor_tensor(cum[0][:, at:at + width], src, -1.0 / CH,
                                                               cum[0][:, at:at + width], ALU.mult, ALU.add),
                                   centred, 2 * ct + n + 1)
                        dve.wait_ge(y_root, 2 * (ct + 1))
                        step(v.reciprocal(tmp[:], tmp[:]))
                        step(v.tensor_tensor(cum[0][:], cum[0][:], tmp[:], ALU.mult))
                        step(v.tensor_scalar(cum[0][:], cum[0][:], col(LG),
                                             col(LB), ALU.mult, ALU.add))
                        step(v.tensor_tensor(cum[0][:], cum[0][:], sig_w[0][:], ALU.add))
                        dve.wait_ge(gated, 2 * (ct + 1))
                        signal(dve, v.tensor_tensor(rkv[0][:, ct, :], cum[0][:], gate[:], ALU.mult), pair_done, ct + 1)
                    step.leave(CT)

            @block.scalar
            def _(act):
                a = nc.scalar

                def inv(g, j, p, part):
                    if part == 0:
                        act.wait_ge(turned, 3 * g)
                        if j:
                            act.wait_ge(y_ready, 2 * g - 2)
                        for e, b in enumerate(blocks(j)):
                            for h in range(2):
                                a.copy(arbd[p][half(h), 2 * e:2 * e + 2, :, half(h)],
                                       ar[e][half(h), 2 * b:2 * b + 2, :, :])
                                ins = a.copy(vbd[half(h), 2 * e:2 * e + 2, half(h)],
                                             chunks(rkv[2][half(h), act_ct[0], 2 * b * CH:2 * (b + 1) * CH]))
                                if (e, h) == (1, 1):
                                    signal(act, ins, bd_act, g + 1)
                    else:
                        for n in range(3):
                            act.wait_ge(turned, 3 * g + n + 1)
                            signal(act, a.copy(tok[p][:, n], bank[n % 2][:].rearrange("p (u t) -> p u t", t=P)),
                                   tok_copied, 3 * g + n + 1)

                def inv_level(g, p, n):
                    if n:
                        act.wait_ge(t_ready, (LEVELS - 1) * g + n)
                        act.wait_ge(x_ready, LEVELS * g + n)
                        signal(act, a.copy(t_sb[:], bank[2][:].rearrange("p (u t) -> p u t", t=P)),
                               t_copied, (LEVELS - 1) * g + n)

                def rhs_(g, j, p, q):
                    act.wait_ge(rhs_ready, 2 * g + q + 1)
                    signal(act, a.copy(rhs[:], bank[5][:, 0:256].rearrange("p (e t) -> p e t", t=P)),
                           rhs_copied, 2 * g + q + 1)

                def u_(g, j, p, q):
                    act.wait_ge(u_ready, 2 * g + q + 1)
                    act.wait_ge(y_ready, 2 * g + q)
                    signal(act, a.copy(u_sb[:], bank[5][:, 256:512].rearrange("p (e t) -> p e t", t=P)),
                           u_copied, 2 * g + q + 1)

                def y_out(g, j, p):
                    act.wait_ge(y_ready, 2 * g + 2)
                    for e, b in enumerate(blocks(j)):
                        for h in range(2):
                            ins = a.copy(chunks(cum[e][half(h), 2 * b * CH:2 * (b + 1) * CH]),
                                         bank[7][half(h), 256 * e:256 * e + 256].rearrange("p (s t) -> p s t", t=P)[:, :, half(h)])
                            if (e, h) == (1, 1):
                                signal(act, ins, y_copied, g + 1)

                act_ct = [None]
                act.wait_ge(zeroed, 1)
                together = schedule(inv, inv_level, rhs_, u_, lambda *_: None, y_out, None)
                with act.Fori(0, CT) as ct:
                    act_ct[0] = ct
                    act.wait_ge(kk_raw, ct + 1)
                    signal(act, a.activation(tmp[:], kk[:], ACT.Square), kk_sq, ct + 1)
                    for n, (dst, param) in enumerate(((sig_w[0], W0), (sig_w[1], W0 + 1), (b_in[0], A0), (b_in[1], A0 + 1))):
                        act.wait_ge(maps, 4 * ct + n + 1)
                        for m, (src, at, width) in enumerate(tokens(bank[2 * n], bank[2 * n + 1])):
                            signal(act, a.activation(dst[:, at:at + width], src, ACT.Sigmoid,
                                                     bias=col(param)), sigm, 8 * ct + 2 * n + m + 1)
                    act.wait_ge(lora_used, ct + 1)
                    for n, (src, at, width) in enumerate(tokens(bank[0], bank[1])):
                        signal(act, a.copy(gate[:, at:at + width], src), gated, 2 * ct + n + 1)
                    for e in range(2):
                        act.wait_ge(cumd, 2 * ct + e + 1)
                        through = ep[e][:, :, 1:CH + 1] if e == 0 else ep[e][:, :, 0:CH]
                        signal(act, a.activation(through, chunks(cum[e][:]), ACT.Exp, scale=-DECAY), decays, 4 * ct + 2 * e + 1)
                        signal(act, a.activation(sig_w[e][:], cum[e][:], ACT.Exp, scale=DECAY), decays, 4 * ct + 2 * e + 2)
                    act.wait_ge(sum_read, 2 * (ct + 1))
                    signal(act, a.activation(tmp[:], tmp[:], ACT.Sqrt), kk_root, ct + 1)
                    act.wait_ge(features, ct + 1)
                    batches(ct, together)
                    act.wait_ge(centred, 2 * (ct + 1))
                    signal(act, a.activation(tmp[:], cum[0][:], ACT.Square), y_sq, ct + 1)
                    act.wait_ge(head_sum, 4 * (ct + 1))
                    for n, (src, at, width) in enumerate(tokens(bank[2], bank[3])):
                        signal(act, a.activation(tmp[:, at:at + width], src, ACT.Sqrt, scale=1.0 / CH, bias=c.eps[:, 1:2]),
                               y_root, 2 * ct + n + 1)
                    act.wait_ge(pair_done, ct + 1)

            @block.gpsimd
            def _(pool):
                def inv_level(g, p, n):
                    if n == 0:
                        pool.wait_ge(masked, 2 * g + 2)
                    if n == 2:
                        pool.wait_ge(xt_added, LEVELS * g + 1)
                    pool.wait_ge(x_ready, LEVELS * g + max(n - 1, 0))
                    for e in range(2):
                        ins = nc.gpsimd.tensor_tensor(
                            lvl[n % 2][:, 2 * e:2 * e + 2, :], sc[p][:, 2 * e:2 * e + 2, 0, :],
                            c.level_mask[:, n, e, :].unsqueeze(1).to_broadcast([P, 2, P]), ALU.mult)
                        if e:
                            signal(pool, ins, lvl_ready, LEVELS * g + n + 1)

                def rhs_(g, j, p, q):
                    pool.wait_ge(s_done, 2 * (2 * g + q))
                    if q == 0:
                        pool.wait_ge(features, pool_ct[0] + 1)
                    for e, b in enumerate(blocks(j)):
                        n = 2 * b + (q if e == 0 else 1 - q)
                        at = n * (CH + 1) + (CH if e == 0 else 0)
                        signal(pool, nc.gpsimd.tensor_tensor(
                            decayed[:, e, :], state[q][:, e, :],
                            ep[e][:].rearrange("p n t -> p (n t)")[:, at:at + 1].to_broadcast([P, P]), ALU.mult),
                            s_decayed, 2 * (2 * g + q) + e + 1)

                nop = lambda *a: None
                pool_ct = [None]
                together = schedule(nop, inv_level, rhs_, nop, nop, nop, None)
                with pool.Fori(0, CT) as ct:
                    pool_ct[0] = ct
                    batches(ct, together)


DVE_STEPS = 24


def zero_padding(c, apad):
    nc = c.nc
    with ExitStack() as ctx:
        padded = ctx.enter_context(nc.semaphore("padded"))
        with nc.Block() as block:
            @block.vector
            def _(dve):
                for at in (0, CTX + 1, TOK + 2):
                    nc.vector.memset(apad[:, :, at:at + 1], 0.0).then_inc(padded, 1)
                dve.wait_ge(padded, 3)


def dense(c, name, weight, k_tiles, m_tiles, rhs, segs, h, layer, gate_row):
    nc = c.nc
    with ExitStack() as ctx:
        w = [ctx.enter_context(nc.sbuf_tensor(f"{name}_w{s}", [P, k_tiles, P], F32)) for s in range(2)]
        loaded = [ctx.enter_context(nc.semaphore(f"{name}_w_loaded{s}")) for s in range(2)]
        product = ctx.enter_context(nc.semaphore(f"{name}_product"))
        added = ctx.enter_context(nc.semaphore(f"{name}_added"))
        view = weight.rearrange("(k p) e -> p k e", p=P)
        with nc.Block() as block:
            @block.sync
            def _(sp):
                for s in range(2):
                    sp.dma_start(w[s][:], view[:, :, s * P:(s + 1) * P]).then_inc(loaded[s], 16)
                with sp.Fori(1, m_tiles // 2) as i:
                    for s in range(2):
                        sp.wait_ge(product, 2 * i + s - 1)
                        sp.dma_start(w[s][:], view[:, :, bass.ds((2 * i + s) * P, P)]).then_inc(loaded[s], 16)

            @block.tensor
            def _(pe):
                def pair(i, first):
                    for s in range(2):
                        pe.wait_ge(loaded[s], 16 * (i + 1))
                        if not first:
                            pe.wait_ge(added, len(segs) * (2 * i + s - 1))
                        for k in range(k_tiles):
                            for n, (at, width) in enumerate(segs):
                                mm = pe.matmul(c.bank[2 * s + n][:, 0:width], w[s][:, k, :], rhs(k, at, width),
                                               start=(k == 0), stop=(k == k_tiles - 1))
                        mm.then_inc(product, 1)

                pair(0, True)
                with pe.Fori(1, m_tiles // 2) as i:
                    pair(i, False)

            @block.vector
            def _(dve):
                with dve.Fori(0, m_tiles // 2) as i:
                    for s in range(2):
                        m = 2 * i + s
                        dve.wait_ge(product, m + 1)
                        for n, (at, width) in enumerate(segs):
                            r = 1 if at == 0 else 0
                            gate = c.mod[:, layer, :, r][:, bass.ds(gate_row + m, 1)]
                            signal(dve, nc.vector.scalar_tensor_tensor(
                                h[:, m, at:at + width], c.bank[2 * s + n][:, 0:width], gate, h[:, m, at:at + width],
                                ALU.mult, ALU.add), added, len(segs) * m + n + 1)


def swiglu_up(c, name, w1, w3, f, segs, g):
    nc = c.nc
    with ExitStack() as ctx:
        w = [ctx.enter_context(nc.sbuf_tensor(f"{name}_w{s}", [P, 2, CT, P], F32)) for s in range(2)]
        silu = [ctx.enter_context(nc.sbuf_tensor(f"{name}_silu{s}", [P, TOK], F32)) for s in range(2)]
        loaded = [ctx.enter_context(nc.semaphore(f"{name}_w_loaded{s}")) for s in range(2)]
        product = ctx.enter_context(nc.semaphore(f"{name}_product"))
        activated = ctx.enter_context(nc.semaphore(f"{name}_activated"))
        multiplied = ctx.enter_context(nc.semaphore(f"{name}_multiplied"))
        views = [x.rearrange("(k p) e -> p k e", p=P) for x in (w1, w3)]
        ns = len(segs)
        with nc.Block() as block:
            @block.sync
            def _(sp):
                def load(s, cols):
                    for n in range(2):
                        sp.dma_start(w[s][:, n], views[n][:, :, cols]).then_inc(loaded[s], 16)

                for s in range(2):
                    load(s, slice(s * P, (s + 1) * P))
                with sp.Fori(1, FT // 2) as i:
                    for s in range(2):
                        sp.wait_ge(product, 2 * i + s - 1)
                        load(s, bass.ds((2 * i + s) * P, P))

            @block.tensor
            def _(pe):
                def pair(i, first):
                    for s in range(2):
                        pe.wait_ge(loaded[s], 32 * (i + 1))
                        if not first:
                            pe.wait_ge(multiplied, ns * (2 * i + s - 1))
                        for n in range(2):
                            for k in range(CT):
                                for q, (at, width) in enumerate(segs):
                                    mm = pe.matmul(c.bank[4 * s + 2 * n + q][:, 0:width], w[s][:, n, k, :],
                                                   f[:, k, at:at + width], start=(k == 0), stop=(k == CT - 1))
                        mm.then_inc(product, 1)

                pair(0, True)
                with pe.Fori(1, FT // 2) as i:
                    pair(i, False)

            @block.scalar
            def _(act):
                def pair(i, first):
                    for s in range(2):
                        m = 2 * i + s
                        act.wait_ge(product, m + 1)
                        if not first:
                            act.wait_ge(multiplied, ns * (m - 1))
                        for q, (at, width) in enumerate(segs):
                            signal(act, nc.scalar.activation(silu[s][:, at:at + width], c.bank[4 * s + q][:, 0:width],
                                                             ACT.Silu), activated, ns * m + q + 1)

                pair(0, True)
                with act.Fori(1, FT // 2) as i:
                    pair(i, False)

            @block.vector
            def _(dve):
                with dve.Fori(0, FT // 2) as i:
                    for s in range(2):
                        m = 2 * i + s
                        for q, (at, width) in enumerate(segs):
                            dve.wait_ge(activated, ns * m + q + 1)
                            dve.wait_ge(product, m + 1)
                            signal(dve, nc.vector.tensor_tensor(
                                g[:, m, at:at + width], c.bank[4 * s + 2 + q][:, 0:width], silu[s][:, at:at + width],
                                ALU.mult), multiplied, ns * m + q + 1)


def reload(c, dst, src):
    nc = c.nc
    with ExitStack() as ctx:
        loaded = ctx.enter_context(nc.semaphore("residual_loaded"))
        with nc.Block() as block:
            @block.sync
            def _(sp):
                sp.dma_start(dst, src).then_inc(loaded, 16)
                sp.wait_ge(loaded, 16)


def qkv(c, d, f, q, k, v):
    nc = c.nc
    NH = KV_HEADS + HEADS
    KVD = KV_HEADS * P
    with ExitStack() as ctx:
        sb = lambda n, s: ctx.enter_context(nc.sbuf_tensor(n, s, F32))
        sem = lambda n: ctx.enter_context(nc.semaphore(n))
        w = [sb(f"qk_w{s}", [P, CT, P]) for s in range(2)]
        wv = sb("wv", [P, CT, KVD])
        cos, sin, swap = sb("cos", [P, LAT]), sb("sin", [P, LAT]), sb("swap", [P, P])
        raw, sq, std, turned = sb("qk_raw", [P, TOK]), sb("qk_sq", [P, TOK]), sb("qk_std", [P, TOK]), sb("qk_turned", [P, LAT])
        tables, v_loaded = sem("rope_loaded"), sem("wv_loaded")
        loaded = [sem(f"qk_w_loaded{s}") for s in range(2)]
        product, v_product, v_copied = sem("qk_product"), sem("v_product"), sem("v_copied")
        copied, squared, summed, rooted, normed, swapped, rotated, ctx_out, order = (sem(n) for n in (
            "qk_copied", "qk_squared", "qk_summed", "qk_rooted", "qk_normed", "qk_swapped", "qk_rotated", "qk_ctx_out",
            "qk_dve_order"))
        wk = d["at_wk"][0].rearrange("(k p) e -> p k e", p=P)
        wq = d["at_wq"][0].rearrange("(k p) e -> p k e", p=P)
        with nc.Block() as block:
            @block.sync
            def _(sp):
                sp.dma_start(wv[:], d["at_wv"][0].rearrange("(k p) e -> p k e", p=P)).then_inc(v_loaded, 16)
                for s in range(2):
                    sp.dma_start(w[s][:], wk[:, :, s * P:(s + 1) * P]).then_inc(loaded[s], 16)
                for t, s in ((cos, "k_cos"), (sin, "k_sin"), (swap, "k_swap")):
                    sp.dma_start(t[:], d[s]).then_inc(tables, 16)
                with sp.Fori(0, HEADS // 2) as i:
                    for s in range(2):
                        sp.wait_ge(product, 2 * i + s + 1)
                        sp.dma_start(w[s][:], wq[:, :, bass.ds((2 * i + s) * P, P)]).then_inc(loaded[s], 16)

            @block.tensor
            def _(pe):
                pe.wait_ge(v_loaded, 16)
                for t in range(TOK // P):
                    if t >= 2:
                        pe.wait_ge(v_copied, t - 1)
                    for kt in range(CT):
                        mm = pe.matmul(c.bank[6 + t % 2][:, 0:KVD], f[:, kt, t * P:(t + 1) * P], wv[:, kt, :],
                                       start=(kt == 0), stop=(kt == CT - 1))
                    mm.then_inc(v_product, 1)
                pe.wait_ge(tables, 48)
                with pe.Fori(0, NH // 2) as i:
                    for s in range(2):
                        n = 2 * i + s
                        pe.wait_ge(loaded[s], 16 * (i + 1))
                        pe.wait_ge(copied, 2 * n)
                        for kt in range(CT):
                            for b, (at, width) in enumerate(SEGS):
                                mm = pe.matmul(c.bank[b][:, 0:width], w[s][:, kt, :], f[:, kt, at:at + width],
                                               start=(kt == 0), stop=(kt == CT - 1))
                        mm.then_inc(product, 1)
                        pe.wait_ge(squared, n + 1)
                        pe.wait_ge(rooted, 2 * n)
                        for b, (at, width) in enumerate(SEGS):
                            mm = pe.matmul(c.bank[2 + b][:, 0:width], c.ones[:], sq[:, at:at + width],
                                           start=True, stop=True)
                        mm.then_inc(summed, 1)
                        pe.wait_ge(normed, n + 1)
                        pe.wait_ge(rotated, n)
                        pe.matmul(c.bank[4][:, 0:LAT], swap[:], raw[:, CTX:TOK], start=True, stop=True)\
                            .then_inc(swapped, 1)

            @block.scalar
            def _(act):
                for t in range(TOK // P):
                    act.wait_ge(v_product, t + 1)
                    signal(act, nc.scalar.copy(v[:, t, :], c.bank[6 + t % 2][:, 0:KVD]), v_copied, t + 1)
                with act.Fori(0, NH // 2) as i:
                    for s in range(2):
                        n = 2 * i + s
                        act.wait_ge(product, n + 1)
                        act.wait_ge(rotated, n)
                        for b, (at, width) in enumerate(SEGS):
                            signal(act, nc.scalar.copy(raw[:, at:at + width], c.bank[b][:, 0:width]), copied, 2 * n + b + 1)
                        signal(act, nc.scalar.activation(sq[:], raw[:], ACT.Square), squared, n + 1)
                        act.wait_ge(summed, n + 1)
                        for b, (at, width) in enumerate(SEGS):
                            signal(act, nc.scalar.activation(std[:, at:at + width], c.bank[2 + b][:, 0:width], ACT.Sqrt,
                                                             scale=1.0 / P, bias=c.eps[:, 0:1]), rooted, 2 * n + b + 1)

            @block.vector
            def _(dve):
                step = Order(dve, order)
                v_ = nc.vector

                def head(n, gain, out, at_n):
                    dve.wait_ge(rooted, 2 * (n + 1))
                    step(v_.reciprocal(std[:], std[:]))
                    signal(dve, v_.scalar_tensor_tensor(raw[:], raw[:], c.par[:, gain:gain + 1], std[:], ALU.mult, ALU.mult),
                           normed, n + 1)
                    step(v_.tensor_tensor(turned[:], raw[:, CTX:TOK], cos[:], ALU.mult))
                    dve.wait_ge(swapped, n + 1)
                    step(v_.tensor_tensor(out[:, at_n, CTX - lo(out):TOK - lo(out)], c.bank[4][:, 0:LAT], sin[:], ALU.mult))
                    if out is k:
                        step(v_.tensor_copy(out[:, at_n, 0:CTX], raw[:, 0:CTX]))
                    o = out[:, at_n, CTX - lo(out):TOK - lo(out)]
                    signal(dve, v_.tensor_tensor(o, o, turned[:], ALU.add), rotated, n + 1)

                lo = lambda out: 0 if out is k else CTX
                for n in range(KV_HEADS):
                    head(n, PGK, k, n)
                with dve.Fori(0, HEADS // 2) as i:
                    step.enter(i, 6)
                    for s in range(2):
                        head(KV_HEADS + 2 * i + s, PGQ, q, 2 * i + s)
                    step.leave(HEADS // 2)


def attend(c, q, k, v, o):
    nc = c.nc
    QT = LAT // P
    T = TOK // P
    SCALE = float(P) ** -0.5
    G = HEADS // KV_HEADS
    with ExitStack() as ctx:
        sb = lambda n, s: ctx.enter_context(nc.sbuf_tensor(n, s, F32))
        sem = lambda n: ctx.enter_context(nc.semaphore(n))
        qh = sb("qh", [P, LAT])
        prob = [sb(f"prob{s}", [P, TOK]) for s in range(2)]
        pt = sb("prob_t", [P, T, LAT])
        mx, nmx, den, rec = sb("mx", [P, 2, 2]), sb("nmx", [P, 2]), sb("den", [P, 2, 2]), sb("rec", [P, 2])
        q_placed, scored, maxed, expd, scaled, turned, copied_a, copied_b, out_ready, out_copied, order = (sem(n) for n in (
            "q_placed", "scored", "maxed", "exponentials", "prob_scaled", "prob_turned", "prob_copied_act",
            "prob_copied_dve", "out_ready", "out_copied", "att_order"))
        with nc.Block() as block:
            def heads(eng, body):
                for kv in range(KV_HEADS):
                    with eng.Fori(0, G) as i:
                        body(kv, G * kv + i, i)

            @block.tensor
            def _(pe):
                def body(kv, h, i):
                    pe.wait_ge(q_placed, h + 1)
                    def turn(t):
                        n = QT * h + t
                        pe.wait_ge(scaled, n + 1)
                        pe.wait_ge(copied_a, n)
                        pe.wait_ge(copied_b, n)
                        for s in range(T):
                            out = c.bank[4][:, s * P:(s + 1) * P] if s < 4 else c.bank[5][:, (s - 4) * P:(s - 3) * P]
                            mm = pe.transpose(out, prob[t % 2][:, s * P:(s + 1) * P], c.ident[:])
                        mm.then_inc(turned, 1)

                    for t in range(QT):
                        n = QT * h + t
                        s = 2 * (t % 2)
                        if t >= 2:
                            pe.wait_ge(expd, 2 * (n - 1))
                        else:
                            pe.wait_ge(expd, 2 * QT * h)
                        pe.matmul(c.bank[s][:, 0:CTX], qh[:, t * P:(t + 1) * P], k[:, kv, 0:CTX], start=True, stop=True)
                        pe.matmul(c.bank[s + 1][:, 0:LAT], qh[:, t * P:(t + 1) * P], k[:, kv, CTX:TOK],
                                  start=True, stop=True).then_inc(scored, 1)
                        if t:
                            turn(t - 1)
                    turn(QT - 1)
                    pe.wait_ge(copied_a, QT * (h + 1))
                    pe.wait_ge(copied_b, QT * (h + 1))
                    pe.wait_ge(out_copied, h)
                    for s in range(T):
                        mm = pe.matmul(c.bank[6][:, 0:LAT], v[:, s, kv * P:(kv + 1) * P], pt[:, s, :],
                                       start=(s == 0), stop=(s == T - 1))
                    mm.then_inc(out_ready, 1)

                heads(pe, body)

            @block.scalar
            def _(act):
                def body(kv, h, i):
                    def copy(t):
                        n = QT * h + t
                        act.wait_ge(turned, n + 1)
                        signal(act, nc.scalar.copy(pt[:, 4:T, t * P:(t + 1) * P],
                                                   c.bank[5][:, 0:256].rearrange("p (s t) -> p s t", t=P)), copied_a, n + 1)

                    for t in range(QT):
                        n = QT * h + t
                        act.wait_ge(maxed, n + 1)
                        act.wait_ge(turned, n - 1 if t >= 2 else QT * h)
                        for b, (at, width) in enumerate(SEGS):
                            signal(act, nc.scalar.activation(prob[t % 2][:, at:at + width], c.bank[2 * (t % 2) + b][:, 0:width],
                                                             ACT.Exp, scale=SCALE, bias=nmx[:, t % 2:t % 2 + 1],
                                                             accum_out=den[:, t % 2, b:b + 1]), expd, 2 * n + b + 1)
                        if t:
                            copy(t - 1)
                    copy(QT - 1)
                    act.wait_ge(out_ready, h + 1)
                    signal(act, nc.scalar.copy(o[:, h, :], c.bank[6][:, 0:LAT]), out_copied, h + 1)

                heads(act, body)

            @block.vector
            def _(dve):
                step = Order(dve, order)
                v_ = nc.vector

                def body(kv, h, i):
                    step.enter(i, 4 * QT)
                    dve.wait_ge(out_copied, h)
                    signal(dve, v_.tensor_copy(qh[:], q[:, h, :]), q_placed, h + 1)

                    def scale(t):
                        n = QT * h + t
                        dve.wait_ge(expd, 2 * (n + 1))
                        step(v_.tensor_tensor(rec[:, t % 2:t % 2 + 1], den[:, t % 2, 0:1], den[:, t % 2, 1:2], ALU.add))
                        step(v_.reciprocal(rec[:, t % 2:t % 2 + 1], rec[:, t % 2:t % 2 + 1]))
                        signal(dve, v_.tensor_scalar(prob[t % 2][:], prob[t % 2][:], rec[:, t % 2:t % 2 + 1], None, ALU.mult),
                               scaled, n + 1)

                    def copy(t):
                        n = QT * h + t
                        dve.wait_ge(turned, n + 1)
                        signal(dve, v_.tensor_copy(pt[:, 0:4, t * P:(t + 1) * P],
                                                   c.bank[4][:].rearrange("p (s t) -> p s t", t=P)), copied_b, n + 1)

                    for t in range(QT):
                        n = QT * h + t
                        dve.wait_ge(scored, n + 1)
                        for b, (at, width) in enumerate(SEGS):
                            ins = v_.tensor_reduce(mx[:, t % 2, b:b + 1], c.bank[2 * (t % 2) + b][:, 0:width], AX, ALU.max)
                            step(ins)
                        signal(dve, v_.tensor_scalar(nmx[:, t % 2:t % 2 + 1], mx[:, t % 2, 0:1], mx[:, t % 2, 1:2], -SCALE,
                                                     ALU.max, ALU.mult), maxed, n + 1)
                        if t:
                            scale(t - 1)
                        if t:
                            copy(t - 1)
                    scale(QT - 1)
                    copy(QT - 1)
                    step.leave(G)

                heads(dve, body)


def store(c, h, out):
    nc = c.nc
    T = LAT // P
    with ExitStack() as ctx:
        y = ctx.enter_context(nc.sbuf_tensor("y_rows", [P, T, D], F32))
        turned, copied, stored = (ctx.enter_context(nc.semaphore(n)) for n in ("out_turned", "out_turned_copied", "stored"))
        rows = out[0].rearrange("(t p) e -> t p e", p=P)
        with nc.Block() as block:
            @block.tensor
            def _(pe):
                for t in range(T):
                    for q in range(2):
                        n = 2 * t + q
                        if n >= 4:
                            pe.wait_ge(copied, n - 3)
                        for k in range(4):
                            mm = pe.transpose(c.bank[n % 4][:, k * P:(k + 1) * P],
                                              h[:, 4 * q + k, CTX + t * P:CTX + (t + 1) * P], c.ident[:])
                        mm.then_inc(turned, 1)

            @block.vector
            def _(dve):
                for n in range(2 * T):
                    dve.wait_ge(turned, n + 1)
                    nc.vector.tensor_copy(y[:, n // 2, 512 * (n % 2):512 * (n % 2) + 512], c.bank[n % 4][:])\
                        .then_inc(copied, 1)

            @block.sync
            def _(sp):
                for t in range(T):
                    sp.wait_ge(copied, 2 * t + 2)
                    sp.dma_start(rows[t], y[:, t, :]).then_inc(stored, 16)
                sp.wait_ge(stored, 16 * T)


def backbone(nc, d, out):
    with ExitStack() as ctx:
        c = Core(nc, ctx)
        c.bank = [ctx.enter_context(nc.psum_tensor(f"bank{n}", [P, 512], F32)) for n in range(8)]
        c.ident, c.ones_head, c.ones = c.sb("ident", [P, P]), c.sb("ones_head", [P, P]), c.sb("ones", [P, P])
        c.level_mask = c.sb("level_mask", [P, LEVELS, 2, P])
        c.score_mask = c.sb("score_mask", [P, 2, 4, CH])
        c.keep = c.sb("keep", [P, TOK])
        c.par, c.mod, c.gain = c.sb("par", [P, NPAR]), c.sb("mod", [P, 2, 48, 2]), c.sb("gain", [P, 2, 2, 2, CT])
        c.cond, c.eps = c.sb("cond", [P, 16]), c.sb("eps", [P, 2])
        spill = nc.dram_tensor("residual", [P, CT, TOK], F32, kind="Internal").ap()
        both, latent = SEGS, SEGS[1:]

        setup(c, d)
        modulation(c, d)
        mixer_out, h, f = (c.sb(n, [P, CT, TOK]) for n in ("r_or_mixer_out", "k_or_residual", "v_or_normed"))

        with nc.sbuf_tensor("hidden", [P, 3, TOK], F32) as hidden:
            with nc.sbuf_tensor("apad", [P, CT, TOK + 3], F32) as apad:
                load_tokens(c, d, h, spill)
                zero_padding(c, apad)
                norm(c, "norm0", h, 0, 0,
                     lambda k, at, n: apad[:, k, (1 if at == 0 else at + 2):(1 if at == 0 else at + 2) + n], both)
                rwkv_inputs(c, d, apad, (mixer_out, h, f), hidden)
            recurrence(c, d, (mixer_out, h, f), hidden)
        reload(c, h[:], spill)
        dense(c, "rwkv_out", d["rw_wo"][0], CT, CT, lambda k, at, n: mixer_out[:, k, at:at + n], both, h, 0, 16)
        feed_forward(c, d, h, f, 0, both)

        norm(c, "norm1", h, 1, 0, lambda k, at, n: f[:, k, at:at + n], both)
        with nc.sbuf_tensor("q_heads", [P, HEADS, LAT], F32) as q, nc.sbuf_tensor("k_heads", [P, KV_HEADS, TOK], F32) as k, \
                nc.sbuf_tensor("v_rows", [P, TOK // P, KV_HEADS * P], F32) as v:
            qkv(c, d, f, q, k, v)
            attend(c, q, k, v, mixer_out[:, :, CTX:TOK])
        dense(c, "att_out", d["at_wo"][0], CT, CT, lambda k, at, n: mixer_out[:, k, at:at + n], latent, h, 1, 16)
        feed_forward(c, d, h, f, 1, latent)
        store(c, h, out)


def feed_forward(c, d, h, f, layer, segs):
    norm(c, f"norm_ffn{layer}", h, layer, 1, lambda k, at, n: f[:, k, at:at + n], segs)
    with c.nc.sbuf_tensor(f"g{layer}", [P, FT, TOK], F32) as g:
        swiglu_up(c, f"up{layer}", d["ff_w1"][layer], d["ff_w3"][layer], f, segs, g)
        dense(c, f"down{layer}", d["ff_w2"][layer], FT, CT, lambda k, at, n: g[:, k, at:at + n], segs, h, layer, 40)


_INS = ["x", "c", "ctx", "c_ctx", "mod_w", "mod_b", "norm_mix", "norm_ffn", "ff_w1", "ff_w3", "ff_w2", "rw_mu", "rw_wr",
        "rw_wk", "rw_wv", "rw_wo", "rw_w0", "rw_w1", "rw_w2", "rw_a0", "rw_a1", "rw_a2", "rw_g1", "rw_g2", "rw_kk",
        "rw_ka", "rw_rk", "rw_lnx_g", "rw_lnx_b", "at_wq", "at_wk", "at_wv", "at_wo", "at_gq", "at_gk"]


def shape_tables():
    f = np.float32
    i, j = np.indices((P, P))
    level = np.zeros((P, LEVELS, 2, P), f)
    for n in range(LEVELS):
        same = (i >> (n + 1)) == (j >> (n + 1))
        first_i, first_j = (i >> n) & 1 == 0, (j >> n) & 1 == 0
        level[:, n, 0, :] = same & first_i & ~first_j
        level[:, n, 1, :] = same & ~first_i & first_j
    s, t = np.arange(P)[:, None] % CH, np.arange(CH)[None, :]
    score = np.stack([np.stack([m1, m2, m1, m2], 1) for m1, m2 in ((s < t, s <= t), (s > t, s >= t))], 1).astype(f)
    keep = np.broadcast_to(np.arange(TOK) % CH != 0, (P, TOK)).astype(f)
    tok = np.arange(LAT)
    inv = f(10000.0) ** (-np.arange(0, P // 2, 2, dtype=f) / f(P // 2))
    ang = np.concatenate([(tok // 64).astype(f)[:, None] * inv, (tok % 64).astype(f)[:, None] * inv], 1)
    pair = np.arange(P) // 2
    sign = np.where(np.arange(P) % 2 == 0, -1.0, 1.0)[:, None]
    return {
        "k_ident": np.eye(P, dtype=f),
        "k_ones_head": (i // CH == j // CH).astype(f),
        "k_level_mask": level,
        "k_score_mask": score,
        "k_keep": keep,
        "k_cos": np.cos(ang).T[pair].astype(f),
        "k_sin": (np.sin(ang).T[pair] * sign).astype(f),
        "k_swap": (i == (j ^ 1)).astype(f),
    }


def kernel(**inputs):
    import concourse.bacc as _bacc
    from concourse.bass_utils import run_bass_kernel_spmd as _run

    nc = _bacc.Bacc("TRN2", target_bir_lowering=False, num_devices=1)
    arrays, args = {}, {}
    for name, a in [(n, inputs[n]) for n in _INS] + list(shape_tables().items()):
        a = np.ascontiguousarray(a)
        arrays[f"in_{name}"] = a
        args[name] = nc.dram_tensor(f"in_{name}", a.shape, mybir.dt.from_np(a.dtype), kind="ExternalInput").ap()
    out = nc.dram_tensor("out", (1, LAT, D), F32, kind="ExternalOutput").ap()
    backbone(nc, args, out)
    r = _run(nc, [arrays], core_ids=[0])
    return r.results[0]["out"]
```

```python
from contextlib import ExitStack

import numpy as np

import concourse.bass as bass
from concourse import mybir

F32 = mybir.dt.float32
ALU = mybir.AluOpType
ACT = mybir.ActivationFunctionType
AX = mybir.AxisListType.X

P = 128
D = 1024
CT = D // P
CTX, LAT = 256, 512
TOK = CTX + LAT
SEGS = ((0, CTX), (CTX, LAT))
FF = 2816
FT = FF // P
CH = 64
NCH = TOK // CH
NB = NCH // 2
LEVELS = 6
DECAY = float(np.exp(-0.5))
HEADS, KV_HEADS = 8, 2

PMODB, PC, PGQ, PGK = 0, 96, 112, 113
PMU = 114
PW0, PA0 = PMU + 48, PMU + 64
PKK, PKA, PRK, PLG, PLB = (PMU + 80 + 8 * n for n in range(5))
PLESS = PMU + 120
PNM = PLESS + CT
PNF = PNM + 16
NPAR = PNF + 16


class Order:

    def __init__(self, eng, sem):
        self.eng, self.sem, self.off, self.n, self.outer = eng, sem, 0, 0, []

    def __call__(self, ins):
        ins.then_inc(self.sem, 1)
        self.n += 1
        self.eng.wait_ge(self.sem, self.off + self.n)

    def enter(self, at, per):
        self.outer.append((self.off, self.n, per))
        self.off, self.n = self.off + self.n + at * per, 0

    def leave(self, trips):
        self.off, n, per = self.outer.pop()
        assert self.n == per, f"{self.n} steps, {per} expected"
        self.n = n + trips * per


def signal(eng, ins, sem, value):
    ins.then_inc(sem, 1)
    eng.wait_ge(sem, value)


def need(eng, sem, n):
    if not isinstance(n, int) or n > 0:
        eng.wait_ge(sem, n)


def by_two(eng, start, stop, pair):
    if start == 0:
        pair(0)
        start = 1
    with eng.Fori(start, stop) as i:
        pair(i)


class Core:

    def __init__(self, nc, ctx):
        self.nc, self.ctx, self.count = nc, ctx, 0

    def sb(self, name, shape):
        return self.ctx.enter_context(self.nc.sbuf_tensor(name, shape, F32))

    def sem(self, name):
        return self.ctx.enter_context(self.nc.semaphore(name))


def tokens(bank_ctx, bank_lat):
    return ((bank_ctx[:, 0:CTX], 0, CTX), (bank_lat[:, 0:LAT], CTX, LAT))


def setup(c, d):
    nc = c.nc
    with ExitStack() as ctx:
        rows = [ctx.enter_context(nc.sbuf_tensor(f"par_rows{n}", [P, P], F32)) for n in range(3)]
        loaded = ctx.enter_context(nc.semaphore("setup_loaded"))
        turned = ctx.enter_context(nc.semaphore("par_turned"))
        copied = ctx.enter_context(nc.semaphore("par_copied"))
        gated = ctx.enter_context(nc.semaphore("cond_silu"))
        row_of = lambda a: a.rearrange("(m p) -> m p", p=P)
        lists = [
            [d["mod_b"].rearrange("l (m p) -> (l m) p", p=P), d["c"].rearrange("b (m p) -> (b m) p", p=P),
             row_of(d["c_ctx"]), d["at_gq"], d["at_gk"]],
            [d["rw_mu"].rearrange("a n (m p) -> (a n m) p", p=P)]
            + [d[n].rearrange("a e (m p) -> (a e m) p", p=P) for n in ("rw_w0", "rw_a0")]
            + [d[n].rearrange("a (m p) -> (a m) p", p=P) for n in ("rw_kk", "rw_ka")]
            + [d["rw_rk"].rearrange("a (m h) k -> (a m) (h k)", h=2)]
            + [d[n].rearrange("a (m p) -> (a m) p", p=P) for n in ("rw_lnx_g", "rw_lnx_b")],
            [d[n].rearrange("a (m p) -> (a m) p", p=P) for n in ("norm_mix", "norm_ffn")],
        ]
        sizes = [114, 120, 32]
        n_loads = 5 + sum(len(x) for x in lists)
        with nc.Block() as block:
            @block.sync
            def _(sp):
                for t, s in ((c.ident, "k_ident"), (c.ones_head, "k_ones_head"), (c.level_mask, "k_level_mask"),
                             (c.score_mask, "k_score_mask"), (c.keep, "k_keep")):
                    sp.dma_start(t[:], d[s]).then_inc(loaded, 16)
                for tile, parts in zip(rows, lists):
                    at = 0
                    for part in parts:
                        n = part.shape[0]
                        sp.dma_start(tile[at:at + n, :], part).then_inc(loaded, 16)
                        at += n

            @block.tensor
            def _(pe):
                pe.wait_ge(loaded, 16 * n_loads)
                for n, m in enumerate(sizes):
                    pe.transpose(c.bank[n][:, 0:m], rows[n][0:m, :], c.ident[0:m, 0:m]).then_inc(turned, 1)

            @block.vector
            def _(dve):
                at = 0
                nc.vector.memset(c.ones[:], 1.0).then_inc(copied, 1)
                nc.vector.memset(c.eps[:, 0:1], 1e-6).then_inc(copied, 1)
                nc.vector.memset(c.eps[:, 1:2], 64e-5).then_inc(copied, 1)
                dve.wait_ge(turned, 3)
                for n, m in enumerate(sizes):
                    at += CT if n == 2 else 0
                    nc.vector.tensor_copy(c.par[:, at:at + m], c.bank[n][:, 0:m]).then_inc(copied, 1)
                    at += m
                dve.wait_ge(copied, 6)
                nc.vector.tensor_scalar(c.par[:, PLESS:PLESS + CT], c.par[:, PKA:PKA + CT], -1.0, 1.0, ALU.mult, ALU.add)\
                    .then_inc(copied, 1)

            @block.scalar
            def _(act):
                act.wait_ge(copied, 6)
                nc.scalar.activation(c.cond[:], c.par[:, PC:PC + 16], ACT.Silu).then_inc(gated, 1)


def modulation(c, d):
    nc = c.nc
    W = 512
    steps = 6 * D // W
    with ExitStack() as ctx:
        w = [ctx.enter_context(nc.sbuf_tensor(f"modw{s}", [P, CT, W], F32)) for s in range(2)]
        row = [ctx.enter_context(nc.sbuf_tensor(f"modrow{s}", [2, W], F32)) for s in range(2)]
        loaded = [ctx.enter_context(nc.semaphore(f"modw_loaded{s}")) for s in range(2)]
        product = ctx.enter_context(nc.semaphore("mod_product"))
        copied = ctx.enter_context(nc.semaphore("mod_row_copied"))
        turned = ctx.enter_context(nc.semaphore("mod_turned"))
        stored = ctx.enter_context(nc.semaphore("mod_stored"))
        gains = ctx.enter_context(nc.semaphore("norm_gains"))
        src = d["mod_w"].rearrange("l (k p) e -> l p k e", p=P)
        cond = c.cond[:].rearrange("p (r k) -> p r k", k=CT)
        with nc.Block() as block:
            @block.sync
            def _(sp):
                for s in range(2):
                    sp.dma_start(w[s][:], src[0][:, :, s * W:(s + 1) * W]).then_inc(loaded[s], 16)
                for l in range(2):
                    with sp.Fori(1 - l, steps // 2) as i:
                        for s in range(2):
                            sp.wait_ge(product, steps * l + 2 * i + s - 1)
                            sp.dma_start(w[s][:], src[l][:, :, bass.ds((2 * i + s) * W, W)]).then_inc(loaded[s], 16)

            @block.tensor
            def _(pe):
                def pair(i):
                    for s in range(2):
                        n = 2 * i + s
                        pe.wait_ge(loaded[s], 16 * (i + 1))
                        need(pe, copied, n)
                        for k in range(CT):
                            mm = pe.matmul(c.bank[s][0:2, :], cond[:, :, k], w[s][:, k, :],
                                           start=(k == 0), stop=(k == CT - 1))
                        mm.then_inc(product, 1)
                        pe.wait_ge(copied, n + 1)
                        need(pe, stored, n)
                        for q in range(4):
                            mm = pe.matmul(c.bank[2][:, 2 * q:2 * q + 2], row[s][:, q * P:(q + 1) * P],
                                           c.ident[0:2, 0:2], start=True, stop=True)
                        mm.then_inc(turned, 1)

                by_two(pe, 0, steps, pair)

            @block.scalar
            def _(act):
                def pair(i):
                    for s in range(2):
                        n = 2 * i + s
                        act.wait_ge(product, n + 1)
                        need(act, turned, n)
                        signal(act, nc.scalar.copy(row[s][:], c.bank[s][0:2, :]), copied, n + 1)

                by_two(act, 0, steps, pair)

            @block.vector
            def _(dve):
                for l in range(2):
                    with dve.Fori(0, steps // 2) as i:
                        for s in range(2):
                            n = steps * l + 2 * i + s
                            dve.wait_ge(turned, n + 1)
                            at = bass.ds((2 * i + s) * 4, 4)
                            signal(dve, nc.vector.tensor_tensor(
                                c.mod[:, l, at, :], c.bank[2][:, 0:8].rearrange("p (q r) -> p q r", r=2),
                                c.par[:, bass.ds(PMODB + 48 * l + (2 * i + s) * 4, 4)].unsqueeze(2).to_broadcast([P, 4, 2]),
                                ALU.add), stored, n + 1)
                n = 0
                for l in range(2):
                    for kind, base in ((0, PNM), (1, PNF)):
                        for r in range(2):
                            nc.vector.scalar_tensor_tensor(
                                c.gain[:, l, kind, r, :], c.mod[:, l, 24 * kind + 8:24 * kind + 16, r], 1.0,
                                c.par[:, base + 8 * l:base + 8 * l + 8], ALU.add, ALU.mult).then_inc(gains, 1)


def load_tokens(c, d, h, spilled):
    nc = c.nc
    T = TOK // P
    with ExitStack() as ctx:
        xt = ctx.enter_context(nc.sbuf_tensor("xt", [P, T, D], F32))
        loaded = ctx.enter_context(nc.semaphore("x_loaded"))
        turned = ctx.enter_context(nc.semaphore("x_turned"))
        lat_copied = ctx.enter_context(nc.semaphore("x_lat_copied"))
        ctx_copied = ctx.enter_context(nc.semaphore("x_ctx_copied"))
        spill_done = ctx.enter_context(nc.semaphore("x_spilled"))
        with nc.Block() as block:
            @block.sync
            def _(sp):
                sp.dma_start(xt[:, 0:2, :], d["ctx"][0].rearrange("(t p) e -> p t e", p=P)).then_inc(loaded, 16)
                sp.dma_start(xt[:, 2:T, :], d["x"][0].rearrange("(t p) e -> p t e", p=P)).then_inc(loaded, 16)
                sp.wait_ge(lat_copied, CT)
                sp.wait_ge(ctx_copied, CT)
                sp.dma_start(spilled, h[:]).then_inc(spill_done, 16)
                sp.wait_ge(spill_done, 16)

            @block.tensor
            def _(pe):
                pe.wait_ge(loaded, 32)
                for k in range(CT):
                    s = 2 * (k % 2)
                    if k >= 2:
                        pe.wait_ge(lat_copied, k - 1)
                        pe.wait_ge(ctx_copied, k - 1)
                    for t in range(T):
                        out = c.bank[s][:, t * P:(t + 1) * P] if t < 2 else c.bank[s + 1][:, (t - 2) * P:(t - 1) * P]
                        mm = pe.transpose(out, xt[:, t, k * P:(k + 1) * P], c.ident[:])
                    mm.then_inc(turned, 1)

            @block.vector
            def _(dve):
                for k in range(CT):
                    dve.wait_ge(turned, k + 1)
                    nc.vector.tensor_copy(h[:, k, CTX:TOK], c.bank[2 * (k % 2) + 1][:, 0:LAT]).then_inc(lat_copied, 1)

            @block.scalar
            def _(act):
                for k in range(CT):
                    act.wait_ge(turned, k + 1)
                    nc.scalar.copy(h[:, k, 0:CTX], c.bank[2 * (k % 2)][:, 0:CTX]).then_inc(ctx_copied, 1)


def norm(c, name, h, layer, kind, out, segs):
    nc = c.nc
    with ExitStack() as ctx:
        sb = lambda n, s: ctx.enter_context(nc.sbuf_tensor(f"{name}_{n}", s, F32))
        sem = lambda n: ctx.enter_context(nc.semaphore(f"{name}_{n}"))
        sq = sb("sq", [P, 2, TOK])
        std = sb("std", [P, TOK])
        scaled = sb("scaled", [P, 2, TOK])
        squared, summed, rooted, inverted, normed, written = (
            sem(n) for n in ("squared", "summed", "rooted", "inverted", "normed", "written"))
        lo = segs[0][0]
        banks = {CTX: c.bank[0], 0: c.bank[1]}
        with nc.Block() as block:
            @block.tensor
            def _(pe):
                for k in range(CT):
                    pe.wait_ge(squared, k + 1)
                    for at, n in segs:
                        mm = pe.matmul(banks[at][:, 0:n], c.ones[:], sq[:, k % 2, at:at + n],
                                       start=(k == 0), stop=(k == CT - 1))
                    mm.then_inc(summed, 1)

            @block.scalar
            def _(act):
                for k in range(CT):
                    if k >= 2:
                        act.wait_ge(summed, k - 1)
                    nc.scalar.activation(sq[:, k % 2, lo:], h[:, k, lo:], ACT.Square).then_inc(squared, 1)
                    act.wait_ge(squared, k + 1)
                act.wait_ge(summed, CT)
                for at, n in segs:
                    nc.scalar.activation(std[:, at:at + n], banks[at][:, 0:n], ACT.Sqrt, scale=1.0 / D,
                                         bias=c.eps[:, 0:1]).then_inc(rooted, 1)
                for k in range(CT):
                    act.wait_ge(normed, k + 1)
                    for s, (at, n) in enumerate(segs):
                        r = 1 if at == 0 else 0
                        nc.scalar.activation(out(k, at, n), scaled[:, k % 2, at:at + n], ACT.Identity,
                                             scale=c.gain[:, layer, kind, r, k:k + 1],
                                             bias=c.mod[:, layer, 24 * kind + k, r:r + 1]).then_inc(written, 1)

            @block.vector
            def _(dve):
                dve.wait_ge(rooted, len(segs))
                signal(dve, nc.vector.reciprocal(std[:, lo:], std[:, lo:]), inverted, 1)
                for k in range(CT):
                    if k >= 2:
                        dve.wait_ge(written, len(segs) * (k - 1))
                    signal(dve, nc.vector.tensor_tensor(scaled[:, k % 2, lo:], h[:, k, lo:], std[:, lo:], ALU.mult),
                           normed, k + 1)


WID = TOK + 1
GSEG = ((0, 0, CTX), (CTX + 1, CTX, LAT))


def rwkv_inputs(c, d, apad, rkv, hidden, dram):
    nc = c.nc
    with ExitStack() as ctx:
        sb = lambda n, s: ctx.enter_context(nc.sbuf_tensor(n, s, F32))
        sem = lambda n: ctx.enter_context(nc.semaphore(n))
        xx = sb("xx", [P, CT, WID])
        mix = [sb(f"mix{s}", [P, CT, WID]) for s in range(2)]
        w = [sb(f"proj_w{s}", [P, CT, P]) for s in range(2)]
        shifted, mixed, used = sem("shifted"), sem("mixed"), sem("mix_used")
        loaded = [sem(f"proj_w_loaded{s}") for s in range(2)]
        product, evac_lat, evac_ctx = sem("proj_product"), sem("proj_lat_copied"), sem("proj_ctx_copied")
        order, kept = sem("rwkv_in_order"), sem("rkv_stored")
        small = (d["rw_w1"][0].rearrange("e (k p) r -> p k e r", p=P),
                 d["rw_a1"][0].rearrange("e (k p) r -> p k e r", p=P),
                 d["rw_g1"][0].rearrange("(k p) r -> p k r", p=P))
        large = [d[n][0].rearrange("(k p) e -> p k e", p=P) for n in ("rw_wr", "rw_wk", "rw_wv")]
        MIXES = (1, 4, 5, 0, 2, 3)
        with nc.Block() as block:
            @block.sync
            def _(sp):
                for n in range(3):
                    if n >= 2:
                        sp.wait_ge(product, n - 1)
                    if n < 2:
                        for e in range(2):
                            sp.dma_start(w[n % 2][:, :, 64 * e:64 * e + 64], small[n][:, :, e, :])\
                                .then_inc(loaded[n % 2], 16)
                    else:
                        sp.dma_start(w[0][:], small[2]).then_inc(loaded[0], 16)
                for m in range(3):
                    with sp.Fori(0, CT // 2) as i:
                        for s in range(2):
                            n = 3 + CT * m + 2 * i + s
                            sp.wait_ge(product, n - 1)
                            sp.dma_start(w[1 - s][:], large[m][:, :, bass.ds((2 * i + s) * P, P)])\
                                .then_inc(loaded[1 - s], 16)

            def evac_bank(n_mod):
                return c.bank[2 * n_mod], c.bank[2 * n_mod + 1]

            @block.tensor
            def _(pe):
                def tile(n, slot, x, loads):
                    pe.wait_ge(loaded[slot], 16 * loads)
                    bctx, blat = evac_bank(slot)
                    for k in range(CT):
                        for (g, at, width), bank in zip(GSEG, (bctx, blat)):
                            mm = pe.matmul(bank[:, 0:width], w[slot][:, k, :], x[:, k, g:g + width],
                                           start=(k == 0), stop=(k == CT - 1))
                    return mm

                for n in range(3):
                    if n == 2:
                        pe.wait_ge(evac_lat, 1)
                        pe.wait_ge(evac_ctx, 1)
                    pe.wait_ge(mixed, CT * (n + 1))
                    tile(n, n % 2, mix[n % 2], (2, 2, 3)[n]).then_inc(product, 1)
                for m in range(3):
                    pe.wait_ge(mixed, CT * (4 + m))
                    with pe.Fori(0, CT // 2) as i:
                        for s in range(2):
                            n = 3 + CT * m + 2 * i + s
                            pe.wait_ge(evac_lat, n - 1)
                            pe.wait_ge(evac_ctx, n - 1)
                            base = 2 if s == 0 else 3
                            tile(n, 1 - s, mix[(3 + m) % 2], CT // 2 * m + i + 1 + base).then_inc(product, 1)

            @block.vector
            def _(dve):
                step = Order(dve, order)
                with dve.Fori(0, CT) as k:
                    step.enter(k, 1)
                    step(nc.vector.tensor_tensor(xx[:, k, :], apad[:, k, 0:WID], apad[:, k, 2:WID + 2], ALU.add))
                    signal(dve, nc.vector.scalar_tensor_tensor(xx[:, k, :], xx[:, k, :], 0.5, apad[:, k, 1:WID + 1],
                                                               ALU.mult, ALU.subtract), shifted, k + 1)
                    step.leave(CT)

                def mixes(q):
                    if q >= 2:
                        dve.wait_ge(product, (1, 2, 3, 3 + CT)[q - 2])
                    with dve.Fori(0, CT) as k:
                        signal(dve, nc.vector.scalar_tensor_tensor(
                            mix[q % 2][:, k, :], xx[:, k, :], c.par[:, bass.ds(PMU + 8 * MIXES[q] + k, 1)],
                            apad[:, k, 1:WID + 1], ALU.mult, ALU.add), mixed, CT * q + k + 1)

                def copies(m):
                    with dve.Fori(0, CT // 2) as i:
                        for s in range(2):
                            n = 3 + CT * m + 2 * i + s
                            dve.wait_ge(product, n + 1)
                            signal(dve, nc.vector.tensor_copy(rkv[m][:, 2 * i + s, CTX:TOK],
                                                              evac_bank(1 - s)[1][:, 0:LAT]), evac_lat, n + 1)

                mixes(0), mixes(1), mixes(2), mixes(3), mixes(4)
                for m in range(3):
                    copies(m)
                    if m == 0:
                        mixes(5)

            @block.scalar
            def _(act):
                for n, f in enumerate((ACT.Tanh, ACT.Copy, ACT.Sigmoid)):
                    act.wait_ge(product, n + 1)
                    bctx, blat = evac_bank(n % 2)
                    nc.scalar.activation(hidden[:, n, CTX:TOK], blat[:, 0:LAT], f).then_inc(evac_lat, 1)
                    signal(act, nc.scalar.activation(hidden[:, n, 0:CTX], bctx[:, 0:CTX], f), evac_ctx, n + 1)
                for m in range(3):
                    with act.Fori(0, CT // 2) as i:
                        for s in range(2):
                            n = 3 + CT * m + 2 * i + s
                            act.wait_ge(product, n + 1)
                            signal(act, nc.scalar.copy(rkv[m][:, 2 * i + s, 0:CTX], evac_bank(1 - s)[0][:, 0:CTX]),
                                   evac_ctx, n + 1)

            @block.gpsimd
            def _(pool):
                for m in range(3):
                    pool.wait_ge(evac_lat, 3 + CT * (m + 1))
                    pool.wait_ge(evac_ctx, 3 + CT * (m + 1))
                    pool.dma_start(dram[m], rkv[m][:]).then_inc(kept, 16)
                pool.wait_ge(kept, 48)


def half(h):
    return slice(CH * h, CH * h + CH)


NF, NR = 36, 13


def recurrence(c, d, dram, hidden, big):
    nc = c.nc
    with ExitStack() as ctx:
        sb = lambda n, s: ctx.enter_context(nc.sbuf_tensor(n, s, F32))
        sem = lambda n: ctx.enter_context(nc.semaphore(n))
        b_in = [[big[0][:, 2 * s + e, :] for e in range(2)] for s in range(2)]
        k_in = [[big[0][:, 4 + 2 * s + e, :] for e in range(2)] for s in range(2)]
        ar = [[big[1][:, 4 * s + 2 * e:4 * s + 2 * e + 2, :].rearrange("p a t -> p (a t)")
               for e in range(2)] for s in range(2)]
        y = [[big[2][:, 2 * s + e, :] for e in range(2)] for s in range(2)]
        gate = [big[2][:, 4 + s, :] for s in range(2)]
        bonus = [big[2][:, 6 + s, :] for s in range(2)]
        ar4 = [[t.rearrange("p (n k t) -> p n k t", k=2, t=CH) for t in a] for a in ar]
        ep = [[sb(f"ep{s}{e}", [P, NCH, CH + 1]) for e in range(2)] for s in range(2)]
        v_s = [sb(f"v_pair{s}", [P, TOK]) for s in range(2)]
        r_s, k_s = sb("r_pair", [P, TOK]), sb("k_pair", [P, TOK])
        cols = [sb(f"pair_params{s}", [P, 10]) for s in range(2)]
        W0, A0, KK, KA, RK, LG, LB, LESS = 0, 2, 4, 5, 6, 7, 8, 9
        lora_w = sb("lora_w", [P, 3, P])
        kk, tmp, ytmp, gated = sb("kk", [P, TOK]), sb("tmp", [P, TOK]), sb("ytmp", [P, TOK]), sb("gated", [P, TOK])
        sig_w = [sb(f"sig_w{e}", [P, TOK]) for e in range(2)]
        cum = [sb(f"cum{e}", [P, TOK]) for e in range(2)]
        bk = sb("bk", [P, 2, 4, P])
        vbd = sb("vbd", [P, 4, P])
        arbd = [sb(f"arbd{p}", [P, 4, 2, P]) for p in range(2)]
        sc = [sb(f"sc{p}", [P, 4, 4, P]) for p in range(2)]
        tok = [sb(f"tok{p}", [P, 3, 4, P]) for p in range(2)]
        inv_x = [sb(f"inverse{p}", [P, 2, 2, 2, P]) for p in range(2)]
        t_sb = sb("t_sb", [P, 2, 2, P])
        lvl = [sb(f"lvl{n}", [P, 2, 2, P]) for n in range(2)]
        rhs, u_sb, decayed = sb("rhs", [P, 2, P]), sb("u_sb", [P, 2, P]), sb("decayed", [P, 2, P])
        state = [sb(f"state{q}", [P, 2, P]) for q in range(2)]

        zeroed, slices, features, pair_done, stored = (sem(n) for n in (
            "zeroed", "slices_loaded", "features_done", "pair_done", "pair_stored"))
        f_ready, f_read = sem("side_bank_ready"), sem("side_bank_read")
        kk_raw, kk_sq, cumd, decays, kk_root, bonus_in = (sem(n) for n in (
            "kk_raw", "kk_squared", "decay_sums", "decays", "kk_root", "bonus_in"))
        y_in, centred, y_sq = sem("y_summed_directions"), sem("y_centred"), sem("y_squared")
        dve_order = sem("dve_order")
        bd_dve, bd_act, scores, masked = sem("bk_placed"), sem("ar_v_placed"), sem("scores"), sem("scores_masked")
        turned, tok_copied = sem("bkv_turned"), sem("bkv_copied")
        lvl_ready, t_ready, t_copied, x_ready, x_added = (sem(n) for n in (
            "level_masked", "t_product", "t_copied", "x_products", "x_added"))
        rhs_ready, rhs_copied, u_ready, u_copied = (sem(n) for n in ("rhs_ready", "rhs_copied", "u_ready", "u_copied"))
        s_decayed, s_ready, s_done = sem("state_decayed"), sem("state_products"), sem("state_done")
        y_ready, y_copied = sem("y_ready"), sem("y_copied")
        T_BANK, X_BANK = c.bank[0:2], c.bank[2:4]
        SC_BANK = (c.bank[4], T_BANK[0])
        TURN_BANK = (T_BANK[1], X_BANK[0], X_BANK[1])
        CHAIN, Y_BANK, SIDE = c.bank[5:8]
        pair4 = lambda t: t.rearrange("p (s t) -> p s t", t=P)

        def blocks(j):
            return j, (NB + 1 - j) % NB

        def chunks(tile):
            return tile.rearrange("p (n t) -> p n t", t=CH)

        def units(q):
            return ((0, q, q), (1, 2 + 1 - q, 1 - q))

        def chunk_end(s, e, n):
            at = CH if e == 0 else 0
            return ep[s][e][:, n, at:at + 1]

        class Pair:

            def __init__(self, at, s):
                self.at, self.s = at, s

            def plus(self, n):
                return Pair(self.at + n, (self.s + n) % 2)

        class Batch:

            def __init__(self, t, j):
                self.t, self.j, self.g, self.p = t, j, t.at * NB + j, j % 2

        def side_uses(t, readout):
            if readout:
                return 18 * (CT - 1) + 14 if isinstance(t.at, int) and t.at == CT - 1 else 18 * t.at + 28
            return 0 if isinstance(t.at, int) and t.at == 0 else 18 * t.at - 4

        def schedule(E):
            def slot(C, I, N, extra):
                if I:
                    E.score(I, 0), E.score(I, 1), E.turn(I, 0), E.turn(I, 1)
                E.rhs(C, 0), extra()
                if I:
                    E.turn(I, 2)
                E.u(C, 0), extra()
                if I:
                    E.level0(I)
                extra(), E.sy(C, 0), extra()
                if I:
                    E.level(I, 1)
                extra(), E.rhs(C, 1)
                if I:
                    E.level(I, 2)
                extra(), E.u(C, 1)
                if I:
                    E.level(I, 3)
                extra(), E.sy(C, 1), extra()
                if I:
                    E.level(I, 4)
                extra()
                if N:
                    E.place_bk(N)
                if I:
                    E.level(I, 5)
                extra()
                E.y_out(C)
                if N:
                    E.place_arv(N)

            def body(t, first, last):
                if not first:
                    slot(Batch(t.plus(-1), NB - 1), Batch(t, 0), Batch(t, 1), lambda: None)
                count = [0]

                def extra():
                    n = count[0]
                    count[0] += 1
                    if first:
                        if n < NF:
                            E.feature(t.plus(1), n)
                    elif n < NR:
                        E.readout(t.plus(-1), n)
                    elif not last and n < NR + NF:
                        E.feature(t.plus(1), n - NR)

                for j in range(NB - 1):
                    after = Batch(t, j + 2) if j + 2 < NB else None if last else Batch(t.plus(1), 0)
                    slot(Batch(t, j), Batch(t, j + 1), after, extra)
                assert count[0] >= NR + NF

            for n in range(NF):
                E.feature(Pair(0, 0), n)
            I = Batch(Pair(0, 0), 0)
            E.place_bk(I), E.place_arv(I), E.score(I, 0), E.score(I, 1), E.turn(I, 0), E.turn(I, 1), E.turn(I, 2), E.level0(I)
            for n in range(1, LEVELS):
                E.level(I, n)
            E.place_bk(Batch(Pair(0, 0), 1)), E.place_arv(Batch(Pair(0, 0), 1))
            body(Pair(0, 0), True, False)
            with E.eng.Fori(0, CT // 2 - 1) as i:
                if E.order:
                    E.order.enter(i, E.per)
                body(Pair(2 * i + 1, 1), False, False)
                body(Pair(2 * i + 2, 0), False, False)
                if E.order:
                    E.order.leave(CT // 2 - 1)
            last = Pair(CT - 1, 1)
            body(last, False, True)
            slot(Batch(last, NB - 1), None, None, lambda: None)
            for n in range(NR):
                E.readout(last, n)

        class Part:
            order, per = None, 0

            def nothing(self, *_):
                pass

            place_bk = place_arv = score = turn = level0 = level = rhs = u = sy = y_out = feature = readout = nothing

        def map_piece(n):
            return (n - 1) // 2, SEGS[(n - 1) % 2]

        with nc.Block() as block:
            @block.sync
            def _(sp):
                def load(t, first):
                    at = t.at if isinstance(t.at, int) else None
                    one = bass.ds(t.at, 1) if at is None else slice(at, at + 1)
                    wide = bass.ds(t.at * P, P) if at is None else slice(at * P, at * P + P)
                    need(sp, bd_act, NB * t.at - NB)
                    if not first:
                        sp.wait_ge(features, t.at)
                    for dst, src in ((r_s, dram[0]), (k_s, dram[1]), (v_s[t.s], dram[2])):
                        sp.dma_start(dst[:], src[:, one, :].rearrange("p o t -> p (o t)")).then_inc(slices, 16)
                    sp.dma_start(lora_w[:, 0, :], d["rw_w2"][0].rearrange("e r n -> (e r) n")[:, wide]).then_inc(slices, 16)
                    sp.dma_start(lora_w[:, 1, :], d["rw_a2"][0].rearrange("e r n -> (e r) n")[:, wide]).then_inc(slices, 16)
                    sp.dma_start(lora_w[:, 2, :], d["rw_g2"][0][:, wide]).then_inc(slices, 16)

                def put(t):
                    one = slice(t.at, t.at + 1) if isinstance(t.at, int) else bass.ds(t.at, 1)
                    sp.wait_ge(pair_done, t.at + 2)
                    sp.dma_start(dram[3][:, one, :].rearrange("p o t -> p (o t)"), gated[:]).then_inc(stored, 16)

                load(Pair(0, 0), True)
                load(Pair(1, 1), False)
                with sp.Fori(0, CT // 2 - 1) as i:
                    for k in range(2):
                        load(Pair(2 * i + 2 + k, k), False)
                        put(Pair(2 * i + k, k))
                put(Pair(CT - 2, 0))
                put(Pair(CT - 1, 1))
                sp.wait_ge(stored, 16 * (CT + 1))

            @block.tensor
            def _(pe):
                class Pe(Part):
                    eng = pe

                    def score(self, I, s):
                        if s == 0:
                            pe.wait_ge(bd_dve, I.g + 1)
                            need(pe, masked, 2 * I.g - 1)
                        else:
                            need(pe, t_copied, 10 * I.g)
                        for e, b in enumerate(blocks(I.j)):
                            for n in range(2):
                                mm = pe.matmul(SC_BANK[s][:, 256 * e + 128 * n:256 * e + 128 * n + 128], bk[:, n, 2 * e + s, :],
                                               ar[I.t.s][e][:, (2 * b + s) * P:(2 * b + s + 1) * P], start=True, stop=True)
                        mm.then_inc(scores, 1)

                    def turn(self, I, n):
                        if n:
                            need(pe, x_added, 12 * I.g + n - 2)
                        if n == 2:
                            pe.wait_ge(bd_act, I.g + 1)
                        src = vbd if n == 2 else bk[:, n]
                        for u in range(4):
                            mm = pe.transpose(TURN_BANK[n][:, u * P:(u + 1) * P], src[:, u, :], c.ident[:])
                        mm.then_inc(turned, 1)

                    def level0(self, I):
                        for e in range(2):
                            pe.wait_ge(lvl_ready, 12 * I.g + e + 1)
                            pe.wait_ge(tok_copied, 3 * I.g + 2 + e)
                            for s in range(2):
                                mm = pe.matmul(X_BANK[e][:, s * P:(s + 1) * P], lvl[0][:, e, s, :], c.ident[:],
                                               start=True, stop=True)
                            mm.then_inc(x_ready, 1)

                    def level(self, I, n):
                        x = inv_x[I.p]
                        for e in range(2):
                            pe.wait_ge(lvl_ready, 12 * I.g + 2 * n + e + 1)
                            pe.wait_ge(x_added, 12 * I.g + 2 * n + e - 1)
                            need(pe, t_copied, 10 * I.g + 2 * n + e - 3)
                            if n == 1 and e == 0:
                                pe.wait_ge(masked, 2 * I.g + 2)
                            for s in range(2):
                                mm = pe.matmul(T_BANK[e][:, s * P:(s + 1) * P], lvl[n % 2][:, e, s, :], x[:, e, 0, s, :],
                                               start=True, stop=True)
                            mm.then_inc(t_ready, 1)
                        for e in range(2):
                            pe.wait_ge(t_copied, 10 * I.g + 2 * n + e - 1)
                            for s in range(2):
                                mm = pe.matmul(X_BANK[e][:, (2 + s) * P:(3 + s) * P], t_sb[:, e, s, :], x[:, e, 1, s, :],
                                               start=True, stop=True)
                                if n < LEVELS - 1:
                                    mm = pe.matmul(X_BANK[e][:, s * P:(s + 1) * P], x[:, e, 1, s, :], t_sb[:, e, s, :],
                                                   start=True, stop=True)
                            mm.then_inc(x_ready, 1)

                    def rhs(self, C, q):
                        pe.wait_ge(tok_copied, 3 * C.g + 3)
                        need(pe, s_done, 2 * (2 * C.g + q))
                        for e, u, s in units(q):
                            out = CHAIN[:, e * P:(e + 1) * P]
                            alone = C.j == q == 0
                            mm = pe.matmul(out, sc[C.p][:, u, 2, :], tok[C.p][:, 2, u, :], start=True, stop=alone)
                            if not alone:
                                mm = pe.matmul(out, arbd[C.p][:, u, 0, :], state[q][:, e, :], start=False, stop=True)
                        mm.then_inc(rhs_ready, 1)

                    def u(self, C, q):
                        pe.wait_ge(rhs_copied, 2 * C.g + q + 1)
                        pe.wait_ge(x_added, 12 * (C.g + 1))
                        for e, u, s in units(q):
                            mm = pe.matmul(CHAIN[:, 256 + e * P:256 + (e + 1) * P], inv_x[C.p][:, e, 1, s, :], rhs[:, e, :],
                                           start=True, stop=True)
                        mm.then_inc(u_ready, 1)

                    def sy(self, C, q):
                        pe.wait_ge(u_copied, 2 * C.g + q + 1)
                        for e, u, s in units(q):
                            out = CHAIN[:, e * P:(e + 1) * P]
                            pe.matmul(out, tok[C.p][:, 1, u, :], tok[C.p][:, 2, u, :], start=True, stop=False)
                            mm = pe.matmul(out, tok[C.p][:, 0, u, :], u_sb[:, e, :], start=False, stop=True)
                        mm.then_inc(s_ready, 1)
                        if q == 0:
                            need(pe, y_copied, C.g)
                        for e, u, s in units(q):
                            out = Y_BANK[:, u * P:(u + 1) * P]
                            alone = C.j == q == 0
                            pe.matmul(out, tok[C.p][:, 2, u, :], sc[C.p][:, u, 3, :], start=True, stop=False)
                            if not alone:
                                pe.matmul(out, state[q][:, e, :], arbd[C.p][:, u, 1, :], start=False, stop=False)
                            mm = pe.matmul(out, u_sb[:, e, :], sc[C.p][:, u, 1, :], start=False, stop=True)
                        mm.then_inc(y_ready, 1)

                    def use_side(self, n, lhs, src, seg):
                        need(pe, f_read, n)
                        pe.matmul(SIDE[:, 0:seg[1]], lhs, src[:, seg[0]:seg[0] + seg[1]], start=True, stop=True)\
                            .then_inc(f_ready, 1)

                    def feature(self, t, n):
                        base = side_uses(t, False)
                        if n == 1:
                            pe.wait_ge(slices, 96 * (t.at + 1))
                        if 1 <= n <= 10:
                            m, seg = map_piece(n)
                            rows = slice(64 * (m % 2), 64 * (m % 2) + 64) if m < 4 else slice(0, P)
                            self.use_side(base + n - 1, lora_w[rows, m // 2, :], hidden[rows, m // 2, :], seg)
                        if n in (11, 12):
                            pe.wait_ge(kk_sq, t.at + 1)
                            self.use_side(base + n - 1, c.ones_head[:], tmp, SEGS[n - 11])
                        if n in (26, 27):
                            pe.wait_ge(bonus_in, t.at + 1)
                            self.use_side(base + n - 14, c.ones_head[:], tmp, SEGS[n - 26])

                    def readout(self, t, n):
                        base = side_uses(t, True)
                        if n in (1, 2):
                            pe.wait_ge(y_in, t.at + 1)
                            self.use_side(base + n - 1, c.ones_head[:], y[t.s][0], SEGS[n - 1])
                        if n in (4, 5):
                            pe.wait_ge(y_sq, t.at + 1)
                            self.use_side(base + n - 2, c.ones_head[:], ytmp, SEGS[n - 4])

                pe.wait_ge(zeroed, 1)
                schedule(Pe())

            @block.vector
            def _(dve):
                v = nc.vector
                step = Order(dve, dve_order)

                class Dve(Part):
                    eng, order, per = dve, step, DVE_STEPS

                    def place_bk(self, I):
                        need(dve, turned, 3 * I.g - 1)
                        for n, src in enumerate((b_in, k_in)):
                            for e, b in enumerate(blocks(I.j)):
                                for h in range(2):
                                    ins = v.tensor_copy(bk[half(h), n, 2 * e:2 * e + 2, half(h)],
                                                        chunks(src[I.t.s][e][half(h), 2 * b * CH:2 * (b + 1) * CH]))
                        signal(dve, ins, bd_dve, I.g + 1)

                    def score(self, I, s):
                        dve.wait_ge(scores, 2 * I.g + s + 1)
                        if s == 0:
                            need(dve, y_ready, 2 * I.g - 2)
                        for h in range(2):
                            psum = SC_BANK[s][half(h), :].rearrange("p (e k t) -> p e k t", e=2, t=CH)
                            ins = v.tensor_tensor(sc[I.p][half(h), s:s + 3:2, :, half(h)], psum,
                                                  c.score_mask[half(h), :, :, :], ALU.mult)
                        signal(dve, ins, masked, 2 * I.g + s + 1)

                    def level0(self, I):
                        for e in range(2):
                            x = inv_x[I.p][:, e]
                            ident2 = c.ident[:].unsqueeze(1).to_broadcast([P, 2, P])
                            dve.wait_ge(lvl_ready, 12 * I.g + e + 1)
                            v.tensor_tensor(x[:, 1], lvl[0][:, e], ident2, ALU.add)
                            dve.wait_ge(x_ready, 12 * I.g + e + 1)
                            signal(dve, v.tensor_tensor(x[:, 0], pair4(X_BANK[e][:, 0:256]), ident2, ALU.add),
                                   x_added, 12 * I.g + e + 1)

                    def level(self, I, n):
                        for e in range(2):
                            x = inv_x[I.p][:, e].rearrange("p k s t -> p (k s t)")
                            lo = 256 if n == LEVELS - 1 else 0
                            dve.wait_ge(x_ready, 12 * I.g + 2 * n + e + 1)
                            signal(dve, v.tensor_tensor(x[:, lo:], X_BANK[e][:, lo:], x[:, lo:], ALU.add),
                                   x_added, 12 * I.g + 2 * n + e + 1)

                    def sy(self, C, q):
                        dve.wait_ge(s_ready, 2 * C.g + q + 1)
                        need(dve, y_ready, 2 * C.g + q)
                        for e, b in enumerate(blocks(C.j)):
                            m = 2 * C.j + q
                            end = chunk_end(C.t.s, e, 2 * b + (q if e == 0 else 1 - q))
                            psum = CHAIN[:, e * P:(e + 1) * P]
                            if m:
                                dve.wait_ge(s_decayed, 22 * C.t.at + 2 * m + e - 1)
                                ins = v.scalar_tensor_tensor(state[1 - q][:, e, :], psum, end, decayed[:, e, :],
                                                             ALU.mult, ALU.add)
                            else:
                                ins = v.tensor_scalar(state[1 - q][:, e, :], psum, end, None, ALU.mult)
                            signal(dve, ins, s_done, 2 * (2 * C.g + q) + e + 1)

                    def side_read(self, n, ins):
                        signal(dve, ins, f_read, n + 1)

                    def feature(self, t, n):
                        base, p = side_uses(t, False), cols[t.s]
                        col = lambda i: p[:, i:i + 1]
                        third = lambda i: slice(256 * i, 256 * i + 256)
                        if n == 0:
                            at = slice(t.at, t.at + 1) if isinstance(t.at, int) else bass.ds(t.at, 1)
                            step(v.tensor_copy(p[:], c.par[:, PW0:PW0 + 10 * CT].rearrange("p (n k) -> p n k", k=CT)
                                               [:, :, at].rearrange("p n k -> p (n k)")))
                            dve.wait_ge(slices, 96 * (t.at + 1))
                            signal(dve, v.tensor_scalar(kk[:], k_s[:], col(KK), None, ALU.mult), kk_raw, t.at + 1)
                        elif n == 4:
                            dve.wait_ge(f_read, base + 2)
                            signal(dve, v.tensor_tensor_scan(cum[0][:], c.keep[:], sig_w[0][:], 0.0, ALU.mult, ALU.add),
                                   cumd, 2 * t.at + 1)
                        elif n == 6:
                            dve.wait_ge(f_read, base + 4)
                            signal(dve, v.tensor_tensor_scan(cum[1][:, ::-1], c.keep[:], sig_w[1][:, ::-1], 0.0,
                                                             ALU.mult, ALU.add), cumd, 2 * t.at + 2)
                        elif n in (11, 12):
                            at, width = SEGS[n - 11]
                            dve.wait_ge(f_ready, base + n)
                            self.side_read(base + n - 1, v.tensor_scalar(tmp[:, at:at + width], SIDE[:, 0:width], 1e-24,
                                                                         None, ALU.max))
                        elif n in (13, 15):
                            e = (n - 13) // 2
                            dve.wait_ge(f_read, base + 8)
                            step(v.tensor_scalar(k_in[t.s][e], b_in[t.s][e], col(KA), col(LESS), ALU.mult, ALU.add))
                        elif n in (14, 16):
                            e = (n - 14) // 2
                            step(v.tensor_tensor(k_in[t.s][e], k_in[t.s][e], k_s[:], ALU.mult))
                        elif n in (18, 19, 20):
                            dve.wait_ge(kk_root, t.at + 1)
                            part = tmp[:, third(n - 18)]
                            step(v.reciprocal(part, part))
                        elif n == 21:
                            step(v.tensor_tensor(kk[:], kk[:], tmp[:], ALU.mult))
                        elif n in (22, 23):
                            step(v.tensor_tensor(b_in[t.s][n - 22], b_in[t.s][n - 22], kk[:], ALU.mult))
                        elif n == 24:
                            step(v.tensor_tensor(tmp[:], k_in[t.s][0], k_in[t.s][1], ALU.add))
                        elif n == 25:
                            signal(dve, v.scalar_tensor_tensor(tmp[:], tmp[:], col(RK), r_s[:], ALU.mult, ALU.mult),
                                   bonus_in, t.at + 1)
                        elif n in (26, 27):
                            at, width = SEGS[n - 26]
                            dve.wait_ge(f_ready, base + n - 13)
                            self.side_read(base + n - 14, v.tensor_tensor(bonus[t.s][:, at:at + width], SIDE[:, 0:width],
                                                                          v_s[t.s][:, at:at + width], ALU.mult))
                        elif n >= 28:
                            e = (n - 28) // 4
                            before, through = ((ep[t.s][0][:, :, 0:CH], ep[t.s][0][:, :, 1:]) if e == 0 else
                                               (ep[t.s][1][:, :, 1:], ep[t.s][1][:, :, 0:CH]))
                            dve.wait_ge(decays, 4 * t.at + 2 * e + 2)
                            out = ar4[t.s][e]
                            ins = (lambda: v.scalar_tensor_tensor(out[:, :, 0, :], chunks(kk[:]), -1.0, before, ALU.mult, ALU.mult),
                                   lambda: v.tensor_tensor(out[:, :, 1, :], chunks(r_s[:]), through, ALU.mult),
                                   lambda: v.tensor_tensor(b_in[t.s][e], b_in[t.s][e], sig_w[e][:], ALU.mult),
                                   lambda: v.tensor_tensor(k_in[t.s][e], k_in[t.s][e], sig_w[e][:], ALU.mult))[(n - 28) % 4]()
                            if n == NF - 1:
                                signal(dve, ins, features, t.at + 1)
                            else:
                                step(ins)

                    def readout(self, t, n):
                        base, p, out = side_uses(t, True), cols[t.s], y[t.s][0]
                        if n == 0:
                            dve.wait_ge(y_copied, NB * (t.at + 1))
                            signal(dve, v.tensor_tensor(out, out, y[t.s][1], ALU.add), y_in, t.at + 1)
                        elif n in (1, 2):
                            at, width = SEGS[n - 1]
                            dve.wait_ge(f_ready, base + n)
                            self.side_read(base + n - 1, v.scalar_tensor_tensor(out[:, at:at + width], SIDE[:, 0:width],
                                                                                -1.0 / CH, out[:, at:at + width],
                                                                                ALU.mult, ALU.add))
                        elif n in (6, 7, 8):
                            dve.wait_ge(f_read, base + 4)
                            part = ytmp[:, 256 * (n - 6):256 * (n - 5)]
                            step(v.reciprocal(part, part))
                        elif n == 9:
                            step(v.tensor_tensor(out, out, ytmp[:], ALU.mult))
                        elif n == 10:
                            step(v.tensor_scalar(out, out, p[:, LG:LG + 1], p[:, LB:LB + 1], ALU.mult, ALU.add))
                        elif n == 11:
                            step(v.tensor_tensor(out, out, bonus[t.s], ALU.add))
                        elif n == 12:
                            dve.wait_ge(stored, 16 * t.at + 16)
                            signal(dve, v.tensor_tensor(gated[:], out, gate[t.s], ALU.mult), pair_done, t.at + 2)

                for t in (bk, vbd, arbd[0], arbd[1], sc[0], sc[1]):
                    step(v.memset(t[:], 0.0))
                for s in range(2):
                    step(v.memset(ep[s][0][:, :, 0:1], 1.0))
                    step(v.memset(ep[s][1][:, :, CH:CH + 1], 1.0))
                signal(dve, v.memset(kk[:], 0.0), zeroed, 1)
                signal(dve, v.memset(gated[:], 0.0), pair_done, 1)
                v.memset(ytmp[:], 0.0).then_inc(stored, 16)
                dve.wait_ge(stored, 16)
                schedule(Dve())

            @block.scalar
            def _(act):
                a = nc.scalar

                class Act(Part):
                    eng = act

                    def place_arv(self, I):
                        need(act, turned, 3 * I.g)
                        need(act, y_ready, 2 * I.g - 2)
                        act.wait_ge(features, I.t.at + 1)
                        for e, b in enumerate(blocks(I.j)):
                            for h in range(2):
                                a.copy(arbd[I.p][half(h), 2 * e:2 * e + 2, :, half(h)],
                                       ar4[I.t.s][e][half(h), 2 * b:2 * b + 2, :, :])
                                ins = a.copy(vbd[half(h), 2 * e:2 * e + 2, half(h)],
                                             chunks(v_s[I.t.s][half(h), 2 * b * CH:2 * (b + 1) * CH]))
                        signal(act, ins, bd_act, I.g + 1)

                    def turn(self, I, n):
                        act.wait_ge(turned, 3 * I.g + n + 1)
                        signal(act, a.copy(tok[I.p][:, n], pair4(TURN_BANK[n][:, :])), tok_copied, 3 * I.g + n + 1)

                    def level(self, I, n):
                        for e in range(2):
                            act.wait_ge(t_ready, 10 * I.g + 2 * n + e - 1)
                            act.wait_ge(x_ready, 12 * I.g + 2 * n + e - 1)
                            signal(act, a.copy(t_sb[:, e], pair4(T_BANK[e][:, 0:256])), t_copied, 10 * I.g + 2 * n + e - 1)

                    def rhs(self, C, q):
                        act.wait_ge(rhs_ready, 2 * C.g + q + 1)
                        signal(act, a.copy(rhs[:], pair4(CHAIN[:, 0:256])), rhs_copied, 2 * C.g + q + 1)

                    def u(self, C, q):
                        act.wait_ge(u_ready, 2 * C.g + q + 1)
                        need(act, y_ready, 2 * C.g + q)
                        signal(act, a.copy(u_sb[:], pair4(CHAIN[:, 256:512])), u_copied, 2 * C.g + q + 1)

                    def y_out(self, C):
                        act.wait_ge(y_ready, 2 * C.g + 2)
                        if C.j == 0:
                            need(act, pair_done, C.t.at)
                        for e, b in enumerate(blocks(C.j)):
                            for h in range(2):
                                ins = a.copy(chunks(y[C.t.s][e][half(h), 2 * b * CH:2 * (b + 1) * CH]),
                                             pair4(Y_BANK[half(h), 256 * e:256 * e + 256])[:, :, half(h)])
                        signal(act, ins, y_copied, C.g + 1)

                    def side_read(self, n, ins):
                        signal(act, ins, f_read, n + 1)

                    def feature(self, t, n):
                        base = side_uses(t, False)
                        if n == 1:
                            act.wait_ge(kk_raw, t.at + 1)
                            signal(act, a.activation(tmp[:], kk[:], ACT.Square), kk_sq, t.at + 1)
                        if 1 <= n <= 10:
                            m, (at, width) = map_piece(n)
                            act.wait_ge(f_ready, base + n)
                            src = SIDE[:, 0:width]
                            if m < 4:
                                dst = (sig_w if m < 2 else b_in[t.s])[m % 2]
                                param = (W0 if m < 2 else A0) + m % 2
                                ins = a.activation(dst[:, at:at + width], src, ACT.Sigmoid, bias=cols[t.s][:, param:param + 1])
                            else:
                                ins = a.copy(gate[t.s][:, at:at + width], src)
                            self.side_read(base + n - 1, ins)
                        elif n in (13, 15):
                            e = (n - 13) // 2
                            act.wait_ge(cumd, 2 * t.at + e + 1)
                            through = ep[t.s][0][:, :, 1:] if e == 0 else ep[t.s][1][:, :, 0:CH]
                            signal(act, a.activation(through, chunks(cum[e][:]), ACT.Exp, scale=-DECAY),
                                   decays, 4 * t.at + 2 * e + 1)
                        elif n in (14, 16):
                            e = (n - 14) // 2
                            signal(act, a.activation(sig_w[e][:], cum[e][:], ACT.Exp, scale=DECAY),
                                   decays, 4 * t.at + 2 * e + 2)
                        elif n == 17:
                            act.wait_ge(f_read, base + 12)
                            signal(act, a.activation(tmp[:], tmp[:], ACT.Sqrt), kk_root, t.at + 1)

                    def readout(self, t, n):
                        base = side_uses(t, True)
                        if n == 3:
                            act.wait_ge(f_read, base + 2)
                            signal(act, a.activation(ytmp[:], y[t.s][0], ACT.Square), y_sq, t.at + 1)
                        elif n in (4, 5):
                            at, width = SEGS[n - 4]
                            act.wait_ge(f_ready, base + n - 1)
                            self.side_read(base + n - 2, a.activation(ytmp[:, at:at + width], SIDE[:, 0:width], ACT.Sqrt,
                                                                      scale=1.0 / CH, bias=c.eps[:, 1:2]))

                act.wait_ge(zeroed, 1)
                schedule(Act())

            @block.gpsimd
            def _(pool):
                class Pool(Part):
                    eng = pool

                    def cut(self, I, n):
                        if n == 0:
                            pool.wait_ge(masked, 2 * I.g + 2)
                        for e in range(2):
                            need(pool, x_ready, 12 * I.g + 2 * n + e - 3)
                            if n == 2:
                                pool.wait_ge(x_added, 12 * I.g + e + 1)
                            signal(pool, nc.gpsimd.tensor_tensor(
                                lvl[n % 2][:, e], sc[I.p][:, 2 * e:2 * e + 2, 0, :],
                                c.level_mask[:, n, e, :].unsqueeze(1).to_broadcast([P, 2, P]), ALU.mult),
                                lvl_ready, 12 * I.g + 2 * n + e + 1)

                    def level0(self, I):
                        self.cut(I, 0)
                        self.cut(I, 1)

                    def level(self, I, n):
                        if n < LEVELS - 1:
                            self.cut(I, n + 1)

                    def rhs(self, C, q):
                        m = 2 * C.j + q
                        if m == 0:
                            return
                        pool.wait_ge(s_done, 2 * (2 * C.g + q))
                        for e, b in enumerate(blocks(C.j)):
                            end = chunk_end(C.t.s, e, 2 * b + (q if e == 0 else 1 - q))
                            signal(pool, nc.gpsimd.tensor_tensor(decayed[:, e, :], state[q][:, e, :],
                                                                 end.to_broadcast([P, P]), ALU.mult),
                                   s_decayed, 22 * C.t.at + 2 * m + e - 1)

                schedule(Pool())


DVE_STEPS = 50


def zero_padding(c, apad):
    nc = c.nc
    with ExitStack() as ctx:
        padded = ctx.enter_context(nc.semaphore("padded"))
        with nc.Block() as block:
            @block.vector
            def _(dve):
                for at in (0, CTX + 1, TOK + 2):
                    nc.vector.memset(apad[:, :, at:at + 1], 0.0).then_inc(padded, 1)
                dve.wait_ge(padded, 3)


def dense(c, name, weight, k_tiles, m_tiles, rhs, segs, h, layer, gate_row):
    nc = c.nc
    with ExitStack() as ctx:
        w = [ctx.enter_context(nc.sbuf_tensor(f"{name}_w{s}", [P, k_tiles, P], F32)) for s in range(2)]
        loaded = [ctx.enter_context(nc.semaphore(f"{name}_w_loaded{s}")) for s in range(2)]
        product = ctx.enter_context(nc.semaphore(f"{name}_product"))
        added = ctx.enter_context(nc.semaphore(f"{name}_added"))
        view = weight.rearrange("(k p) e -> p k e", p=P)
        with nc.Block() as block:
            @block.sync
            def _(sp):
                for s in range(2):
                    sp.dma_start(w[s][:], view[:, :, s * P:(s + 1) * P]).then_inc(loaded[s], 16)
                with sp.Fori(1, m_tiles // 2) as i:
                    for s in range(2):
                        sp.wait_ge(product, 2 * i + s - 1)
                        sp.dma_start(w[s][:], view[:, :, bass.ds((2 * i + s) * P, P)]).then_inc(loaded[s], 16)

            @block.tensor
            def _(pe):
                def pair(i, first):
                    for s in range(2):
                        pe.wait_ge(loaded[s], 16 * (i + 1))
                        if not first:
                            pe.wait_ge(added, len(segs) * (2 * i + s - 1))
                        for k in range(k_tiles):
                            for n, (at, width) in enumerate(segs):
                                mm = pe.matmul(c.bank[2 * s + n][:, 0:width], w[s][:, k, :], rhs(k, at, width),
                                               start=(k == 0), stop=(k == k_tiles - 1))
                        mm.then_inc(product, 1)

                pair(0, True)
                with pe.Fori(1, m_tiles // 2) as i:
                    pair(i, False)

            @block.vector
            def _(dve):
                with dve.Fori(0, m_tiles // 2) as i:
                    for s in range(2):
                        m = 2 * i + s
                        dve.wait_ge(product, m + 1)
                        for n, (at, width) in enumerate(segs):
                            r = 1 if at == 0 else 0
                            gate = c.mod[:, layer, :, r][:, bass.ds(gate_row + m, 1)]
                            signal(dve, nc.vector.scalar_tensor_tensor(
                                h[:, m, at:at + width], c.bank[2 * s + n][:, 0:width], gate, h[:, m, at:at + width],
                                ALU.mult, ALU.add), added, len(segs) * m + n + 1)


def swiglu_up(c, name, w1, w3, f, segs, g):
    nc = c.nc
    with ExitStack() as ctx:
        w = [ctx.enter_context(nc.sbuf_tensor(f"{name}_w{s}", [P, 2, CT, P], F32)) for s in range(2)]
        silu = [ctx.enter_context(nc.sbuf_tensor(f"{name}_silu{s}", [P, TOK], F32)) for s in range(2)]
        loaded = [ctx.enter_context(nc.semaphore(f"{name}_w_loaded{s}")) for s in range(2)]
        product = ctx.enter_context(nc.semaphore(f"{name}_product"))
        activated = ctx.enter_context(nc.semaphore(f"{name}_activated"))
        multiplied = ctx.enter_context(nc.semaphore(f"{name}_multiplied"))
        views = [x.rearrange("(k p) e -> p k e", p=P) for x in (w1, w3)]
        ns = len(segs)
        with nc.Block() as block:
            @block.sync
            def _(sp):
                def load(s, cols):
                    for n in range(2):
                        sp.dma_start(w[s][:, n], views[n][:, :, cols]).then_inc(loaded[s], 16)

                for s in range(2):
                    load(s, slice(s * P, (s + 1) * P))
                with sp.Fori(1, FT // 2) as i:
                    for s in range(2):
                        sp.wait_ge(product, 2 * i + s - 1)
                        load(s, bass.ds((2 * i + s) * P, P))

            @block.tensor
            def _(pe):
                def pair(i, first):
                    for s in range(2):
                        pe.wait_ge(loaded[s], 32 * (i + 1))
                        if not first:
                            pe.wait_ge(multiplied, ns * (2 * i + s - 1))
                        for n in range(2):
                            for k in range(CT):
                                for q, (at, width) in enumerate(segs):
                                    mm = pe.matmul(c.bank[4 * s + 2 * n + q][:, 0:width], w[s][:, n, k, :],
                                                   f[:, k, at:at + width], start=(k == 0), stop=(k == CT - 1))
                        mm.then_inc(product, 1)

                pair(0, True)
                with pe.Fori(1, FT // 2) as i:
                    pair(i, False)

            @block.scalar
            def _(act):
                def pair(i, first):
                    for s in range(2):
                        m = 2 * i + s
                        act.wait_ge(product, m + 1)
                        if not first:
                            act.wait_ge(multiplied, ns * (m - 1))
                        for q, (at, width) in enumerate(segs):
                            signal(act, nc.scalar.activation(silu[s][:, at:at + width], c.bank[4 * s + q][:, 0:width],
                                                             ACT.Silu), activated, ns * m + q + 1)

                pair(0, True)
                with act.Fori(1, FT // 2) as i:
                    pair(i, False)

            @block.vector
            def _(dve):
                with dve.Fori(0, FT // 2) as i:
                    for s in range(2):
                        m = 2 * i + s
                        for q, (at, width) in enumerate(segs):
                            dve.wait_ge(activated, ns * m + q + 1)
                            dve.wait_ge(product, m + 1)
                            signal(dve, nc.vector.tensor_tensor(
                                g[:, m, at:at + width], c.bank[4 * s + 2 + q][:, 0:width], silu[s][:, at:at + width],
                                ALU.mult), multiplied, ns * m + q + 1)


def reload(c, parts):
    nc = c.nc
    with ExitStack() as ctx:
        loaded = ctx.enter_context(nc.semaphore("residual_loaded"))
        with nc.Block() as block:
            @block.sync
            def _(sp):
                for dst, src in parts:
                    sp.dma_start(dst, src).then_inc(loaded, 16)
                sp.wait_ge(loaded, 16 * len(parts))


def qkv(c, d, f, q, k, v):
    nc = c.nc
    NH = KV_HEADS + HEADS
    KVD = KV_HEADS * P
    with ExitStack() as ctx:
        sb = lambda n, s: ctx.enter_context(nc.sbuf_tensor(n, s, F32))
        sem = lambda n: ctx.enter_context(nc.semaphore(n))
        w = [sb(f"qk_w{s}", [P, CT, P]) for s in range(2)]
        wv = sb("wv", [P, CT, KVD])
        cos, sin, swap = sb("cos", [P, LAT]), sb("sin", [P, LAT]), sb("swap", [P, P])
        raw, sq, std, turned = sb("qk_raw", [P, TOK]), sb("qk_sq", [P, TOK]), sb("qk_std", [P, TOK]), sb("qk_turned", [P, LAT])
        tables, v_loaded = sem("rope_loaded"), sem("wv_loaded")
        loaded = [sem(f"qk_w_loaded{s}") for s in range(2)]
        product, v_product, v_copied = sem("qk_product"), sem("v_product"), sem("v_copied")
        copied, squared, summed, rooted, normed, swapped, rotated, ctx_out, order = (sem(n) for n in (
            "qk_copied", "qk_squared", "qk_summed", "qk_rooted", "qk_normed", "qk_swapped", "qk_rotated", "qk_ctx_out",
            "qk_dve_order"))
        wk = d["at_wk"][0].rearrange("(k p) e -> p k e", p=P)
        wq = d["at_wq"][0].rearrange("(k p) e -> p k e", p=P)
        with nc.Block() as block:
            @block.sync
            def _(sp):
                sp.dma_start(wv[:], d["at_wv"][0].rearrange("(k p) e -> p k e", p=P)).then_inc(v_loaded, 16)
                for s in range(2):
                    sp.dma_start(w[s][:], wk[:, :, s * P:(s + 1) * P]).then_inc(loaded[s], 16)
                for t, s in ((cos, "k_cos"), (sin, "k_sin"), (swap, "k_swap")):
                    sp.dma_start(t[:], d[s]).then_inc(tables, 16)
                with sp.Fori(0, HEADS // 2) as i:
                    for s in range(2):
                        sp.wait_ge(product, 2 * i + s + 1)
                        sp.dma_start(w[s][:], wq[:, :, bass.ds((2 * i + s) * P, P)]).then_inc(loaded[s], 16)

            @block.tensor
            def _(pe):
                pe.wait_ge(v_loaded, 16)
                for t in range(TOK // P):
                    if t >= 2:
                        pe.wait_ge(v_copied, t - 1)
                    for kt in range(CT):
                        mm = pe.matmul(c.bank[6 + t % 2][:, 0:KVD], f[:, kt, t * P:(t + 1) * P], wv[:, kt, :],
                                       start=(kt == 0), stop=(kt == CT - 1))
                    mm.then_inc(v_product, 1)
                pe.wait_ge(tables, 48)

                def pair(i):
                    for s in range(2):
                        n = 2 * i + s
                        pe.wait_ge(loaded[s], 16 * (i + 1))
                        need(pe, copied, 2 * n)
                        for kt in range(CT):
                            for b, (at, width) in enumerate(SEGS):
                                mm = pe.matmul(c.bank[b][:, 0:width], w[s][:, kt, :], f[:, kt, at:at + width],
                                               start=(kt == 0), stop=(kt == CT - 1))
                        mm.then_inc(product, 1)
                        pe.wait_ge(squared, n + 1)
                        need(pe, rooted, 2 * n)
                        for b, (at, width) in enumerate(SEGS):
                            mm = pe.matmul(c.bank[2 + b][:, 0:width], c.ones[:], sq[:, at:at + width],
                                           start=True, stop=True)
                        mm.then_inc(summed, 1)
                        pe.wait_ge(normed, n + 1)
                        need(pe, rotated, n)
                        pe.matmul(c.bank[4][:, 0:LAT], swap[:], raw[:, CTX:TOK], start=True, stop=True)\
                            .then_inc(swapped, 1)

                by_two(pe, 0, NH // 2, pair)

            @block.scalar
            def _(act):
                for t in range(TOK // P):
                    act.wait_ge(v_product, t + 1)
                    signal(act, nc.scalar.copy(v[:, t, :], c.bank[6 + t % 2][:, 0:KVD]), v_copied, t + 1)

                def pair(i):
                    for s in range(2):
                        n = 2 * i + s
                        act.wait_ge(product, n + 1)
                        need(act, rotated, n)
                        for b, (at, width) in enumerate(SEGS):
                            signal(act, nc.scalar.copy(raw[:, at:at + width], c.bank[b][:, 0:width]), copied, 2 * n + b + 1)
                        signal(act, nc.scalar.activation(sq[:], raw[:], ACT.Square), squared, n + 1)
                        act.wait_ge(summed, n + 1)
                        for b, (at, width) in enumerate(SEGS):
                            signal(act, nc.scalar.activation(std[:, at:at + width], c.bank[2 + b][:, 0:width], ACT.Sqrt,
                                                             scale=1.0 / P, bias=c.eps[:, 0:1]), rooted, 2 * n + b + 1)

                by_two(act, 0, NH // 2, pair)

            @block.vector
            def _(dve):
                step = Order(dve, order)
                v_ = nc.vector

                def head(n, gain, out, at_n):
                    dve.wait_ge(rooted, 2 * (n + 1))
                    step(v_.reciprocal(std[:], std[:]))
                    signal(dve, v_.scalar_tensor_tensor(raw[:], raw[:], c.par[:, gain:gain + 1], std[:], ALU.mult, ALU.mult),
                           normed, n + 1)
                    step(v_.tensor_tensor(turned[:], raw[:, CTX:TOK], cos[:], ALU.mult))
                    dve.wait_ge(swapped, n + 1)
                    step(v_.tensor_tensor(out[:, at_n, CTX - lo(out):TOK - lo(out)], c.bank[4][:, 0:LAT], sin[:], ALU.mult))
                    if out is k:
                        step(v_.tensor_copy(out[:, at_n, 0:CTX], raw[:, 0:CTX]))
                    o = out[:, at_n, CTX - lo(out):TOK - lo(out)]
                    signal(dve, v_.tensor_tensor(o, o, turned[:], ALU.add), rotated, n + 1)

                lo = lambda out: 0 if out is k else CTX
                for n in range(KV_HEADS):
                    head(n, PGK, k, n)
                with dve.Fori(0, HEADS // 2) as i:
                    step.enter(i, 6)
                    for s in range(2):
                        head(KV_HEADS + 2 * i + s, PGQ, q, 2 * i + s)
                    step.leave(HEADS // 2)


def attend(c, q, k, v, o):
    nc = c.nc
    QT = LAT // P
    T = TOK // P
    SCALE = float(P) ** -0.5
    G = HEADS // KV_HEADS
    with ExitStack() as ctx:
        sb = lambda n, s: ctx.enter_context(nc.sbuf_tensor(n, s, F32))
        sem = lambda n: ctx.enter_context(nc.semaphore(n))
        qh = sb("qh", [P, LAT])
        prob = [sb(f"prob{s}", [P, TOK]) for s in range(2)]
        pt = sb("prob_t", [P, T, LAT])
        mx, nmx, den, rec = sb("mx", [P, 2, 2]), sb("nmx", [P, 2]), sb("den", [P, 2, 2]), sb("rec", [P, 2])
        q_placed, scored, maxed, expd, scaled, turned, copied_a, copied_b, out_ready, out_copied, order = (sem(n) for n in (
            "q_placed", "scored", "maxed", "exponentials", "prob_scaled", "prob_turned", "prob_copied_act",
            "prob_copied_dve", "out_ready", "out_copied", "att_order"))
        with nc.Block() as block:
            def heads(eng, body, step=None):
                body(0, 0)
                for kv in range(KV_HEADS):
                    start = 1 if kv == 0 else 0
                    with eng.Fori(start, G) as i:
                        if step:
                            step.enter(i - start if start else i, 4 * QT)
                        body(kv, G * kv + i)
                        if step:
                            step.leave(G - start)

            @block.tensor
            def _(pe):
                def body(kv, h):
                    pe.wait_ge(q_placed, h + 1)
                    def turn(t):
                        n = QT * h + t
                        pe.wait_ge(scaled, n + 1)
                        need(pe, copied_a, n)
                        need(pe, copied_b, n)
                        for s in range(T):
                            out = c.bank[4][:, s * P:(s + 1) * P] if s < 4 else c.bank[5][:, (s - 4) * P:(s - 3) * P]
                            mm = pe.transpose(out, prob[t % 2][:, s * P:(s + 1) * P], c.ident[:])
                        mm.then_inc(turned, 1)

                    for t in range(QT):
                        n = QT * h + t
                        s = 2 * (t % 2)
                        if t >= 2:
                            pe.wait_ge(expd, 2 * (n - 1))
                        else:
                            need(pe, expd, 2 * QT * h)
                        pe.matmul(c.bank[s][:, 0:CTX], qh[:, t * P:(t + 1) * P], k[:, kv, 0:CTX], start=True, stop=True)
                        pe.matmul(c.bank[s + 1][:, 0:LAT], qh[:, t * P:(t + 1) * P], k[:, kv, CTX:TOK],
                                  start=True, stop=True).then_inc(scored, 1)
                        if t:
                            turn(t - 1)
                    turn(QT - 1)
                    pe.wait_ge(copied_a, QT * (h + 1))
                    pe.wait_ge(copied_b, QT * (h + 1))
                    need(pe, out_copied, h)
                    for s in range(T):
                        mm = pe.matmul(c.bank[6][:, 0:LAT], v[:, s, kv * P:(kv + 1) * P], pt[:, s, :],
                                       start=(s == 0), stop=(s == T - 1))
                    mm.then_inc(out_ready, 1)

                heads(pe, body)

            @block.scalar
            def _(act):
                def body(kv, h):
                    def copy(t):
                        n = QT * h + t
                        act.wait_ge(turned, n + 1)
                        signal(act, nc.scalar.copy(pt[:, 4:T, t * P:(t + 1) * P],
                                                   c.bank[5][:, 0:256].rearrange("p (s t) -> p s t", t=P)), copied_a, n + 1)

                    for t in range(QT):
                        n = QT * h + t
                        act.wait_ge(maxed, n + 1)
                        need(act, turned, n - 1 if t >= 2 else QT * h)
                        for b, (at, width) in enumerate(SEGS):
                            signal(act, nc.scalar.activation(prob[t % 2][:, at:at + width], c.bank[2 * (t % 2) + b][:, 0:width],
                                                             ACT.Exp, scale=SCALE, bias=nmx[:, t % 2:t % 2 + 1],
                                                             accum_out=den[:, t % 2, b:b + 1]), expd, 2 * n + b + 1)
                        if t:
                            copy(t - 1)
                    copy(QT - 1)
                    act.wait_ge(out_ready, h + 1)
                    signal(act, nc.scalar.copy(o[:, h, :], c.bank[6][:, 0:LAT]), out_copied, h + 1)

                heads(act, body)

            @block.vector
            def _(dve):
                step = Order(dve, order)
                v_ = nc.vector

                def body(kv, h):
                    need(dve, out_copied, h)
                    signal(dve, v_.tensor_copy(qh[:], q[:, h, :]), q_placed, h + 1)

                    def scale(t):
                        n = QT * h + t
                        dve.wait_ge(expd, 2 * (n + 1))
                        step(v_.tensor_tensor(rec[:, t % 2:t % 2 + 1], den[:, t % 2, 0:1], den[:, t % 2, 1:2], ALU.add))
                        step(v_.reciprocal(rec[:, t % 2:t % 2 + 1], rec[:, t % 2:t % 2 + 1]))
                        signal(dve, v_.tensor_scalar(prob[t % 2][:], prob[t % 2][:], rec[:, t % 2:t % 2 + 1], None, ALU.mult),
                               scaled, n + 1)

                    def copy(t):
                        n = QT * h + t
                        dve.wait_ge(turned, n + 1)
                        signal(dve, v_.tensor_copy(pt[:, 0:4, t * P:(t + 1) * P],
                                                   c.bank[4][:].rearrange("p (s t) -> p s t", t=P)), copied_b, n + 1)

                    for t in range(QT):
                        n = QT * h + t
                        dve.wait_ge(scored, n + 1)
                        for b, (at, width) in enumerate(SEGS):
                            ins = v_.tensor_reduce(mx[:, t % 2, b:b + 1], c.bank[2 * (t % 2) + b][:, 0:width], AX, ALU.max)
                            step(ins)
                        signal(dve, v_.tensor_scalar(nmx[:, t % 2:t % 2 + 1], mx[:, t % 2, 0:1], mx[:, t % 2, 1:2], -SCALE,
                                                     ALU.max, ALU.mult), maxed, n + 1)
                        if t:
                            scale(t - 1)
                        if t:
                            copy(t - 1)
                    scale(QT - 1)
                    copy(QT - 1)

                heads(dve, body, step)


def store(c, h, out):
    nc = c.nc
    T = LAT // P
    with ExitStack() as ctx:
        y = ctx.enter_context(nc.sbuf_tensor("y_rows", [P, T, D], F32))
        turned, copied, stored = (ctx.enter_context(nc.semaphore(n)) for n in ("out_turned", "out_turned_copied", "stored"))
        rows = out[0].rearrange("(t p) e -> t p e", p=P)
        with nc.Block() as block:
            @block.tensor
            def _(pe):
                for t in range(T):
                    for q in range(2):
                        n = 2 * t + q
                        if n >= 4:
                            pe.wait_ge(copied, n - 3)
                        for k in range(4):
                            mm = pe.transpose(c.bank[n % 4][:, k * P:(k + 1) * P],
                                              h[:, 4 * q + k, CTX + t * P:CTX + (t + 1) * P], c.ident[:])
                        mm.then_inc(turned, 1)

            @block.vector
            def _(dve):
                for n in range(2 * T):
                    dve.wait_ge(turned, n + 1)
                    nc.vector.tensor_copy(y[:, n // 2, 512 * (n % 2):512 * (n % 2) + 512], c.bank[n % 4][:])\
                        .then_inc(copied, 1)

            @block.sync
            def _(sp):
                for t in range(T):
                    sp.wait_ge(copied, 2 * t + 2)
                    sp.dma_start(rows[t], y[:, t, :]).then_inc(stored, 16)
                sp.wait_ge(stored, 16 * T)


def backbone(nc, d, out):
    with ExitStack() as ctx:
        c = Core(nc, ctx)
        c.bank = [ctx.enter_context(nc.psum_tensor(f"bank{n}", [P, 512], F32)) for n in range(8)]
        c.ident, c.ones_head, c.ones = c.sb("ident", [P, P]), c.sb("ones_head", [P, P]), c.sb("ones", [P, P])
        c.level_mask = c.sb("level_mask", [P, LEVELS, 2, P])
        c.score_mask = c.sb("score_mask", [P, 2, 4, CH])
        c.keep = c.sb("keep", [P, TOK])
        c.par, c.mod, c.gain = c.sb("par", [P, NPAR]), c.sb("mod", [P, 2, 48, 2]), c.sb("gain", [P, 2, 2, 2, CT])
        c.cond, c.eps = c.sb("cond", [P, 16]), c.sb("eps", [P, 2])
        rkv_dram = [nc.dram_tensor(n, [P, CT, TOK], F32, kind="Internal").ap() for n in ("r_all", "k_all", "v_all", "mixed_all")]
        spill = nc.dram_tensor("residual", [P, CT, TOK], F32, kind="Internal").ap()
        both, latent = SEGS, SEGS[1:]

        setup(c, d)
        modulation(c, d)
        mixer_out, h, f = (c.sb(n, [P, CT, TOK]) for n in ("r_or_mixer_out", "k_or_residual", "v_or_normed"))

        with nc.sbuf_tensor("hidden", [P, 3, TOK], F32) as hidden:
            with nc.sbuf_tensor("apad", [P, CT, TOK + 3], F32) as apad:
                load_tokens(c, d, h, spill)
                zero_padding(c, apad)
                norm(c, "norm0", h, 0, 0,
                     lambda k, at, n: apad[:, k, (1 if at == 0 else at + 2):(1 if at == 0 else at + 2) + n], both)
                rwkv_inputs(c, d, apad, (mixer_out, h, f), hidden, rkv_dram)
            recurrence(c, d, rkv_dram, hidden, (h, f, mixer_out))
        reload(c, ((h[:], spill), (mixer_out[:], rkv_dram[3])))
        dense(c, "rwkv_out", d["rw_wo"][0], CT, CT, lambda k, at, n: mixer_out[:, k, at:at + n], both, h, 0, 16)
        feed_forward(c, d, h, f, 0, both)

        norm(c, "norm1", h, 1, 0, lambda k, at, n: f[:, k, at:at + n], both)
        with nc.sbuf_tensor("q_heads", [P, HEADS, LAT], F32) as q, nc.sbuf_tensor("k_heads", [P, KV_HEADS, TOK], F32) as k, \
                nc.sbuf_tensor("v_rows", [P, TOK // P, KV_HEADS * P], F32) as v:
            qkv(c, d, f, q, k, v)
            attend(c, q, k, v, mixer_out[:, :, CTX:TOK])
        dense(c, "att_out", d["at_wo"][0], CT, CT, lambda k, at, n: mixer_out[:, k, at:at + n], latent, h, 1, 16)
        feed_forward(c, d, h, f, 1, latent)
        store(c, h, out)


def feed_forward(c, d, h, f, layer, segs):
    norm(c, f"norm_ffn{layer}", h, layer, 1, lambda k, at, n: f[:, k, at:at + n], segs)
    with c.nc.sbuf_tensor(f"g{layer}", [P, FT, TOK], F32) as g:
        swiglu_up(c, f"up{layer}", d["ff_w1"][layer], d["ff_w3"][layer], f, segs, g)
        dense(c, f"down{layer}", d["ff_w2"][layer], FT, CT, lambda k, at, n: g[:, k, at:at + n], segs, h, layer, 40)


_INS = ["x", "c", "ctx", "c_ctx", "mod_w", "mod_b", "norm_mix", "norm_ffn", "ff_w1", "ff_w3", "ff_w2", "rw_mu", "rw_wr",
        "rw_wk", "rw_wv", "rw_wo", "rw_w0", "rw_w1", "rw_w2", "rw_a0", "rw_a1", "rw_a2", "rw_g1", "rw_g2", "rw_kk",
        "rw_ka", "rw_rk", "rw_lnx_g", "rw_lnx_b", "at_wq", "at_wk", "at_wv", "at_wo", "at_gq", "at_gk"]


def shape_tables():
    f = np.float32
    i, j = np.indices((P, P))
    level = np.zeros((P, LEVELS, 2, P), f)
    for n in range(LEVELS):
        same = (i >> (n + 1)) == (j >> (n + 1))
        first_i, first_j = (i >> n) & 1 == 0, (j >> n) & 1 == 0
        level[:, n, 0, :] = same & first_i & ~first_j
        level[:, n, 1, :] = same & ~first_i & first_j
    s, t = np.arange(P)[:, None] % CH, np.arange(CH)[None, :]
    score = np.stack([np.stack([m1, m2, m1, m2], 1) for m1, m2 in ((s < t, s <= t), (s > t, s >= t))], 1).astype(f)
    keep = np.broadcast_to(np.arange(TOK) % CH != 0, (P, TOK)).astype(f)
    tok = np.arange(LAT)
    inv = f(10000.0) ** (-np.arange(0, P // 2, 2, dtype=f) / f(P // 2))
    ang = np.concatenate([(tok // 64).astype(f)[:, None] * inv, (tok % 64).astype(f)[:, None] * inv], 1)
    pair = np.arange(P) // 2
    sign = np.where(np.arange(P) % 2 == 0, -1.0, 1.0)[:, None]
    return {
        "k_ident": np.eye(P, dtype=f),
        "k_ones_head": (i // CH == j // CH).astype(f),
        "k_level_mask": level,
        "k_score_mask": score,
        "k_keep": keep,
        "k_cos": np.cos(ang).T[pair].astype(f),
        "k_sin": (np.sin(ang).T[pair] * sign).astype(f),
        "k_swap": (i == (j ^ 1)).astype(f),
    }


def kernel(**inputs):
    import concourse.bacc as _bacc
    from concourse.bass_utils import run_bass_kernel_spmd as _run

    nc = _bacc.Bacc("TRN2", target_bir_lowering=False, num_devices=1)
    arrays, args = {}, {}
    for name, a in [(n, inputs[n]) for n in _INS] + list(shape_tables().items()):
        a = np.ascontiguousarray(a)
        arrays[f"in_{name}"] = a
        args[name] = nc.dram_tensor(f"in_{name}", a.shape, mybir.dt.from_np(a.dtype), kind="ExternalInput").ap()
    out = nc.dram_tensor("out", (1, LAT, D), F32, kind="ExternalOutput").ap()
    backbone(nc, args, out)
    r = _run(nc, [arrays], core_ids=[0])
    return r.results[0]["out"]
```

```python
from contextlib import ExitStack

import numpy as np

import concourse.bass as bass
from concourse import mybir

F32 = mybir.dt.float32
F32R = mybir.dt.float32r
ALU = mybir.AluOpType
ACT = mybir.ActivationFunctionType
AX = mybir.AxisListType.X

P = 128
D = 1024
CT = D // P
CTX, LAT = 256, 512
TOK = CTX + LAT
SEGS = ((0, CTX), (CTX, LAT))
FF = 2816
FT = FF // P
CH = 64
NCH = TOK // CH
NB = NCH // 2
LEVELS = 6
DECAY = float(np.exp(-0.5))
HEADS, KV_HEADS = 8, 2

PMODB, PC, PGQ, PGK = 0, 96, 112, 113
PMU = 114
PW0, PA0 = PMU + 48, PMU + 64
PKK, PKA, PRK, PLG, PLB = (PMU + 80 + 8 * n for n in range(5))
PLESS = PMU + 120
PNM = PLESS + CT
PNF = PNM + 16
NPAR = PNF + 16


class Order:

    def __init__(self, eng, sem):
        self.eng, self.sem, self.off, self.n, self.outer = eng, sem, 0, 0, []

    def __call__(self, ins):
        ins.then_inc(self.sem, 1)
        self.n += 1
        self.eng.wait_ge(self.sem, self.off + self.n)

    def enter(self, at, per):
        self.outer.append((self.off, self.n, per))
        self.off, self.n = self.off + self.n + at * per, 0

    def leave(self, trips):
        self.off, n, per = self.outer.pop()
        assert self.n == per, f"{self.n} steps, {per} expected"
        self.n = n + trips * per


def signal(eng, ins, sem, value):
    ins.then_inc(sem, 1)
    eng.wait_ge(sem, value)


def need(eng, sem, n):
    if not isinstance(n, int) or n > 0:
        eng.wait_ge(sem, n)


def by_two(eng, start, stop, pair):
    if start == 0:
        pair(0)
        start = 1
    with eng.Fori(start, stop) as i:
        pair(i)


class Core:

    def __init__(self, nc, ctx):
        self.nc, self.ctx, self.count = nc, ctx, 0

    def sb(self, name, shape):
        return self.ctx.enter_context(self.nc.sbuf_tensor(name, shape, F32))

    def sem(self, name):
        return self.ctx.enter_context(self.nc.semaphore(name))


def setup(c, d):
    nc = c.nc
    with ExitStack() as ctx:
        rows = [ctx.enter_context(nc.sbuf_tensor(f"par_rows{n}", [P, P], F32)) for n in range(3)]
        loaded = ctx.enter_context(nc.semaphore("setup_loaded"))
        turned = ctx.enter_context(nc.semaphore("par_turned"))
        copied = ctx.enter_context(nc.semaphore("par_copied"))
        gated = ctx.enter_context(nc.semaphore("cond_silu"))
        row_of = lambda a: a.rearrange("(m p) -> m p", p=P)
        lists = [
            [d["mod_b"].rearrange("l (m p) -> (l m) p", p=P), d["c"].rearrange("b (m p) -> (b m) p", p=P),
             row_of(d["c_ctx"]), d["at_gq"], d["at_gk"]],
            [d["rw_mu"].rearrange("a n (m p) -> (a n m) p", p=P)]
            + [d[n].rearrange("a e (m p) -> (a e m) p", p=P) for n in ("rw_w0", "rw_a0")]
            + [d[n].rearrange("a (m p) -> (a m) p", p=P) for n in ("rw_kk", "rw_ka")]
            + [d["rw_rk"].rearrange("a (m h) k -> (a m) (h k)", h=2)]
            + [d[n].rearrange("a (m p) -> (a m) p", p=P) for n in ("rw_lnx_g", "rw_lnx_b")],
            [d[n].rearrange("a (m p) -> (a m) p", p=P) for n in ("norm_mix", "norm_ffn")],
        ]
        sizes = [114, 120, 32]
        n_loads = 5 + sum(len(x) for x in lists)
        with nc.Block() as block:
            @block.sync
            def _(sp):
                for t, s in ((c.ident, "k_ident"), (c.ones_head, "k_ones_head"), (c.level_mask, "k_level_mask"),
                             (c.score_mask, "k_score_mask"), (c.keep, "k_keep")):
                    sp.dma_start(t[:], d[s]).then_inc(loaded, 16)
                for tile, parts in zip(rows, lists):
                    at = 0
                    for part in parts:
                        n = part.shape[0]
                        sp.dma_start(tile[at:at + n, :], part).then_inc(loaded, 16)
                        at += n

            @block.tensor
            def _(pe):
                pe.wait_ge(loaded, 16 * n_loads)
                for n, m in enumerate(sizes):
                    pe.transpose(c.bank[n][:, 0:m], rows[n][0:m, :], c.ident[0:m, 0:m]).then_inc(turned, 1)

            @block.vector
            def _(dve):
                at = 0
                nc.vector.memset(c.ones[:], 1.0).then_inc(copied, 1)
                nc.vector.memset(c.eps[:, 0:1], 1e-6).then_inc(copied, 1)
                nc.vector.memset(c.eps[:, 1:2], 64e-5).then_inc(copied, 1)
                dve.wait_ge(turned, 3)
                for n, m in enumerate(sizes):
                    at += CT if n == 2 else 0
                    nc.vector.tensor_copy(c.par[:, at:at + m], c.bank[n][:, 0:m]).then_inc(copied, 1)
                    at += m
                dve.wait_ge(copied, 6)
                nc.vector.tensor_scalar(c.par[:, PLESS:PLESS + CT], c.par[:, PKA:PKA + CT], -1.0, 1.0, ALU.mult, ALU.add)\
                    .then_inc(copied, 1)

            @block.scalar
            def _(act):
                act.wait_ge(copied, 6)
                nc.scalar.activation(c.cond[:], c.par[:, PC:PC + 16], ACT.Silu).then_inc(gated, 1)


def modulation(c, d):
    nc = c.nc
    W = 512
    BLOCKS = 2 * 6 * D // W
    BODY = 6
    with ExitStack() as ctx:
        sb = lambda n, s, dt=F32: ctx.enter_context(nc.sbuf_tensor(n, s, dt))
        sem = lambda n: ctx.enter_context(nc.semaphore(n))
        raw = [sb(f"modw{s}", [P, CT, W]) for s in range(3)]
        hi, lo = ([sb(f"modw_{n}{s}", [P, CT, W], F32R) for s in range(2)] for n in ("hi", "lo"))
        cond, cond_hi = sb("cond_parts", [P, CT, 4], F32R), sb("cond_hi", [P, CT, 4], F32R)
        fold, zeros = sb("fold", [4, 2]), sb("zeros", [P, CT, 4])
        row = [sb(f"modrow{s}", [4, W]) for s in range(2)]
        loaded = [sem(f"modw_loaded{s}") for s in range(3)]
        rounded, rest, product, copied, turned, stored = (sem(f"mod_{n}") for n in (
            "rounded", "rest", "product", "row_copied", "turned", "stored"))
        gains, fold_loaded, parts = sem("norm_gains"), sem("fold_loaded"), sem("cond_parts")
        src = d["mod_w"].rearrange("l (k p) e -> l p k e", p=P)

        def blocks(eng, step):
            for j in range(BODY):
                step(j, 0, j)
            with eng.Fori(1, BLOCKS // BODY) as i:
                for j in range(BODY):
                    step(BODY * i + j, i, j)

        with nc.Block() as block:
            @block.sync
            def _(sp):
                sp.dma_start(fold[:], d["k_fold"]).then_inc(fold_loaded, 16)
                per = BLOCKS // 2
                for l in range(2):
                    def step(n, cols, j):
                        need(sp, rest, n - 2)
                        sp.dma_start(raw[j % 3][:], src[l][:, :, cols]).then_inc(loaded[j % 3], 16)

                    if l == 0:
                        for j in range(BODY):
                            step(j, slice(j * W, j * W + W), j)
                    with sp.Fori(1 - l, per // BODY) as i:
                        for j in range(BODY):
                            step(per * l + BODY * i + j, bass.ds((BODY * i + j) * W, W), j)

            @block.tensor
            def _(pe):
                def turn(n, s):
                    pe.wait_ge(copied, n + 1)
                    need(pe, stored, n - 1)
                    for q in range(4):
                        mm = pe.matmul(c.bank[2 + s][:, 2 * q:2 * q + 2], row[s][:, q * P:(q + 1) * P], fold[:],
                                       start=True, stop=True)
                    mm.then_inc(turned, 1)

                def step(n, i, j):
                    s = j % 2
                    pe.wait_ge(rest, n + 1)
                    need(pe, copied, n - 1)
                    for k in range(CT):
                        pe.matmul(c.bank[s][0:4, :], cond[:, k, :], hi[s][:, k, :], start=(k == 0), stop=False)
                        mm = pe.matmul(c.bank[s][0:4, :], cond_hi[:, k, :], lo[s][:, k, :], start=False, stop=(k == CT - 1))
                    mm.then_inc(product, 1)
                    if not isinstance(n, int) or n:
                        turn(n - 1, 1 - s)

                pe.wait_ge(fold_loaded, 16)
                pe.wait_ge(parts, 4)
                blocks(pe, step)
                turn(BLOCKS - 1, 1)

            @block.scalar
            def _(act):
                def copy(n, s):
                    act.wait_ge(product, n + 1)
                    need(act, turned, n - 1)
                    signal(act, nc.scalar.copy(row[s][:], c.bank[s][0:4, :]), copied, n + 1)

                def step(n, i, j):
                    s = j % 2
                    act.wait_ge(loaded[j % 3], 16 * (BODY // 3 * i + j // 3 + 1))
                    need(act, product, n - 1)
                    nc.scalar.copy(hi[s][:], raw[j % 3][:]).then_inc(rounded, 1)
                    if not isinstance(n, int) or n:
                        copy(n - 1, 1 - s)

                blocks(act, step)
                copy(BLOCKS - 1, 1)

            @block.vector
            def _(dve):
                v = nc.vector

                def finish(n, s):
                    dve.wait_ge(turned, n + 1)
                    mod = c.mod[:].rearrange("p l m r -> p (l m) r")
                    signal(dve, v.tensor_tensor(
                        mod[:, bass.ds(4 * n, 4), :], c.bank[2 + s][:, 0:8].rearrange("p (q r) -> p q r", r=2),
                        c.par[:, bass.ds(PMODB + 4 * n, 4)].unsqueeze(2).to_broadcast([P, 4, 2]), ALU.add), stored, n + 1)

                def step(n, i, j):
                    dve.wait_ge(rounded, n + 1)
                    v.tensor_tensor(lo[j % 2][:], raw[j % 3][:], hi[j % 2][:].bitcast(F32), ALU.subtract).then_inc(rest, 1)
                    if not isinstance(n, int) or n > 1:
                        finish(n - 2, j % 2)

                silu = c.cond[:].rearrange("p (r k) -> p k r", k=CT)
                signal(dve, v.memset(zeros[:], 0.0), parts, 1)
                v.tensor_copy(cond_hi[:], zeros[:]).then_inc(parts, 1)
                signal(dve, v.tensor_copy(cond[:, :, 0:2], silu), parts, 3)
                v.tensor_tensor(cond[:, :, 2:4], silu, cond[:, :, 0:2].bitcast(F32), ALU.subtract)
                signal(dve, v.tensor_copy(cond_hi[:, :, 0:2], silu), parts, 4)
                blocks(dve, step)
                finish(BLOCKS - 2, 0)
                finish(BLOCKS - 1, 1)
                n = 0
                for l in range(2):
                    for kind, base in ((0, PNM), (1, PNF)):
                        for r in range(2):
                            nc.vector.scalar_tensor_tensor(
                                c.gain[:, l, kind, r, :], c.mod[:, l, 24 * kind + 8:24 * kind + 16, r], 1.0,
                                c.par[:, base + 8 * l:base + 8 * l + 8], ALU.add, ALU.mult).then_inc(gains, 1)


def load_tokens(c, d, h, spilled):
    nc = c.nc
    T = TOK // P
    with ExitStack() as ctx:
        xt = ctx.enter_context(nc.sbuf_tensor("xt", [P, T, D], F32))
        loaded = ctx.enter_context(nc.semaphore("x_loaded"))
        turned = ctx.enter_context(nc.semaphore("x_turned"))
        lat_copied = ctx.enter_context(nc.semaphore("x_lat_copied"))
        ctx_copied = ctx.enter_context(nc.semaphore("x_ctx_copied"))
        with nc.Block() as block:
            @block.sync
            def _(sp):
                sp.dma_start(xt[:, 0:2, :], d["ctx"][0].rearrange("(t p) e -> p t e", p=P)).then_inc(loaded, 16)
                sp.dma_start(xt[:, 2:T, :], d["x"][0].rearrange("(t p) e -> p t e", p=P)).then_inc(loaded, 16)
                sp.wait_ge(lat_copied, CT)
                sp.wait_ge(ctx_copied, CT)
                sp.dma_start(spilled, h[:]).then_inc(c.spilled, 16)

            @block.tensor
            def _(pe):
                pe.wait_ge(loaded, 32)
                for k in range(CT):
                    s = 2 * (k % 2)
                    if k >= 2:
                        pe.wait_ge(lat_copied, k - 1)
                        pe.wait_ge(ctx_copied, k - 1)
                    for t in range(T):
                        out = c.bank[s][:, t * P:(t + 1) * P] if t < 2 else c.bank[s + 1][:, (t - 2) * P:(t - 1) * P]
                        mm = pe.transpose(out, xt[:, t, k * P:(k + 1) * P], c.ident[:])
                    mm.then_inc(turned, 1)

            @block.vector
            def _(dve):
                for k in range(CT):
                    dve.wait_ge(turned, k + 1)
                    nc.vector.tensor_copy(h[:, k, CTX:TOK], c.bank[2 * (k % 2) + 1][:, 0:LAT]).then_inc(lat_copied, 1)

            @block.scalar
            def _(act):
                for k in range(CT):
                    act.wait_ge(turned, k + 1)
                    nc.scalar.copy(h[:, k, 0:CTX], c.bank[2 * (k % 2)][:, 0:CTX]).then_inc(ctx_copied, 1)


def norm_whole(c, name, h, layer, kind, out, segs):
    nc = c.nc
    with ExitStack() as ctx:
        sb = lambda n, s: ctx.enter_context(nc.sbuf_tensor(f"{name}_{n}", s, F32))
        sem = lambda n: ctx.enter_context(nc.semaphore(f"{name}_{n}"))
        sq = sb("sq", [P, 2, TOK])
        std = sb("std", [P, TOK])
        scaled = sb("scaled", [P, 2, TOK])
        squared, summed, rooted, inverted, normed, written = (
            sem(n) for n in ("squared", "summed", "rooted", "inverted", "normed", "written"))
        lo = segs[0][0]
        banks = {CTX: c.bank[0], 0: c.bank[1]}
        with nc.Block() as block:
            @block.sync
            def _(sp):
                sp.wait_ge(c.spilled, 16)

            @block.tensor
            def _(pe):
                for k in range(CT):
                    pe.wait_ge(squared, k + 1)
                    for at, n in segs:
                        mm = pe.matmul(banks[at][:, 0:n], c.ones[:], sq[:, k % 2, at:at + n],
                                       start=(k == 0), stop=(k == CT - 1))
                    mm.then_inc(summed, 1)

            @block.scalar
            def _(act):
                for k in range(CT):
                    if k >= 2:
                        act.wait_ge(summed, k - 1)
                    nc.scalar.activation(sq[:, k % 2, lo:], h[:, k, lo:], ACT.Square).then_inc(squared, 1)
                    act.wait_ge(squared, k + 1)
                act.wait_ge(summed, CT)
                for at, n in segs:
                    nc.scalar.activation(std[:, at:at + n], banks[at][:, 0:n], ACT.Sqrt, scale=1.0 / D,
                                         bias=c.eps[:, 0:1]).then_inc(rooted, 1)
                for k in range(CT):
                    act.wait_ge(normed, k + 1)
                    for s, (at, n) in enumerate(segs):
                        r = 1 if at == 0 else 0
                        nc.scalar.activation(out(k, at, n), scaled[:, k % 2, at:at + n], ACT.Identity,
                                             scale=c.gain[:, layer, kind, r, k:k + 1],
                                             bias=c.mod[:, layer, 24 * kind + k, r:r + 1]).then_inc(written, 1)

            @block.vector
            def _(dve):
                dve.wait_ge(rooted, len(segs))
                signal(dve, nc.vector.reciprocal(std[:, lo:], std[:, lo:]), inverted, 1)
                for k in range(CT):
                    if k >= 2:
                        dve.wait_ge(written, len(segs) * (k - 1))
                    signal(dve, nc.vector.tensor_tensor(scaled[:, k % 2, lo:], h[:, k, lo:], std[:, lo:], ALU.mult),
                           normed, k + 1)


class Norm:

    def __init__(self, c, ctx, name, h, layer, kind, hi, lo, segs):
        sb = lambda n, s: ctx.enter_context(c.nc.sbuf_tensor(f"{name}_{n}", s, F32))
        self.c, self.h, self.layer, self.kind, self.hi, self.lo, self.segs = c, h, layer, kind, hi, lo, segs
        self.std, self.scaled = sb("std", [P, TOK]), sb("scaled", [P, 2, TOK])
        self.full = sb("full", [P, 2, TOK])
        (self.squared, self.summed, self.rooted, self.inverted, self.normed, self.written, self.rounded,
         self.rest) = c.norm_sems
        self.tiles, self.before = CT * c.norms, c.norm_segs
        c.norms, c.norm_segs = c.norms + 1, c.norm_segs + len(segs)
        self.number = c.norms
        self.at0 = segs[0][0]
        self.banks = {CTX: c.bank[6], 0: c.bank[7]}

    def ready(self, pe, k):
        pe.wait_ge(self.rest, self.tiles + k + 1)

    def sums(self, pe):
        for k in range(CT):
            pe.wait_ge(self.squared, self.tiles + k + 1)
            for at, n in self.segs:
                mm = pe.matmul(self.banks[at][:, 0:n], self.c.ones[:], self.full[:, k % 2, at:at + n],
                               start=(k == 0), stop=(k == CT - 1))
            mm.then_inc(self.summed, 1)

    def squares(self, act):
        for k in range(CT):
            if k >= 2:
                act.wait_ge(self.summed, self.tiles + k - 1)
            signal(act, act.activation(self.full[:, k % 2, self.at0:], self.h[:, k, self.at0:], ACT.Square),
                   self.squared, self.tiles + k + 1)

    def write(self, act):
        c, ns, at0 = self.c, len(self.segs), self.at0
        act.wait_ge(self.summed, self.tiles + CT)
        for at, n in self.segs:
            act.activation(self.std[:, at:at + n], self.banks[at][:, 0:n], ACT.Sqrt, scale=1.0 / D,
                           bias=c.eps[:, 0:1]).then_inc(self.rooted, 1)
        for k in range(CT):
            act.wait_ge(self.normed, self.tiles + k + 1)
            if k >= 2:
                act.wait_ge(self.rest, self.tiles + k - 1)
            for at, n in self.segs:
                r = 1 if at == 0 else 0
                act.activation(self.full[:, k % 2, at:at + n], self.scaled[:, k % 2, at:at + n], ACT.Identity,
                               scale=c.gain[:, self.layer, self.kind, r, k:k + 1],
                               bias=c.mod[:, self.layer, 24 * self.kind + k, r:r + 1]).then_inc(self.written, 1)
            act.wait_ge(self.written, CT * self.before + ns * (k + 1))
            act.copy(self.hi[:, k, at0:TOK], self.full[:, k % 2, at0:]).then_inc(self.rounded, 1)

    def scale(self, dve):
        ns, at0 = len(self.segs), self.at0

        def scale(k):
            if k >= 2:
                dve.wait_ge(self.written, CT * self.before + ns * (k - 1))
            dve.tensor_tensor(self.scaled[:, k % 2, at0:], self.h[:, k, at0:], self.std[:, at0:], ALU.mult)\
                .then_inc(self.normed, 1)

        dve.wait_ge(self.rooted, self.before + ns)
        signal(dve, dve.reciprocal(self.std[:, at0:], self.std[:, at0:]), self.inverted, self.number)
        scale(0)
        for k in range(CT):
            if k + 1 < CT:
                scale(k + 1)
            dve.wait_ge(self.rounded, self.tiles + k + 1)
            dve.tensor_tensor(self.lo[:, k, at0:TOK], self.full[:, k % 2, at0:], self.hi[:, k, at0:TOK].bitcast(F32),
                              ALU.subtract).then_inc(self.rest, 1)


class SplitWeights:

    def __init__(self, c, ctx, name, k_tiles):
        sb = lambda n, dt: [ctx.enter_context(c.nc.sbuf_tensor(f"{name}_{n}{s}", [P, k_tiles, P], dt)) for s in range(2)]
        sem = lambda n: ctx.enter_context(c.nc.semaphore(f"{name}_{n}"))
        self.nc = c.nc
        self.raw, self.hi, self.lo = sb("raw", F32), sb("hi", F32R), sb("lo", F32R)
        self.loaded = [sem("loaded0"), sem("loaded1")]
        self.rounded, self.rest, self.product = sem("rounded"), sem("rest"), sem("product")

    def load(self, sp, n, s, src):
        need(sp, self.rest, n - 1)
        sp.dma_start(self.raw[s][:, 0:src.shape[1], :], src).then_inc(self.loaded[s], 16)

    def round(self, act, n, s, pairs_before, k_tiles):
        act.wait_ge(self.loaded[s], 16 * (pairs_before + 1))
        need(act, self.product, n - 1)
        signal(act, self.nc.scalar.copy(self.hi[s][:, 0:k_tiles, :], self.raw[s][:, 0:k_tiles, :]), self.rounded, n + 1)

    def subtract(self, eng, n, s, k_tiles):
        eng.wait_ge(self.rounded, n + 1)
        signal(eng, eng.tensor_tensor(self.lo[s][:, 0:k_tiles, :], self.raw[s][:, 0:k_tiles, :],
                                                 self.hi[s][:, 0:k_tiles, :].bitcast(F32), ALU.subtract), self.rest, n + 1)


def three_passes(pe, out, w, x, first, last):
    pe.matmul(out, w[0], x[0], start=first, stop=False)
    pe.matmul(out, w[0], x[1], start=False, stop=False)
    return pe.matmul(out, w[1], x[0], start=False, stop=last)


def rwkv_inputs(c, d, a, xx, hidden, dram):
    nc = c.nc
    with ExitStack() as ctx:
        sb = lambda n, s, dt=F32: ctx.enter_context(nc.sbuf_tensor(n, s, dt))
        sem = lambda n: ctx.enter_context(nc.semaphore(n))
        w = SplitWeights(c, ctx, "proj", CT)
        mix_hi = [sb(f"mix_hi{s}", [P, CT, TOK], F32R) for s in range(2)]
        mix_lo = [sb(f"mix_lo{s}", [P, CT, TOK], F32R) for s in range(2)]
        full = [sb(f"mix_full{s}", [P, TOK]) for s in range(2)]
        out = [sb(f"proj_out{s}", [P, TOK]) for s in range(2)]
        shifted, mixed, mix_rounded, mix_rest = (sem(n) for n in ("shifted", "mixed", "mix_rounded", "mix_rest"))
        small_copied = sem("hidden_copied")
        evac_lat, evac_ctx, kept = sem("proj_lat_copied"), sem("proj_ctx_copied"), sem("rkv_stored")
        small = (d["rw_w1"][0].rearrange("e (k p) r -> p k e r", p=P),
                 d["rw_a1"][0].rearrange("e (k p) r -> p k e r", p=P),
                 d["rw_g1"][0].rearrange("(k p) r -> p k r", p=P))
        large = [d[n][0].rearrange("(k p) e -> p k e", p=P) for n in ("rw_wr", "rw_wk", "rw_wv")]
        MU = (0, 1, 2, 4, 3, 5)
        UNITS = 3 * (CT + 1)

        class Unit:

            def __init__(self, first, i=0):
                if isinstance(i, int):
                    first, i = first + 2 * i, 0
                self.i, self.n, self.s = i, first + 2 * i, first % 2
                self.loads = first // 2 + i + (1 if first >= (CT, 2 * CT + 1)[self.s] else 0)
                self.first = first

            def plus(self, n):
                return Unit(self.first + n, self.i)

        def schedule(E):
            E.split(Unit(0))
            for k in range(CT):
                E.mix(0, k, k % 2)
            for m in range(3):
                base = (CT + 1) * m

                def pair(i):
                    for s in range(2):
                        u = Unit(base + s, i)
                        E.load(u.plus(2))
                        E.split(u.plus(1))
                        E.mix(2 * m + 1, 2 * i + s, s)
                        E.product(u, 2 * m, 2 * i + s)
                        E.finish(u, m, 2 * i + s)

                pair(0)
                with E.eng.Fori(1, CT // 2 - 1) as i:
                    pair(i)
                pair(CT // 2 - 1)
                u = Unit(base + CT)
                E.load(u.plus(2))
                E.split(u.plus(1))
                E.product(u, 2 * m + 1, CT)
                if m < 2:
                    for k in range(CT):
                        E.mix(2 * m + 2, k, k % 2)
                E.finish_small(u, m)

        class Part:
            def nothing(self, *_):
                pass

            load = split = mix = product = finish = finish_small = nothing

        def column(t, k):
            return t[:, slice(k, k + 1) if isinstance(k, int) else bass.ds(k, 1), :].rearrange("p o t -> p (o t)")

        with nc.Block() as block:
            @block.sync
            def _(sp):
                class Sp(Part):
                    eng = sp

                    def load(self, u):
                        if isinstance(u.n, int) and u.n % (CT + 1) == CT and u.n < UNITS:
                            m = u.n // (CT + 1)
                            need(sp, w.rest, u.n - 1)
                            if m < 2:
                                for e in range(2):
                                    sp.dma_start(w.raw[u.s][:, :, 64 * e:64 * e + 64], small[m][:, :, e, :])\
                                        .then_inc(w.loaded[u.s], 16)
                            else:
                                sp.dma_start(w.raw[u.s][:], small[m]).then_inc(w.loaded[u.s], 16)
                        elif not isinstance(u.n, int) or u.n < UNITS:
                            m, tile = self.where(u)
                            cols = slice(tile * P, tile * P + P) if isinstance(tile, int) else bass.ds(tile * P, P)
                            w.load(sp, u.n, u.s, large[m][:, :, cols])

                    def where(self, u):
                        if isinstance(u.n, int):
                            return u.n // (CT + 1), u.n % (CT + 1)
                        m = (u.first - 2) // (CT + 1)
                        return m, u.n - m * (CT + 1)

                    def finish(self, u, m, tile):
                        sp.wait_ge(evac_lat, CT * m + tile + 1)
                        sp.wait_ge(evac_ctx, CT * m + tile + 1)
                        sp.dma_start(column(dram[m], tile), out[u.s][:]).then_inc(kept, 16)

                Sp().load(Unit(0))
                Sp().load(Unit(1))
                schedule(Sp())
                sp.wait_ge(kept, 16 * 3 * CT)

            @block.tensor
            def _(pe):
                class Pe(Part):
                    eng = pe

                    def product(self, u, q, tile):
                        pe.wait_ge(w.rest, u.n + 1)
                        m, static = q // 2, isinstance(tile, int)
                        if static and tile == 1:
                            need(pe, small_copied, 2 * m)
                        else:
                            done = CT * m + (0 if static and tile == 0 else tile - 1)
                            need(pe, evac_lat, done)
                            need(pe, evac_ctx, done)
                        first = static and tile in (0, CT)
                        for k in range(CT):
                            if first:
                                pe.wait_ge(mix_rest, CT * q + k + 1)
                            for b, (at, width) in enumerate(SEGS):
                                mm = three_passes(pe, c.bank[2 * u.s + b][:, 0:width], (w.hi[u.s][:, k, :], w.lo[u.s][:, k, :]),
                                                  (mix_hi[q % 2][:, k, at:at + width], mix_lo[q % 2][:, k, at:at + width]),
                                                  k == 0, k == CT - 1)
                        mm.then_inc(w.product, 1)

                schedule(Pe())

            @block.vector
            def _(dve):
                v = nc.vector
                for k in range(CT):
                    v.tensor_tensor(xx[:, k, 1:TOK - 1], a[:, k, 0:TOK - 2], a[:, k, 2:TOK], ALU.add).then_inc(shifted, 1)
                dve.wait_ge(shifted, CT)
                v.tensor_copy(xx[:, :, 0:CTX + 1:CTX], a[:, :, 1:CTX + 2:CTX]).then_inc(shifted, 1)
                v.tensor_copy(xx[:, :, CTX - 1:TOK:LAT], a[:, :, CTX - 2:TOK - 1:LAT]).then_inc(shifted, 1)
                dve.wait_ge(shifted, CT + 2)
                for k in range(CT):
                    v.scalar_tensor_tensor(xx[:, k, :], xx[:, k, :], 0.5, a[:, k, :], ALU.mult, ALU.subtract).then_inc(shifted, 1)
                dve.wait_ge(shifted, 2 * CT + 2)

                class Dve(Part):
                    eng = dve

                    def split(self, u):
                        if not isinstance(u.n, int) or u.n < UNITS:
                            w.subtract(dve, u.n, u.s, CT)

                    def mix(self, q, k, s):
                        if q in (2, 4) and isinstance(k, int) and k == 0:
                            dve.wait_ge(w.product, (CT + 1) * (q // 2) - 1)
                        m = CT * q + k
                        need(dve, mix_rest, m - 1)
                        signal(dve, v.scalar_tensor_tensor(full[s][:], column(xx, k), c.par[:, bass.ds(PMU + 8 * MU[q] + k, 1)],
                                                           column(a, k), ALU.mult, ALU.add), mixed, m + 1)

                    def finish(self, u, m, tile):
                        dve.wait_ge(w.product, u.n + 1)
                        need(dve, kept, 16 * (CT * m + tile - 1))
                        signal(dve, v.tensor_copy(out[u.s][:, CTX:TOK], c.bank[2 * u.s + 1][:, 0:LAT]), evac_lat,
                               CT * m + tile + 1)

                schedule(Dve())

            @block.scalar
            def _(act):
                class Act(Part):
                    eng = act

                    def split(self, u):
                        if not isinstance(u.n, int) or u.n < UNITS:
                            w.round(act, u.n, u.s, u.loads, CT)

                    def mix(self, q, k, s):
                        m = CT * q + k
                        act.wait_ge(mixed, m + 1)
                        signal(act, nc.scalar.copy(column(mix_hi[q % 2], k), full[s][:]), mix_rounded, m + 1)

                    def finish(self, u, m, tile):
                        act.wait_ge(w.product, u.n + 1)
                        need(act, kept, 16 * (CT * m + tile - 1))
                        signal(act, nc.scalar.copy(out[u.s][:, 0:CTX], c.bank[2 * u.s][:, 0:CTX]), evac_ctx,
                               CT * m + tile + 1)

                    def finish_small(self, u, m):
                        act.wait_ge(w.product, u.n + 1)
                        f = (ACT.Tanh, ACT.Copy, ACT.Sigmoid)[m]
                        nc.scalar.activation(hidden[:, m, CTX:TOK], c.bank[2 * u.s + 1][:, 0:LAT], f).then_inc(small_copied, 1)
                        nc.scalar.activation(hidden[:, m, 0:CTX], c.bank[2 * u.s][:, 0:CTX], f).then_inc(small_copied, 1)

                schedule(Act())

            @block.gpsimd
            def _(pool):
                class Pool(Part):
                    eng = pool

                    def mix(self, q, k, s):
                        m = CT * q + k
                        pool.wait_ge(mix_rounded, m + 1)
                        signal(pool, nc.gpsimd.tensor_tensor(column(mix_lo[q % 2], k), full[s][:],
                                                             column(mix_hi[q % 2], k).bitcast(F32), ALU.subtract), mix_rest, m + 1)

                schedule(Pool())


def half(h):
    return slice(CH * h, CH * h + CH)


NF, NR = 36, 13
F_SIDE, R_SIDE = 14, 4
DVE_STEPS = 50


def recurrence(c, d, dram, hidden, big):
    nc = c.nc
    with ExitStack() as ctx:
        sb = lambda n, s: ctx.enter_context(nc.sbuf_tensor(n, s, F32))
        sem = lambda n: ctx.enter_context(nc.semaphore(n))
        b_in = [[big[0][:, 2 * s + e, :] for e in range(2)] for s in range(2)]
        k_in = [[big[0][:, 4 + 2 * s + e, :] for e in range(2)] for s in range(2)]
        ar = [[big[1][:, 4 * s + 2 * e:4 * s + 2 * e + 2, :].rearrange("p a t -> p (a t)")
               for e in range(2)] for s in range(2)]
        y = [[big[2][:, 2 * s + e, :] for e in range(2)] for s in range(2)]
        gate = [big[2][:, 4 + s, :] for s in range(2)]
        bonus = [big[2][:, 6 + s, :] for s in range(2)]
        ar4 = [[t.rearrange("p (n k t) -> p n k t", k=2, t=CH) for t in a] for a in ar]
        ep = [[sb(f"ep{s}{e}", [P, NCH, CH + 1]) for e in range(2)] for s in range(2)]
        v_s = [sb(f"v_pair{s}", [P, TOK]) for s in range(2)]
        r_s, k_s = sb("r_pair", [P, TOK]), sb("k_pair", [P, TOK])
        cols = [sb(f"pair_params{s}", [P, 10]) for s in range(2)]
        W0, A0, KK, KA, RK, LG, LB, LESS = 0, 2, 4, 5, 6, 7, 8, 9
        lora_w = sb("lora_w", [P, 3, P])
        kk, tmp, ytmp, gated = sb("kk", [P, TOK]), sb("tmp", [P, TOK]), sb("ytmp", [P, TOK]), sb("gated", [P, TOK])
        sig_w = [sb(f"sig_w{e}", [P, TOK]) for e in range(2)]
        cum = [sb(f"cum{e}", [P, TOK]) for e in range(2)]
        bk = sb("bk", [P, 2, 4, P])
        vbd = sb("vbd", [P, 4, P])
        arbd = [sb(f"arbd{p}", [P, 4, 2, P]) for p in range(2)]
        sc = [sb(f"sc{p}", [P, 4, 4, P]) for p in range(2)]
        tok = [sb(f"tok{p}", [P, 3, 4, P]) for p in range(2)]
        inv_x = [sb(f"inverse{p}", [P, 2, 2, 2, P]) for p in range(2)]
        t_sb = sb("t_sb", [P, 2, 2, P])
        lvl = [sb(f"lvl{n}", [P, 2, 2, P]) for n in range(2)]
        rhs, u_sb, decayed = sb("rhs", [P, 2, P]), sb("u_sb", [P, 2, P]), sb("decayed", [P, 2, P])
        state = [sb(f"state{q}", [P, 2, P]) for q in range(2)]

        zeroed, slices, features, pair_done, stored = (sem(n) for n in (
            "zeroed", "slices_loaded", "features_done", "pair_done", "pair_stored"))
        f_ready, f_read = sem("side_bank_ready"), sem("side_bank_read")
        kk_raw, kk_sq, cumd, decays, kk_root, bonus_in = (sem(n) for n in (
            "kk_raw", "kk_squared", "decay_sums", "decays", "kk_root", "bonus_in"))
        y_in, y_sq = sem("y_summed_directions"), sem("y_squared")
        dve_order = sem("dve_order")
        bd_dve, bd_act, scores, masked = sem("bk_placed"), sem("ar_v_placed"), sem("scores"), sem("scores_masked")
        turned, tok_copied = sem("bkv_turned"), sem("bkv_copied")
        lvl_ready, t_ready, t_copied, x_ready, x_added = (sem(n) for n in (
            "level_masked", "t_product", "t_copied", "x_products", "x_added"))
        rhs_ready, rhs_copied, u_ready, u_copied = (sem(n) for n in ("rhs_ready", "rhs_copied", "u_ready", "u_copied"))
        s_decayed, s_ready, s_done = sem("state_decayed"), sem("state_products"), sem("state_done")
        y_ready, y_copied = sem("y_ready"), sem("y_copied")
        T_BANK, X_BANK = c.bank[0:2], c.bank[2:4]
        SC_BANK = (c.bank[4], T_BANK[0])
        TURN_BANK = (T_BANK[1], X_BANK[0], X_BANK[1])
        CHAIN, Y_BANK, SIDE = c.bank[5:8]
        pair4 = lambda t: t.rearrange("p (s t) -> p s t", t=P)

        def blocks(j):
            return j, (NB + 1 - j) % NB

        def chunks(tile):
            return tile.rearrange("p (n t) -> p n t", t=CH)

        def units(q):
            return ((0, q, q), (1, 2 + 1 - q, 1 - q))

        def chunk_end(s, e, n):
            at = CH if e == 0 else 0
            return ep[s][e][:, n, at:at + 1]

        class Pair:

            def __init__(self, at, s):
                self.at, self.s = at, s

            def plus(self, n):
                return Pair(self.at + n, (self.s + n) % 2)

        class Batch:

            def __init__(self, t, j):
                self.t, self.j, self.g, self.p = t, j, t.at * NB + j, j % 2

        def side_uses(t, readout):
            both = F_SIDE + R_SIDE
            if readout:
                return both * t.at + (F_SIDE if isinstance(t.at, int) and t.at == CT - 1 else 2 * F_SIDE)
            return 0 if isinstance(t.at, int) and t.at == 0 else both * t.at - R_SIDE

        def schedule(E):
            def slot(C, I, N, extra):
                if I:
                    E.score(I, 0), E.score(I, 1), E.turn(I, 0), E.turn(I, 1)
                E.rhs(C, 0), extra()
                if I:
                    E.turn(I, 2)
                E.u(C, 0), extra()
                if I:
                    E.level0(I)
                extra(), E.sy(C, 0), extra()
                if I:
                    E.level(I, 1)
                extra(), E.rhs(C, 1)
                if I:
                    E.level(I, 2)
                extra(), E.u(C, 1)
                if I:
                    E.level(I, 3)
                extra(), E.sy(C, 1), extra()
                if I:
                    E.level(I, 4)
                extra(), E.y_out(C)
                if N:
                    E.place_bk(N)
                if I:
                    E.level(I, 5)
                extra()
                if N:
                    E.place_arv(N)

            def body(t, first, last):
                if not first:
                    slot(Batch(t.plus(-1), NB - 1), Batch(t, 0), Batch(t, 1), lambda: None)
                count = [0]

                def extra():
                    n = count[0]
                    count[0] += 1
                    if first:
                        if n < NF:
                            E.feature(t.plus(1), n)
                    elif n < NR:
                        E.readout(t.plus(-1), n)
                    elif not last and n < NR + NF:
                        E.feature(t.plus(1), n - NR)

                for j in range(NB - 1):
                    after = Batch(t, j + 2) if j + 2 < NB else None if last else Batch(t.plus(1), 0)
                    slot(Batch(t, j), Batch(t, j + 1), after, extra)
                assert count[0] >= NR + NF

            for n in range(NF):
                E.feature(Pair(0, 0), n)
            I = Batch(Pair(0, 0), 0)
            E.place_bk(I), E.place_arv(I), E.score(I, 0), E.score(I, 1), E.turn(I, 0), E.turn(I, 1), E.turn(I, 2), E.level0(I)
            for n in range(1, LEVELS):
                E.level(I, n)
            E.place_bk(Batch(Pair(0, 0), 1)), E.place_arv(Batch(Pair(0, 0), 1))
            body(Pair(0, 0), True, False)
            with E.eng.Fori(0, CT // 2 - 1) as i:
                if E.order:
                    E.order.enter(i, E.per)
                body(Pair(2 * i + 1, 1), False, False)
                body(Pair(2 * i + 2, 0), False, False)
                if E.order:
                    E.order.leave(CT // 2 - 1)
            last = Pair(CT - 1, 1)
            body(last, False, True)
            slot(Batch(last, NB - 1), None, None, lambda: None)
            for n in range(NR):
                E.readout(last, n)

        class Part:
            order, per = None, 0

            def nothing(self, *_):
                pass

            place_bk = place_arv = score = turn = level0 = level = rhs = u = sy = y_out = feature = readout = nothing

        def map_piece(n):
            return (n - 1) // 2, SEGS[(n - 1) % 2]

        with nc.Block() as block:
            @block.sync
            def _(sp):
                def load(t, first):
                    at = t.at if isinstance(t.at, int) else None
                    one = bass.ds(t.at, 1) if at is None else slice(at, at + 1)
                    wide = bass.ds(t.at * P, P) if at is None else slice(at * P, at * P + P)
                    need(sp, bd_act, NB * t.at - NB)
                    if not first:
                        sp.wait_ge(features, t.at)
                    for dst, src in ((r_s, dram[0]), (k_s, dram[1]), (v_s[t.s], dram[2])):
                        sp.dma_start(dst[:], src[:, one, :].rearrange("p o t -> p (o t)")).then_inc(slices, 16)
                    sp.dma_start(lora_w[:, 0, :], d["rw_w2"][0].rearrange("e r n -> (e r) n")[:, wide]).then_inc(slices, 16)
                    sp.dma_start(lora_w[:, 1, :], d["rw_a2"][0].rearrange("e r n -> (e r) n")[:, wide]).then_inc(slices, 16)
                    sp.dma_start(lora_w[:, 2, :], d["rw_g2"][0][:, wide]).then_inc(slices, 16)

                def put(t):
                    one = slice(t.at, t.at + 1) if isinstance(t.at, int) else bass.ds(t.at, 1)
                    sp.wait_ge(pair_done, t.at + 2)
                    sp.dma_start(dram[3][:, one, :].rearrange("p o t -> p (o t)"), gated[:]).then_inc(stored, 16)

                load(Pair(0, 0), True)
                load(Pair(1, 1), False)
                with sp.Fori(0, CT // 2 - 1) as i:
                    for k in range(2):
                        load(Pair(2 * i + 2 + k, k), False)
                        put(Pair(2 * i + k, k))
                put(Pair(CT - 2, 0))
                put(Pair(CT - 1, 1))
                sp.wait_ge(stored, 16 * (CT + 1))

            @block.tensor
            def _(pe):
                class Pe(Part):
                    eng = pe

                    def score(self, I, s):
                        if s == 0:
                            pe.wait_ge(bd_dve, I.g + 1)
                            need(pe, masked, 2 * I.g - 1)
                        else:
                            need(pe, t_copied, 10 * I.g)
                        for e, b in enumerate(blocks(I.j)):
                            for n in range(2):
                                mm = pe.matmul(SC_BANK[s][:, 256 * e + 128 * n:256 * e + 128 * n + 128], bk[:, n, 2 * e + s, :],
                                               ar[I.t.s][e][:, (2 * b + s) * P:(2 * b + s + 1) * P], start=True, stop=True)
                        mm.then_inc(scores, 1)

                    def turn(self, I, n):
                        if n:
                            need(pe, x_added, 12 * I.g + n - 2)
                        if n == 2:
                            pe.wait_ge(bd_act, I.g + 1)
                        src = vbd if n == 2 else bk[:, n]
                        for u in range(4):
                            mm = pe.transpose(TURN_BANK[n][:, u * P:(u + 1) * P], src[:, u, :], c.ident[:])
                        mm.then_inc(turned, 1)

                    def level0(self, I):
                        for e in range(2):
                            pe.wait_ge(lvl_ready, 12 * I.g + e + 1)
                            pe.wait_ge(tok_copied, 3 * I.g + 2 + e)
                            for s in range(2):
                                mm = pe.matmul(X_BANK[e][:, s * P:(s + 1) * P], lvl[0][:, e, s, :], c.ident[:],
                                               start=True, stop=True)
                            mm.then_inc(x_ready, 1)

                    def level(self, I, n):
                        x = inv_x[I.p]
                        for e in range(2):
                            pe.wait_ge(lvl_ready, 12 * I.g + 2 * n + e + 1)
                            pe.wait_ge(x_added, 12 * I.g + 2 * n + e - 1)
                            need(pe, t_copied, 10 * I.g + 2 * n + e - 3)
                            if n == 1 and e == 0:
                                pe.wait_ge(masked, 2 * I.g + 2)
                            for s in range(2):
                                mm = pe.matmul(T_BANK[e][:, s * P:(s + 1) * P], lvl[n % 2][:, e, s, :], x[:, e, 0, s, :],
                                               start=True, stop=True)
                            mm.then_inc(t_ready, 1)
                        for e in range(2):
                            pe.wait_ge(t_copied, 10 * I.g + 2 * n + e - 1)
                            for s in range(2):
                                mm = pe.matmul(X_BANK[e][:, (2 + s) * P:(3 + s) * P], t_sb[:, e, s, :], x[:, e, 1, s, :],
                                               start=True, stop=True)
                                if n < LEVELS - 1:
                                    mm = pe.matmul(X_BANK[e][:, s * P:(s + 1) * P], x[:, e, 1, s, :], t_sb[:, e, s, :],
                                                   start=True, stop=True)
                            mm.then_inc(x_ready, 1)

                    def rhs(self, C, q):
                        pe.wait_ge(tok_copied, 3 * C.g + 3)
                        need(pe, s_done, 2 * (2 * C.g + q))
                        for e, u, s in units(q):
                            out = CHAIN[:, e * P:(e + 1) * P]
                            alone = C.j == q == 0
                            mm = pe.matmul(out, sc[C.p][:, u, 2, :], tok[C.p][:, 2, u, :], start=True, stop=alone)
                            if not alone:
                                mm = pe.matmul(out, arbd[C.p][:, u, 0, :], state[q][:, e, :], start=False, stop=True)
                        mm.then_inc(rhs_ready, 1)

                    def u(self, C, q):
                        pe.wait_ge(rhs_copied, 2 * C.g + q + 1)
                        pe.wait_ge(x_added, 12 * (C.g + 1))
                        for e, u, s in units(q):
                            mm = pe.matmul(CHAIN[:, 256 + e * P:256 + (e + 1) * P], inv_x[C.p][:, e, 1, s, :], rhs[:, e, :],
                                           start=True, stop=True)
                        mm.then_inc(u_ready, 1)

                    def sy(self, C, q):
                        pe.wait_ge(u_copied, 2 * C.g + q + 1)
                        for e, u, s in units(q):
                            out = CHAIN[:, e * P:(e + 1) * P]
                            pe.matmul(out, tok[C.p][:, 1, u, :], tok[C.p][:, 2, u, :], start=True, stop=False)
                            mm = pe.matmul(out, tok[C.p][:, 0, u, :], u_sb[:, e, :], start=False, stop=True)
                        mm.then_inc(s_ready, 1)
                        if q == 0:
                            need(pe, y_copied, C.g)
                        for e, u, s in units(q):
                            out = Y_BANK[:, u * P:(u + 1) * P]
                            alone = C.j == q == 0
                            pe.matmul(out, tok[C.p][:, 2, u, :], sc[C.p][:, u, 3, :], start=True, stop=False)
                            if not alone:
                                pe.matmul(out, state[q][:, e, :], arbd[C.p][:, u, 1, :], start=False, stop=False)
                            mm = pe.matmul(out, u_sb[:, e, :], sc[C.p][:, u, 1, :], start=False, stop=True)
                        mm.then_inc(y_ready, 1)

                    def use_side(self, n, lhs, src, seg):
                        need(pe, f_read, n)
                        pe.matmul(SIDE[:, 0:seg[1]], lhs, src[:, seg[0]:seg[0] + seg[1]], start=True, stop=True)\
                            .then_inc(f_ready, 1)

                    def feature(self, t, n):
                        base = side_uses(t, False)
                        if n == 1:
                            pe.wait_ge(slices, 96 * (t.at + 1))
                        if 1 <= n <= 10:
                            m, seg = map_piece(n)
                            rows = slice(64 * (m % 2), 64 * (m % 2) + 64) if m < 4 else slice(0, P)
                            self.use_side(base + n - 1, lora_w[rows, m // 2, :], hidden[rows, m // 2, :], seg)
                        if n in (11, 12):
                            pe.wait_ge(kk_sq, t.at + 1)
                            self.use_side(base + n - 1, c.ones_head[:], tmp, SEGS[n - 11])
                        if n in (26, 27):
                            pe.wait_ge(bonus_in, t.at + 1)
                            self.use_side(base + n - 14, c.ones_head[:], tmp, SEGS[n - 26])

                    def readout(self, t, n):
                        base = side_uses(t, True)
                        if n in (1, 2):
                            pe.wait_ge(y_in, t.at + 1)
                            self.use_side(base + n - 1, c.ones_head[:], y[t.s][0], SEGS[n - 1])
                        if n in (4, 5):
                            pe.wait_ge(y_sq, t.at + 1)
                            self.use_side(base + n - 2, c.ones_head[:], ytmp, SEGS[n - 4])

                pe.wait_ge(zeroed, 1)
                schedule(Pe())

            @block.vector
            def _(dve):
                v = nc.vector
                step = Order(dve, dve_order)

                class Dve(Part):
                    eng, order, per = dve, step, DVE_STEPS

                    def place_bk(self, I):
                        need(dve, turned, 3 * I.g - 1)
                        for n, src in enumerate((b_in, k_in)):
                            for e, b in enumerate(blocks(I.j)):
                                for h in range(2):
                                    ins = v.tensor_copy(bk[half(h), n, 2 * e:2 * e + 2, half(h)],
                                                        chunks(src[I.t.s][e][half(h), 2 * b * CH:2 * (b + 1) * CH]))
                        signal(dve, ins, bd_dve, I.g + 1)

                    def score(self, I, s):
                        dve.wait_ge(scores, 2 * I.g + s + 1)
                        if s == 0:
                            need(dve, y_ready, 2 * I.g - 2)
                        for h in range(2):
                            psum = SC_BANK[s][half(h), :].rearrange("p (e k t) -> p e k t", e=2, t=CH)
                            ins = v.tensor_tensor(sc[I.p][half(h), s:s + 3:2, :, half(h)], psum,
                                                  c.score_mask[half(h), :, :, :], ALU.mult)
                        signal(dve, ins, masked, 2 * I.g + s + 1)

                    def level0(self, I):
                        for e in range(2):
                            x = inv_x[I.p][:, e]
                            ident2 = c.ident[:].unsqueeze(1).to_broadcast([P, 2, P])
                            dve.wait_ge(lvl_ready, 12 * I.g + e + 1)
                            v.tensor_tensor(x[:, 1], lvl[0][:, e], ident2, ALU.add)
                            dve.wait_ge(x_ready, 12 * I.g + e + 1)
                            signal(dve, v.tensor_tensor(x[:, 0], pair4(X_BANK[e][:, 0:256]), ident2, ALU.add),
                                   x_added, 12 * I.g + e + 1)

                    def level(self, I, n):
                        for e in range(2):
                            x = inv_x[I.p][:, e].rearrange("p k s t -> p (k s t)")
                            lo = 256 if n == LEVELS - 1 else 0
                            dve.wait_ge(x_ready, 12 * I.g + 2 * n + e + 1)
                            signal(dve, v.tensor_tensor(x[:, lo:], X_BANK[e][:, lo:], x[:, lo:], ALU.add),
                                   x_added, 12 * I.g + 2 * n + e + 1)

                    def sy(self, C, q):
                        dve.wait_ge(s_ready, 2 * C.g + q + 1)
                        need(dve, y_ready, 2 * C.g + q)
                        for e, b in enumerate(blocks(C.j)):
                            m = 2 * C.j + q
                            end = chunk_end(C.t.s, e, 2 * b + (q if e == 0 else 1 - q))
                            psum = CHAIN[:, e * P:(e + 1) * P]
                            if m:
                                dve.wait_ge(s_decayed, 22 * C.t.at + 2 * m + e - 1)
                                ins = v.scalar_tensor_tensor(state[1 - q][:, e, :], psum, end, decayed[:, e, :],
                                                             ALU.mult, ALU.add)
                            else:
                                ins = v.tensor_scalar(state[1 - q][:, e, :], psum, end, None, ALU.mult)
                            signal(dve, ins, s_done, 2 * (2 * C.g + q) + e + 1)

                    def side_read(self, n, ins):
                        signal(dve, ins, f_read, n + 1)

                    def feature(self, t, n):
                        base, p = side_uses(t, False), cols[t.s]
                        col = lambda i: p[:, i:i + 1]
                        third = lambda i: slice(256 * i, 256 * i + 256)
                        if n == 0:
                            at = slice(t.at, t.at + 1) if isinstance(t.at, int) else bass.ds(t.at, 1)
                            step(v.tensor_copy(p[:], c.par[:, PW0:PW0 + 10 * CT].rearrange("p (n k) -> p n k", k=CT)
                                               [:, :, at].rearrange("p n k -> p (n k)")))
                            dve.wait_ge(slices, 96 * (t.at + 1))
                            signal(dve, v.tensor_scalar(kk[:], k_s[:], col(KK), None, ALU.mult), kk_raw, t.at + 1)
                        elif n == 4:
                            dve.wait_ge(f_read, base + 2)
                            signal(dve, v.tensor_tensor_scan(cum[0][:], c.keep[:], sig_w[0][:], 0.0, ALU.mult, ALU.add),
                                   cumd, 2 * t.at + 1)
                        elif n == 6:
                            dve.wait_ge(f_read, base + 4)
                            signal(dve, v.tensor_tensor_scan(cum[1][:, ::-1], c.keep[:], sig_w[1][:, ::-1], 0.0,
                                                             ALU.mult, ALU.add), cumd, 2 * t.at + 2)
                        elif n in (11, 12):
                            at, width = SEGS[n - 11]
                            dve.wait_ge(f_ready, base + n)
                            self.side_read(base + n - 1, v.tensor_scalar(tmp[:, at:at + width], SIDE[:, 0:width], 1e-24,
                                                                         None, ALU.max))
                        elif n in (13, 15):
                            e = (n - 13) // 2
                            dve.wait_ge(f_read, base + 8)
                            step(v.tensor_scalar(k_in[t.s][e], b_in[t.s][e], col(KA), col(LESS), ALU.mult, ALU.add))
                        elif n in (14, 16):
                            e = (n - 14) // 2
                            step(v.tensor_tensor(k_in[t.s][e], k_in[t.s][e], k_s[:], ALU.mult))
                        elif n in (18, 19, 20):
                            dve.wait_ge(kk_root, t.at + 1)
                            part = tmp[:, third(n - 18)]
                            step(v.reciprocal(part, part))
                        elif n == 21:
                            step(v.tensor_tensor(kk[:], kk[:], tmp[:], ALU.mult))
                        elif n in (22, 23):
                            step(v.tensor_tensor(b_in[t.s][n - 22], b_in[t.s][n - 22], kk[:], ALU.mult))
                        elif n == 24:
                            step(v.tensor_tensor(tmp[:], k_in[t.s][0], k_in[t.s][1], ALU.add))
                        elif n == 25:
                            signal(dve, v.scalar_tensor_tensor(tmp[:], tmp[:], col(RK), r_s[:], ALU.mult, ALU.mult),
                                   bonus_in, t.at + 1)
                        elif n in (26, 27):
                            at, width = SEGS[n - 26]
                            dve.wait_ge(f_ready, base + n - 13)
                            self.side_read(base + n - 14, v.tensor_tensor(bonus[t.s][:, at:at + width], SIDE[:, 0:width],
                                                                          v_s[t.s][:, at:at + width], ALU.mult))
                        elif n >= 28:
                            e = (n - 28) // 4
                            before, through = ((ep[t.s][0][:, :, 0:CH], ep[t.s][0][:, :, 1:]) if e == 0 else
                                               (ep[t.s][1][:, :, 1:], ep[t.s][1][:, :, 0:CH]))
                            dve.wait_ge(decays, 4 * t.at + 2 * e + 2)
                            out = ar4[t.s][e]
                            ins = (lambda: v.scalar_tensor_tensor(out[:, :, 0, :], chunks(kk[:]), -1.0, before, ALU.mult, ALU.mult),
                                   lambda: v.tensor_tensor(out[:, :, 1, :], chunks(r_s[:]), through, ALU.mult),
                                   lambda: v.tensor_tensor(b_in[t.s][e], b_in[t.s][e], sig_w[e][:], ALU.mult),
                                   lambda: v.tensor_tensor(k_in[t.s][e], k_in[t.s][e], sig_w[e][:], ALU.mult))[(n - 28) % 4]()
                            if n == NF - 1:
                                signal(dve, ins, features, t.at + 1)
                            else:
                                step(ins)

                    def readout(self, t, n):
                        base, p, out = side_uses(t, True), cols[t.s], y[t.s][0]
                        if n == 0:
                            dve.wait_ge(y_copied, NB * (t.at + 1))
                            signal(dve, v.tensor_tensor(out, out, y[t.s][1], ALU.add), y_in, t.at + 1)
                        elif n in (1, 2):
                            at, width = SEGS[n - 1]
                            dve.wait_ge(f_ready, base + n)
                            self.side_read(base + n - 1, v.scalar_tensor_tensor(out[:, at:at + width], SIDE[:, 0:width],
                                                                                -1.0 / CH, out[:, at:at + width],
                                                                                ALU.mult, ALU.add))
                        elif n in (6, 7, 8):
                            dve.wait_ge(f_read, base + 4)
                            part = ytmp[:, 256 * (n - 6):256 * (n - 5)]
                            step(v.reciprocal(part, part))
                        elif n == 9:
                            step(v.tensor_tensor(out, out, ytmp[:], ALU.mult))
                        elif n == 10:
                            step(v.tensor_scalar(out, out, p[:, LG:LG + 1], p[:, LB:LB + 1], ALU.mult, ALU.add))
                        elif n == 11:
                            step(v.tensor_tensor(out, out, bonus[t.s], ALU.add))
                        elif n == 12:
                            dve.wait_ge(stored, 16 * t.at + 16)
                            signal(dve, v.tensor_tensor(gated[:], out, gate[t.s], ALU.mult), pair_done, t.at + 2)

                for t in (bk, vbd, arbd[0], arbd[1], sc[0], sc[1]):
                    step(v.memset(t[:], 0.0))
                for s in range(2):
                    step(v.memset(ep[s][0][:, :, 0:1], 1.0))
                    step(v.memset(ep[s][1][:, :, CH:CH + 1], 1.0))
                signal(dve, v.memset(kk[:], 0.0), zeroed, 1)
                signal(dve, v.memset(gated[:], 0.0), pair_done, 1)
                v.memset(ytmp[:], 0.0).then_inc(stored, 16)
                dve.wait_ge(stored, 16)
                schedule(Dve())

            @block.scalar
            def _(act):
                a = nc.scalar

                class Act(Part):
                    eng = act

                    def place_arv(self, I):
                        need(act, turned, 3 * I.g)
                        need(act, y_ready, 2 * I.g - 2)
                        act.wait_ge(features, I.t.at + 1)
                        for e, b in enumerate(blocks(I.j)):
                            for h in range(2):
                                a.copy(arbd[I.p][half(h), 2 * e:2 * e + 2, :, half(h)],
                                       ar4[I.t.s][e][half(h), 2 * b:2 * b + 2, :, :])
                                ins = a.copy(vbd[half(h), 2 * e:2 * e + 2, half(h)],
                                             chunks(v_s[I.t.s][half(h), 2 * b * CH:2 * (b + 1) * CH]))
                        signal(act, ins, bd_act, I.g + 1)

                    def turn(self, I, n):
                        act.wait_ge(turned, 3 * I.g + n + 1)
                        signal(act, a.copy(tok[I.p][:, n], pair4(TURN_BANK[n][:, :])), tok_copied, 3 * I.g + n + 1)

                    def level(self, I, n):
                        for e in range(2):
                            act.wait_ge(t_ready, 10 * I.g + 2 * n + e - 1)
                            act.wait_ge(x_ready, 12 * I.g + 2 * n + e - 1)
                            signal(act, a.copy(t_sb[:, e], pair4(T_BANK[e][:, 0:256])), t_copied, 10 * I.g + 2 * n + e - 1)

                    def rhs(self, C, q):
                        act.wait_ge(rhs_ready, 2 * C.g + q + 1)
                        signal(act, a.copy(rhs[:], pair4(CHAIN[:, 0:256])), rhs_copied, 2 * C.g + q + 1)

                    def u(self, C, q):
                        act.wait_ge(u_ready, 2 * C.g + q + 1)
                        need(act, y_ready, 2 * C.g + q)
                        signal(act, a.copy(u_sb[:], pair4(CHAIN[:, 256:512])), u_copied, 2 * C.g + q + 1)

                    def y_out(self, C):
                        act.wait_ge(y_ready, 2 * C.g + 2)
                        if C.j == 0:
                            need(act, pair_done, C.t.at)
                        for e, b in enumerate(blocks(C.j)):
                            for h in range(2):
                                ins = a.copy(chunks(y[C.t.s][e][half(h), 2 * b * CH:2 * (b + 1) * CH]),
                                             pair4(Y_BANK[half(h), 256 * e:256 * e + 256])[:, :, half(h)])
                        signal(act, ins, y_copied, C.g + 1)

                    def side_read(self, n, ins):
                        signal(act, ins, f_read, n + 1)

                    def feature(self, t, n):
                        base = side_uses(t, False)
                        if n == 1:
                            act.wait_ge(kk_raw, t.at + 1)
                            signal(act, a.activation(tmp[:], kk[:], ACT.Square), kk_sq, t.at + 1)
                        if 1 <= n <= 10:
                            m, (at, width) = map_piece(n)
                            act.wait_ge(f_ready, base + n)
                            src = SIDE[:, 0:width]
                            if m < 4:
                                dst = (sig_w if m < 2 else b_in[t.s])[m % 2]
                                param = (W0 if m < 2 else A0) + m % 2
                                ins = a.activation(dst[:, at:at + width], src, ACT.Sigmoid, bias=cols[t.s][:, param:param + 1])
                            else:
                                ins = a.copy(gate[t.s][:, at:at + width], src)
                            self.side_read(base + n - 1, ins)
                        elif n in (13, 15):
                            e = (n - 13) // 2
                            act.wait_ge(cumd, 2 * t.at + e + 1)
                            through = ep[t.s][0][:, :, 1:] if e == 0 else ep[t.s][1][:, :, 0:CH]
                            signal(act, a.activation(through, chunks(cum[e][:]), ACT.Exp, scale=-DECAY),
                                   decays, 4 * t.at + 2 * e + 1)
                        elif n in (14, 16):
                            e = (n - 14) // 2
                            signal(act, a.activation(sig_w[e][:], cum[e][:], ACT.Exp, scale=DECAY),
                                   decays, 4 * t.at + 2 * e + 2)
                        elif n == 17:
                            act.wait_ge(f_read, base + 12)
                            signal(act, a.activation(tmp[:], tmp[:], ACT.Sqrt), kk_root, t.at + 1)

                    def readout(self, t, n):
                        base = side_uses(t, True)
                        if n == 3:
                            act.wait_ge(f_read, base + 2)
                            signal(act, a.activation(ytmp[:], y[t.s][0], ACT.Square), y_sq, t.at + 1)
                        elif n in (4, 5):
                            at, width = SEGS[n - 4]
                            act.wait_ge(f_ready, base + n - 1)
                            self.side_read(base + n - 2, a.activation(ytmp[:, at:at + width], SIDE[:, 0:width], ACT.Sqrt,
                                                                      scale=1.0 / CH, bias=c.eps[:, 1:2]))

                act.wait_ge(zeroed, 1)
                schedule(Act())

            @block.gpsimd
            def _(pool):
                class Pool(Part):
                    eng = pool

                    def cut(self, I, n):
                        if n == 0:
                            pool.wait_ge(masked, 2 * I.g + 2)
                        for e in range(2):
                            need(pool, x_ready, 12 * I.g + 2 * n + e - 3)
                            if n == 2:
                                pool.wait_ge(x_added, 12 * I.g + e + 1)
                            signal(pool, nc.gpsimd.tensor_tensor(
                                lvl[n % 2][:, e], sc[I.p][:, 2 * e:2 * e + 2, 0, :],
                                c.level_mask[:, n, e, :].unsqueeze(1).to_broadcast([P, 2, P]), ALU.mult),
                                lvl_ready, 12 * I.g + 2 * n + e + 1)

                    def level0(self, I):
                        self.cut(I, 0)
                        self.cut(I, 1)

                    def level(self, I, n):
                        if n < LEVELS - 1:
                            self.cut(I, n + 1)

                    def rhs(self, C, q):
                        m = 2 * C.j + q
                        if m == 0:
                            return
                        pool.wait_ge(s_done, 2 * (2 * C.g + q))
                        for e, b in enumerate(blocks(C.j)):
                            end = chunk_end(C.t.s, e, 2 * b + (q if e == 0 else 1 - q))
                            signal(pool, nc.gpsimd.tensor_tensor(decayed[:, e, :], state[q][:, e, :],
                                                                 end.to_broadcast([P, P]), ALU.mult),
                                   s_decayed, 22 * C.t.at + 2 * m + e - 1)

                schedule(Pool())



def dense(c, name, weight, hi, lo, segs, h, layer, gate_row, from_dram=None):
    nc = c.nc
    ns = len(segs)
    at0 = segs[0][0]
    with ExitStack() as ctx:
        w = SplitWeights(c, ctx, name, CT)
        added = ctx.enter_context(nc.semaphore(f"{name}_added"))
        if from_dram:
            x_hi, x_lo, h_loaded = (ctx.enter_context(nc.semaphore(f"{name}_{n}")) for n in (
                "rhs_rounded", "rhs_rest", "residual_loaded"))
            x_loaded = [ctx.enter_context(nc.semaphore(f"{name}_rhs_loaded{n}")) for n in range(2)]
            whole = ctx.enter_context(nc.sbuf_tensor(f"{name}_rhs", [P, CT, TOK], F32))
        view = weight.rearrange("(k p) e -> p k e", p=P)
        with nc.Block() as block:
            @block.sync
            def _(sp):
                def pair(i):
                    for s in range(2):
                        cols = slice(s * P, s * P + P) if isinstance(i, int) else bass.ds((2 * i + s) * P, P)
                        w.load(sp, 2 * i + s, s, view[:, :, cols])
                        if from_dram and isinstance(i, int):
                            part = slice(4 * s, 4 * s + 4)
                            sp.dma_start(whole[:, part, :], from_dram[0][:, part, :]).then_inc(x_loaded[s], 16)
                    if from_dram and isinstance(i, int):
                        sp.dma_start(h[:], from_dram[1]).then_inc(h_loaded, 16)

                by_two(sp, 0, CT // 2, pair)

            @block.tensor
            def _(pe):
                def pair(i):
                    for s in range(2):
                        n = 2 * i + s
                        pe.wait_ge(w.rest, n + 1)
                        need(pe, added, ns * (n - 1))
                        for k in range(CT):
                            if from_dram and isinstance(i, int) and s == 0:
                                pe.wait_ge(x_lo, k + 1)
                            for q, (at, width) in enumerate(segs):
                                mm = three_passes(pe, c.bank[2 * s + q][:, 0:width], (w.hi[s][:, k, :], w.lo[s][:, k, :]),
                                                  (hi[:, k, at:at + width], lo[:, k, at:at + width]),
                                                  k == 0, k == CT - 1)
                        mm.then_inc(w.product, 1)

                by_two(pe, 0, CT // 2, pair)

            @block.scalar
            def _(act):
                def pair(i):
                    for s in range(2):
                        w.round(act, 2 * i + s, s, i, CT)
                        if from_dram and isinstance(i, int):
                            act.wait_ge(x_loaded[s], 16)
                            for k in range(4 * s, 4 * s + 4):
                                signal(act, nc.scalar.copy(hi[:, k, at0:TOK], whole[:, k, at0:TOK]), x_hi, k + 1)

                by_two(act, 0, CT // 2, pair)

            @block.vector
            def _(dve):
                def add(m, s):
                    dve.wait_ge(w.product, m + 1)
                    for q, (at, width) in enumerate(segs):
                        r = 1 if at == 0 else 0
                        gate = c.mod[:, layer, :, r][:, bass.ds(gate_row + m, 1)]
                        signal(dve, nc.vector.scalar_tensor_tensor(
                            h[:, m, at:at + width], c.bank[2 * s + q][:, 0:width], gate, h[:, m, at:at + width],
                            ALU.mult, ALU.add), added, ns * m + q + 1)

                def pair(i):
                    for s in range(2):
                        w.subtract(dve, 2 * i + s, s, CT)
                        if from_dram and isinstance(i, int):
                            for k in range(4 * s, 4 * s + 4):
                                dve.wait_ge(x_hi, k + 1)
                                signal(dve, nc.vector.tensor_tensor(lo[:, k, at0:TOK], whole[:, k, at0:TOK],
                                                                    hi[:, k, at0:TOK].bitcast(F32), ALU.subtract), x_lo, k + 1)
                        if not isinstance(i, int):
                            add(2 * i + s - 2, s)

                if from_dram:
                    pair(0)
                    dve.wait_ge(h_loaded, 16)
                    by_two(dve, 1, CT // 2, pair)
                else:
                    by_two(dve, 0, CT // 2, pair)
                add(CT - 2, 0)
                add(CT - 1, 1)


def feed_forward(c, d, h, hi, lo, layer, segs):
    nc = c.nc
    name = f"ffn{layer}"
    ns = len(segs)
    HT = FT // 2
    UP, UNITS = 2 * HT, 2 * HT + CT
    at0 = segs[0][0]
    with ExitStack() as ctx:
        sb = lambda n, s: ctx.enter_context(nc.sbuf_tensor(f"{name}_{n}", s, F32))
        sem = lambda n: ctx.enter_context(nc.semaphore(f"{name}_{n}"))
        w = SplitWeights(c, ctx, name, HT)
        norm = Norm(c, ctx, f"norm_{name}", h, layer, 1, hi, lo, segs)
        g_hi, g_lo = (ctx.enter_context(nc.sbuf_tensor(f"{name}_{n}", [P, HT, TOK - at0], F32R)) for n in ("g_hi", "g_lo"))
        silu, prod = sb("silu", [P, TOK - at0]), sb("gated", [P, TOK - at0])
        activated, multiplied, g_rounded, g_rest, added = (sem(n) for n in (
            "activated", "multiplied", "g_rounded", "g_rest", "added"))
        up = [d[n][layer].rearrange("(k p) e -> p k e", p=P) for n in ("ff_w1", "ff_w3")]
        down = d["ff_w2"][layer].rearrange("(k p) e -> p k e", p=P)

        def halves(eng, tile, outputs):
            for half in range(2):
                tile(half, 0, 0)
                with eng.Fori(0, (HT - 1) // 2) as i:
                    tile(half, 2 * i + 1, 1)
                    tile(half, 2 * i + 2, 0)
                outputs(half, 0)
                with eng.Fori(1, CT // 2) as j:
                    outputs(half, j)

        with nc.Block() as block:
            @block.sync
            def _(sp):
                def tile(half, m, parity):
                    col = (half * HT + m) * P
                    cols = slice(col, col + P) if isinstance(m, int) else bass.ds(col, P)
                    for s in range(2):
                        w.load(sp, UNITS * half + 2 * m + s, s, up[s][:, :, cols])

                def outputs(half, j):
                    for s in range(2):
                        col = (2 * j + s) * P
                        cols = slice(col, col + P) if isinstance(j, int) else bass.ds(col, P)
                        w.load(sp, UNITS * half + UP + 2 * j + s, s, down[:, half * HT:(half + 1) * HT, cols])

                halves(sp, tile, outputs)

            @block.tensor
            def _(pe):
                def tile(half, m, parity):
                    for s in range(2):
                        pe.wait_ge(w.rest, UNITS * half + 2 * m + s + 1)
                        for k in range(CT):
                            if isinstance(m, int) and half == s == 0:
                                norm.ready(pe, k)
                            for q, (at, width) in enumerate(segs):
                                mm = three_passes(pe, c.bank[4 * parity + 2 * s + q][:, 0:width],
                                                  (w.hi[s][:, k, :], w.lo[s][:, k, :]),
                                                  (hi[:, k, at:at + width], lo[:, k, at:at + width]),
                                                  k == 0, k == CT - 1)
                        mm.then_inc(w.product, 1)

                def outputs(half, j):
                    for s in range(2):
                        pe.wait_ge(w.rest, UNITS * half + UP + 2 * j + s + 1)
                        if not isinstance(j, int):
                            pe.wait_ge(added, ns * (CT * half + 2 * j + s - 1))
                        for k in range(HT):
                            if isinstance(j, int) and s == 0 and k == HT - 2:
                                pe.wait_ge(g_rest, HT * half + HT - 1)
                            if isinstance(j, int) and s == 0 and k == HT - 1:
                                pe.wait_ge(g_rest, HT * half + HT)
                            for q, (at, width) in enumerate(segs):
                                g = slice(at - at0, at - at0 + width)
                                mm = three_passes(pe, c.bank[4 + 2 * s + q][:, 0:width],
                                                  (w.hi[s][:, k, :], w.lo[s][:, k, :]),
                                                  (g_hi[:, k, g], g_lo[:, k, g]), k == 0, k == HT - 1)
                        mm.then_inc(w.product, 1)

                norm.sums(pe)
                halves(pe, tile, outputs)

            @block.scalar
            def _(act):
                def finish(half, m, parity, s):
                    t = HT * half + m
                    if s == 0:
                        act.wait_ge(w.product, UNITS * half + 2 * m + 1)
                        for q, (at, width) in enumerate(segs):
                            ins = nc.scalar.activation(silu[:, at - at0:at - at0 + width],
                                                       c.bank[4 * parity + q][:, 0:width], ACT.Silu)
                        signal(act, ins, activated, t + 1)
                    else:
                        act.wait_ge(multiplied, t + 1)
                        at = bass.ds(m, 1) if not isinstance(m, int) else slice(m, m + 1)
                        signal(act, nc.scalar.copy(g_hi[:, at, :].rearrange("p o t -> p (o t)"), prod[:]),
                               g_rounded, t + 1)

                def tile(half, m, parity):
                    for s in range(2):
                        w.round(act, UNITS * half + 2 * m + s, s, UNITS // 2 * half + m, CT)
                        if not isinstance(m, int):
                            finish(half, m - 1, 1 - parity, s)
                        elif half == 0 and s == 1:
                            norm.write(act)

                def outputs(half, j):
                    for s in range(2):
                        w.round(act, UNITS * half + UP + 2 * j + s, s, UNITS // 2 * half + HT + j, HT)
                        if isinstance(j, int):
                            finish(half, HT - 1, 0, s)

                norm.squares(act)
                halves(act, tile, outputs)

            @block.vector
            def _(dve):
                def multiply(half, m, parity):
                    t = HT * half + m
                    dve.wait_ge(w.product, UNITS * half + 2 * m + 2)
                    dve.wait_ge(activated, t + 1)
                    for q, (at, width) in enumerate(segs):
                        g = slice(at - at0, at - at0 + width)
                        ins = nc.vector.tensor_tensor(prod[:, g], c.bank[4 * parity + 2 + q][:, 0:width], silu[:, g], ALU.mult)
                    signal(dve, ins, multiplied, t + 1)
                    dve.wait_ge(g_rounded, t + 1)
                    at = bass.ds(m, 1) if not isinstance(m, int) else slice(m, m + 1)
                    flat = lambda g: g[:, at, :].rearrange("p o t -> p (o t)")
                    signal(dve, nc.vector.tensor_tensor(flat(g_lo), prod[:], flat(g_hi).bitcast(F32), ALU.subtract),
                           g_rest, t + 1)

                def add(half, m, s):
                    dve.wait_ge(w.product, UNITS * half + UP + m + 1)
                    for q, (at, width) in enumerate(segs):
                        r = 1 if at == 0 else 0
                        gate = c.mod[:, layer, :, r][:, bass.ds(40 + m, 1)]
                        signal(dve, nc.vector.scalar_tensor_tensor(
                            h[:, m, at:at + width], c.bank[4 + 2 * s + q][:, 0:width], gate, h[:, m, at:at + width],
                            ALU.mult, ALU.add), added, ns * (CT * half + m) + q + 1)

                def tile(half, m, parity):
                    for s in range(2):
                        w.subtract(dve, UNITS * half + 2 * m + s, s, CT)
                        if isinstance(m, int):
                            if half:
                                add(0, CT - 2 + s, s)
                            elif s == 1:
                                norm.scale(dve)
                        elif s == 1:
                            multiply(half, m - 1, 1 - parity)

                def outputs(half, j):
                    for s in range(2):
                        w.subtract(dve, UNITS * half + UP + 2 * j + s, s, HT)
                        if not isinstance(j, int):
                            add(half, 2 * j - 2 + s, s)
                        elif s == 1:
                            multiply(half, HT - 1, 0)

                halves(dve, tile, outputs)
                for s in range(2):
                    add(1, CT - 2 + s, s)


def qkv(c, d, h, hi, lo, q, k, v):
    nc = c.nc
    NH = KV_HEADS + HEADS
    KVD = KV_HEADS * P
    with ExitStack() as ctx:
        sb = lambda n, s: ctx.enter_context(nc.sbuf_tensor(n, s, F32))
        sem = lambda n: ctx.enter_context(nc.semaphore(n))
        w = SplitWeights(c, ctx, "qk_w", CT)
        norm = Norm(c, ctx, "norm1", h, 1, 0, hi, lo, SEGS)
        wv = sb("wv", [P, CT, KVD])
        wv_hi, wv_lo = (ctx.enter_context(nc.sbuf_tensor(n, [P, CT, KVD], F32R)) for n in ("wv_hi", "wv_lo"))
        cos, sin, swap = sb("cos", [P, LAT]), sb("sin", [P, LAT]), sb("swap", [P, P])
        raw = [sb(f"qk_raw{s}", [P, TOK]) for s in range(2)]
        sq = [sb(f"qk_sq{s}", [P, TOK]) for s in range(2)]
        std, turned = sb("qk_std", [P, TOK]), sb("qk_turned", [P, LAT])
        tables, v_loaded, v_rounded, v_rest = sem("rope_loaded"), sem("wv_loaded"), sem("wv_rounded"), sem("wv_rest")
        v_product, v_copied = sem("v_product"), sem("v_copied")
        copied, squared, summed, rooted, normed, swapped, rotated, order_sem = (sem(n) for n in (
            "qk_copied", "qk_squared", "qk_summed", "qk_rooted", "qk_normed", "qk_swapped", "qk_rotated", "qk_dve_order"))
        wk = d["at_wk"][0].rearrange("(k p) e -> p k e", p=P)
        wq = d["at_wq"][0].rearrange("(k p) e -> p k e", p=P)

        def segs_of(n):
            return SEGS if isinstance(n, int) and n < KV_HEADS else SEGS[1:]

        def steps(eng, step, order=None):
            for n in range(4):
                step(n, n % 2)
            with eng.Fori(2, NH // 2 - 1) as i:
                if order:
                    order.enter(i - 2, 6)
                for s in range(2):
                    step(2 * i + s, s, i)
                if order:
                    order.leave(NH // 2 - 3)
            for n in range(NH - 2, NH + 2):
                step(n, n % 2)

        def pair_of(n, s, i):
            return (n + 1) // 2 if isinstance(n, int) else i + s

        def there(n):
            return not isinstance(n, int) or 0 <= n < NH

        with nc.Block() as block:
            @block.sync
            def _(sp):
                sp.dma_start(wv[:], d["at_wv"][0].rearrange("(k p) e -> p k e", p=P)).then_inc(v_loaded, 16)
                for s in range(2):
                    w.load(sp, s, s, wk[:, :, s * P:(s + 1) * P])
                for t, s in ((cos, "k_cos"), (sin, "k_sin"), (swap, "k_swap")):
                    sp.dma_start(t[:], d[s]).then_inc(tables, 16)
                with sp.Fori(0, HEADS // 2) as i:
                    for s in range(2):
                        w.load(sp, 2 * i + s + KV_HEADS, s, wq[:, :, bass.ds((2 * i + s) * P, P)])

            @block.tensor
            def _(pe):
                norm.sums(pe)
                pe.wait_ge(v_rest, 1)
                for t in range(TOK // P):
                    if t >= 2:
                        pe.wait_ge(v_copied, t - 1)
                    at = slice(t * P, (t + 1) * P)
                    for kt in range(CT):
                        if t == 0:
                            norm.ready(pe, kt)
                        mm = three_passes(pe, c.bank[6 + t % 2][:, 0:KVD],
                                          (hi[:, kt, at], lo[:, kt, at]),
                                          (wv_hi[:, kt, :], wv_lo[:, kt, :]), kt == 0, kt == CT - 1)
                    mm.then_inc(v_product, 1)
                pe.wait_ge(v_copied, TOK // P)

                def step(n, s, i=None):
                    if there(n):
                        pe.wait_ge(w.rest, n + 1)
                        need(pe, copied, n - 1)
                        for kt in range(CT):
                            for at, width in segs_of(n):
                                mm = three_passes(pe, c.bank[2 * s + (at > 0)][:, 0:width], (w.hi[s][:, kt, :], w.lo[s][:, kt, :]),
                                                  (hi[:, kt, at:at + width], lo[:, kt, at:at + width]),
                                                  kt == 0, kt == CT - 1)
                        mm.then_inc(w.product, 1)
                    if there(n - 1):
                        pe.wait_ge(squared, n)
                        need(pe, rooted, n - 1)
                        for at, width in segs_of(n - 1):
                            mm = pe.matmul(c.bank[5 + (at > 0)][:, 0:width], c.ones[:], sq[1 - s][:, at:at + width],
                                           start=True, stop=True)
                        mm.then_inc(summed, 1)
                    if there(n - 2):
                        if isinstance(n, int) and n == KV_HEADS:
                            pe.wait_ge(tables, 48)
                        pe.wait_ge(normed, n - 1)
                        need(pe, rotated, n - 2)
                        pe.matmul(c.bank[4][:, 0:LAT], swap[:], raw[s][:, CTX:TOK], start=True, stop=True)\
                            .then_inc(swapped, 1)

                steps(pe, step)

            @block.scalar
            def _(act):
                norm.squares(act)
                act.wait_ge(v_loaded, 16)
                nc.scalar.copy(wv_hi[:], wv[:]).then_inc(v_rounded, 1)
                w.round(act, 0, 0, 0, CT)
                norm.write(act)
                for t in range(TOK // P):
                    act.wait_ge(v_product, t + 1)
                    signal(act, nc.scalar.copy(v[:, t, :], c.bank[6 + t % 2][:, 0:KVD]), v_copied, t + 1)

                def step(n, s, i=None):
                    if not isinstance(n, int) or n + 1 < NH:
                        w.round(act, n + 1, 1 - s, pair_of(n, s, i), CT)
                    if there(n - 1):
                        act.wait_ge(summed, n)
                        need(act, normed, n - 1)
                        for at, width in segs_of(n - 1):
                            ins = nc.scalar.activation(std[:, at:at + width], c.bank[5 + (at > 0)][:, 0:width], ACT.Sqrt,
                                                       scale=1.0 / P, bias=c.eps[:, 0:1])
                        ins.then_inc(rooted, 1)
                    if there(n):
                        act.wait_ge(w.product, n + 1)
                        need(act, rotated, n - 1)
                        need(act, summed, n - 1)
                        for at, width in segs_of(n):
                            ins = nc.scalar.copy(raw[s][:, at:at + width], c.bank[2 * s + (at > 0)][:, 0:width])
                        signal(act, ins, copied, n + 1)
                        at = segs_of(n)[0][0]
                        nc.scalar.activation(sq[s][:, at:], raw[s][:, at:], ACT.Square).then_inc(squared, 1)

                steps(act, step)

            @block.gpsimd
            def _(pool):
                pool.wait_ge(v_rounded, 1)
                signal(pool, nc.gpsimd.tensor_tensor(wv_lo[:], wv[:], wv_hi[:].bitcast(F32), ALU.subtract), v_rest, 1)
                w.subtract(pool, 0, 0, CT)

                def step(n, s, i=None):
                    if not isinstance(n, int) or n + 1 < NH:
                        w.subtract(pool, n + 1, 1 - s, CT)

                steps(pool, step)

            @block.vector
            def _(dve):
                order = Order(dve, order_sem)
                v_ = nc.vector

                def step(n, s, i=None):
                    if there(n - 2):
                        head = n - 2
                        x = raw[s]
                        order(v_.tensor_tensor(turned[:], x[:, CTX:TOK], cos[:], ALU.mult))
                        dve.wait_ge(swapped, n - 1)
                        if isinstance(n, int) and head < KV_HEADS:
                            o = k[:, head, CTX:TOK]
                            order(v_.tensor_copy(k[:, head, 0:CTX], x[:, 0:CTX]))
                        else:
                            at = head - KV_HEADS
                            at = slice(at, at + 1) if isinstance(n, int) else bass.ds(at, 1)
                            o = q[:, at, :].rearrange("p o t -> p (o t)")
                        order(v_.tensor_tensor(o, c.bank[4][:, 0:LAT], sin[:], ALU.mult))
                        signal(dve, v_.tensor_tensor(o, o, turned[:], ALU.add), rotated, n - 1)
                    if there(n - 1):
                        at = segs_of(n - 1)[0][0]
                        gain = PGK if at == 0 else PGQ
                        dve.wait_ge(rooted, n)
                        order(v_.reciprocal(std[:, at:], std[:, at:]))
                        x = raw[1 - s]
                        signal(dve, v_.scalar_tensor_tensor(x[:, at:], x[:, at:], c.par[:, gain:gain + 1], std[:, at:],
                                                            ALU.mult, ALU.mult), normed, n)

                norm.scale(dve)
                steps(dve, step, order)


def attend(c, q, k, v, o_hi, o_lo):
    nc = c.nc
    QT = LAT // P
    T = TOK // P
    SCALE = float(P) ** -0.5
    G = HEADS // KV_HEADS
    with ExitStack() as ctx:
        sb = lambda n, s: ctx.enter_context(nc.sbuf_tensor(n, s, F32))
        sem = lambda n: ctx.enter_context(nc.semaphore(n))
        qh = sb("qh", [P, LAT])
        prob = [sb(f"prob{s}", [P, TOK]) for s in range(2)]
        pt = sb("prob_t", [P, T, LAT])
        mx, nmx, den, rec = sb("mx", [P, 2, 2]), sb("nmx", [P, 2]), sb("den", [P, 2, 2]), sb("rec", [P, 2])
        q_placed, scored, maxed, expd, scaled, turned, copied_a, copied_b, out_ready, out_rounded, out_rest, order = (
            sem(n) for n in ("q_placed", "scored", "maxed", "exponentials", "prob_scaled", "prob_turned",
                             "prob_copied_act", "prob_copied_dve", "out_ready", "out_rounded", "out_rest", "att_order"))

        def one(t, h):
            return t[:, slice(h, h + 1) if isinstance(h, int) else bass.ds(h, 1), :].rearrange("p o t -> p (o t)")

        with nc.Block() as block:
            def heads(eng, body, step=None):
                for kv in range(KV_HEADS):
                    body(G * kv, kv)
                    with eng.Fori(G * kv + 1, G * kv + G) as h:
                        if step:
                            step.enter(h - (G * kv + 1), 4 * QT)
                        body(h, kv)
                        if step:
                            step.leave(G - 1)

            @block.tensor
            def _(pe):
                def turn(n, t):
                    pe.wait_ge(scaled, n + 1)
                    need(pe, copied_a, n)
                    need(pe, copied_b, n)
                    for s in range(T):
                        out = c.bank[4][:, s * P:(s + 1) * P] if s < 4 else c.bank[5][:, (s - 4) * P:(s - 3) * P]
                        mm = pe.transpose(out, prob[t % 2][:, s * P:(s + 1) * P], c.ident[:])
                    mm.then_inc(turned, 1)

                def values(h, kv):
                    pe.wait_ge(copied_a, QT * (h + 1))
                    pe.wait_ge(copied_b, QT * (h + 1))
                    need(pe, out_rest, h)
                    for s in range(T):
                        mm = pe.matmul(c.bank[6][:, 0:LAT], v[:, s, kv * P:(kv + 1) * P], pt[:, s, :],
                                       start=(s == 0), stop=(s == T - 1))
                    mm.then_inc(out_ready, 1)

                def body(h, kv):
                    first = isinstance(h, int) and h == 0
                    before = kv - 1 if isinstance(h, int) else kv
                    pe.wait_ge(q_placed, h + 1)
                    for t in range(QT):
                        n = QT * h + t
                        s = 2 * (t % 2)
                        if not (first and t < 2):
                            pe.wait_ge(expd, 2 * (n - 1))
                        pe.matmul(c.bank[s][:, 0:CTX], qh[:, t * P:(t + 1) * P], k[:, kv, 0:CTX], start=True, stop=True)
                        pe.matmul(c.bank[s + 1][:, 0:LAT], qh[:, t * P:(t + 1) * P], k[:, kv, CTX:TOK],
                                  start=True, stop=True).then_inc(scored, 1)
                        if t == 2 and not first:
                            values(h - 1, before)
                        if not (first and t < 2):
                            turn(n - 2, t)

                heads(pe, body)
                last = QT * HEADS
                turn(last - 2, 0)
                turn(last - 1, 1)
                values(HEADS - 1, KV_HEADS - 1)

            @block.scalar
            def _(act):
                def copy(n, t):
                    act.wait_ge(turned, n + 1)
                    signal(act, nc.scalar.copy(pt[:, 4:T, t * P:(t + 1) * P],
                                               c.bank[5][:, 0:256].rearrange("p (s t) -> p s t", t=P)), copied_a, n + 1)

                def output(h):
                    act.wait_ge(out_ready, h + 1)
                    signal(act, nc.scalar.copy(one(o_hi, h), c.bank[6][:, 0:LAT]), out_rounded, h + 1)

                def body(h, kv):
                    first = isinstance(h, int) and h == 0
                    for t in range(QT):
                        n = QT * h + t
                        act.wait_ge(maxed, n + 1)
                        if not (first and t < 2):
                            act.wait_ge(turned, n - 1)
                        for b, (at, width) in enumerate(SEGS):
                            signal(act, nc.scalar.activation(prob[t % 2][:, at:at + width], c.bank[2 * (t % 2) + b][:, 0:width],
                                                             ACT.Exp, scale=SCALE, bias=nmx[:, t % 2:t % 2 + 1],
                                                             accum_out=den[:, t % 2, b:b + 1]), expd, 2 * n + b + 1)
                        if t == 2 and not first:
                            output(h - 1)
                        if not (first and t < 2):
                            copy(n - 2, (t + 2) % 4)

                heads(act, body)
                copy(QT * HEADS - 2, 2)
                copy(QT * HEADS - 1, 3)
                output(HEADS - 1)

            @block.gpsimd
            def _(pool):
                def body(h, kv):
                    need(pool, scored, QT * h)
                    signal(pool, nc.gpsimd.tensor_copy(qh[:], one(q, h)), q_placed, h + 1)

                heads(pool, body)

            @block.vector
            def _(dve):
                step = Order(dve, order)
                v_ = nc.vector

                def scale(n, t):
                    dve.wait_ge(expd, 2 * (n + 1))
                    s = t % 2
                    step(v_.tensor_tensor(rec[:, s:s + 1], den[:, s, 0:1], den[:, s, 1:2], ALU.add))
                    step(v_.reciprocal(rec[:, s:s + 1], rec[:, s:s + 1]))
                    signal(dve, v_.tensor_scalar(prob[s][:], prob[s][:], rec[:, s:s + 1], None, ALU.mult), scaled, n + 1)

                def copy(n, t):
                    dve.wait_ge(turned, n + 1)
                    signal(dve, v_.tensor_copy(pt[:, 0:4, t * P:(t + 1) * P],
                                               c.bank[4][:].rearrange("p (s t) -> p s t", t=P)), copied_b, n + 1)

                def rest(h):
                    dve.wait_ge(out_rounded, h + 1)
                    signal(dve, v_.tensor_tensor(one(o_lo, h), c.bank[6][:, 0:LAT], one(o_hi, h).bitcast(F32),
                                                 ALU.subtract), out_rest, h + 1)

                def body(h, kv):
                    first = isinstance(h, int) and h == 0
                    for t in range(QT):
                        n = QT * h + t
                        dve.wait_ge(scored, n + 1)
                        for b, (at, width) in enumerate(SEGS):
                            step(v_.tensor_reduce(mx[:, t % 2, b:b + 1], c.bank[2 * (t % 2) + b][:, 0:width], AX, ALU.max))
                        signal(dve, v_.tensor_scalar(nmx[:, t % 2:t % 2 + 1], mx[:, t % 2, 0:1], mx[:, t % 2, 1:2], -SCALE,
                                                     ALU.max, ALU.mult), maxed, n + 1)
                        if not (first and t == 0):
                            scale(n - 1, t + 1)
                        if t == 2 and not first:
                            rest(h - 1)
                        if not (first and t < 2):
                            copy(n - 2, (t + 2) % 4)

                heads(dve, body, step)
                last = QT * HEADS
                scale(last - 1, 1)
                copy(last - 2, 2)
                copy(last - 1, 3)
                rest(HEADS - 1)


def store(c, h, out):
    nc = c.nc
    T = LAT // P
    with ExitStack() as ctx:
        y = ctx.enter_context(nc.sbuf_tensor("y_rows", [P, T, D], F32))
        turned, copied, stored = (ctx.enter_context(nc.semaphore(n)) for n in ("out_turned", "out_turned_copied", "stored"))
        rows = out[0].rearrange("(t p) e -> t p e", p=P)
        with nc.Block() as block:
            @block.tensor
            def _(pe):
                for t in range(T):
                    for q in range(2):
                        n = 2 * t + q
                        if n >= 4:
                            pe.wait_ge(copied, n - 3)
                        for k in range(4):
                            mm = pe.transpose(c.bank[n % 4][:, k * P:(k + 1) * P],
                                              h[:, 4 * q + k, CTX + t * P:CTX + (t + 1) * P], c.ident[:])
                        mm.then_inc(turned, 1)

            @block.vector
            def _(dve):
                for n in range(2 * T):
                    dve.wait_ge(turned, n + 1)
                    nc.vector.tensor_copy(y[:, n // 2, 512 * (n % 2):512 * (n % 2) + 512], c.bank[n % 4][:])\
                        .then_inc(copied, 1)

            @block.sync
            def _(sp):
                for t in range(T):
                    sp.wait_ge(copied, 2 * t + 2)
                    sp.dma_start(rows[t], y[:, t, :]).then_inc(stored, 16)
                sp.wait_ge(stored, 16 * T)


def backbone(nc, d, out):
    with ExitStack() as ctx:
        c = Core(nc, ctx)
        c.bank = [ctx.enter_context(nc.psum_tensor(f"bank{n}", [P, 512], F32)) for n in range(8)]
        c.ident, c.ones_head, c.ones = c.sb("ident", [P, P]), c.sb("ones_head", [P, P]), c.sb("ones", [P, P])
        c.level_mask = c.sb("level_mask", [P, LEVELS, 2, P])
        c.score_mask = c.sb("score_mask", [P, 2, 4, CH])
        c.keep = c.sb("keep", [P, TOK])
        c.par, c.mod, c.gain = c.sb("par", [P, NPAR]), c.sb("mod", [P, 2, 48, 2]), c.sb("gain", [P, 2, 2, 2, CT])
        c.cond, c.eps = c.sb("cond", [P, 16]), c.sb("eps", [P, 2])
        rkv_dram = [nc.dram_tensor(n, [P, CT, TOK], F32, kind="Internal").ap() for n in ("r_all", "k_all", "v_all", "mixed_all")]
        spill = nc.dram_tensor("residual", [P, CT, TOK], F32, kind="Internal").ap()
        both, latent = SEGS, SEGS[1:]
        c.spilled = c.sem("tokens_spilled")
        c.norms, c.norm_segs = 0, 0
        c.norm_sems = [c.sem(f"norm_{n}") for n in (
            "squared", "summed", "rooted", "inverted", "normed", "written", "rounded", "rest")]

        setup(c, d)
        modulation(c, d)
        wide = lambda n, dt=F32: nc.sbuf_tensor(n, [P, CT, TOK], dt)

        with wide("shift_then_f") as xx, wide("normed_then_y") as a, nc.sbuf_tensor("hidden", [P, 3, TOK], F32) as hidden:
            with wide("tokens_in") as x:
                load_tokens(c, d, x, spill)
                norm_whole(c, "norm0", x, 0, 0, lambda k, at, n: a[:, k, at:at + n], both)
            rwkv_inputs(c, d, a, xx, hidden, rkv_dram)
            with wide("b_and_k") as bk:
                recurrence(c, d, rkv_dram, hidden, (bk, xx, a))
        h = c.sb("residual_stream", [P, CT, TOK])
        with wide("operand_hi", F32R) as hi, wide("operand_lo", F32R) as lo:
            dense(c, "rwkv_out", d["rw_wo"][0], hi, lo, both, h, 0, 16, from_dram=(rkv_dram[3], spill))
            feed_forward(c, d, h, hi, lo, 0, both)

            with nc.sbuf_tensor("q_heads", [P, HEADS, LAT], F32) as q, nc.sbuf_tensor("k_heads", [P, KV_HEADS, TOK], F32) as k, \
                    nc.sbuf_tensor("v_rows", [P, TOK // P, KV_HEADS * P], F32) as v:
                qkv(c, d, h, hi, lo, q, k, v)
                attend(c, q, k, v, hi[:, :, CTX:TOK], lo[:, :, CTX:TOK])
            dense(c, "att_out", d["at_wo"][0], hi, lo, latent, h, 1, 16)
            feed_forward(c, d, h, hi, lo, 1, latent)
        store(c, h, out)


_INS = ["x", "c", "ctx", "c_ctx", "mod_w", "mod_b", "norm_mix", "norm_ffn", "ff_w1", "ff_w3", "ff_w2", "rw_mu", "rw_wr",
        "rw_wk", "rw_wv", "rw_wo", "rw_w0", "rw_w1", "rw_w2", "rw_a0", "rw_a1", "rw_a2", "rw_g1", "rw_g2", "rw_kk",
        "rw_ka", "rw_rk", "rw_lnx_g", "rw_lnx_b", "at_wq", "at_wk", "at_wv", "at_wo", "at_gq", "at_gk"]


def shape_tables():
    f = np.float32
    i, j = np.indices((P, P))
    level = np.zeros((P, LEVELS, 2, P), f)
    for n in range(LEVELS):
        same = (i >> (n + 1)) == (j >> (n + 1))
        first_i, first_j = (i >> n) & 1 == 0, (j >> n) & 1 == 0
        level[:, n, 0, :] = same & first_i & ~first_j
        level[:, n, 1, :] = same & ~first_i & first_j
    s, t = np.arange(P)[:, None] % CH, np.arange(CH)[None, :]
    score = np.stack([np.stack([m1, m2, m1, m2], 1) for m1, m2 in ((s < t, s <= t), (s > t, s >= t))], 1).astype(f)
    keep = np.broadcast_to(np.arange(TOK) % CH != 0, (P, TOK)).astype(f)
    tok = np.arange(LAT)
    inv = f(10000.0) ** (-np.arange(0, P // 2, 2, dtype=f) / f(P // 2))
    ang = np.concatenate([(tok // 64).astype(f)[:, None] * inv, (tok % 64).astype(f)[:, None] * inv], 1)
    pair = np.arange(P) // 2
    sign = np.where(np.arange(P) % 2 == 0, -1.0, 1.0)[:, None]
    return {
        "k_ident": np.eye(P, dtype=f),
        "k_ones_head": (i // CH == j // CH).astype(f),
        "k_level_mask": level,
        "k_score_mask": score,
        "k_keep": keep,
        "k_cos": np.cos(ang).T[pair].astype(f),
        "k_sin": (np.sin(ang).T[pair] * sign).astype(f),
        "k_swap": (i == (j ^ 1)).astype(f),
        "k_fold": (np.arange(4)[:, None] % 2 == np.arange(2)[None, :]).astype(f),
    }


def kernel(**inputs):
    import concourse.bacc as _bacc
    from concourse.bass_utils import run_bass_kernel_spmd as _run

    nc = _bacc.Bacc("TRN2", target_bir_lowering=False, num_devices=1)
    arrays, args = {}, {}
    for name, a in [(n, inputs[n]) for n in _INS] + list(shape_tables().items()):
        a = np.ascontiguousarray(a)
        arrays[f"in_{name}"] = a
        args[name] = nc.dram_tensor(f"in_{name}", a.shape, mybir.dt.from_np(a.dtype), kind="ExternalInput").ap()
    out = nc.dram_tensor("out", (1, LAT, D), F32, kind="ExternalOutput").ap()
    backbone(nc, args, out)
    r = _run(nc, [arrays], core_ids=[0])
    return r.results[0]["out"]
```
